# Optimizing a Trainium2 kernel written in Bass

```python
import jax, jax.numpy as jnp
from jax import lax
import numpy as np

D_MODEL = 1024
BATCH = 1
SEQ = 128
DEPTH = 2
DEC_BATCH = 1
DEC_SEQ = 256
PAST_LEN = 128

GRID_W = 64
N_ATTN_LAYERS = (DEPTH + 1) // 2
N_FOURIER_LAYERS = DEPTH // 2
HEAD_DIM = 64
ATTN_WIDTH = D_MODEL // 2
N_HEADS = ATTN_WIDTH // HEAD_DIM
N_KV_HEADS = N_HEADS // 4
KV_GROUPS = N_HEADS // N_KV_HEADS
KV_WIDTH = N_KV_HEADS * HEAD_DIM
WINDOW = 128
Q_BLOCK = 128
POOL_WINDOWS = (2, 4, 8, 16)
POOL_GROUPS = len(POOL_WINDOWS)
POOL_WIDTH = D_MODEL // 2
POOL_GROUP_DIM = POOL_WIDTH // POOL_GROUPS
MIX_IN_A = ATTN_WIDTH + 2 * KV_WIDTH + POOL_WIDTH
MIX_OUT_A = ATTN_WIDTH + POOL_WIDTH
FOURIER_GROUPS = 4
FOURIER_WIDTH = D_MODEL
FOURIER_GROUP_DIM = FOURIER_WIDTH // FOURIER_GROUPS
N_EXPERT_GROUPS = 4
EXPERTS_PER_GROUP = 4
N_EXPERTS = N_EXPERT_GROUPS * EXPERTS_PER_GROUP
TOP_K = 2
D_EXPERT = D_MODEL // 2
ROPE_THETA = 10000.0
EPS = 1e-6
NEG = -1e30

kernel_name = "hybrid_dit_window_pool_fourier_hmoe_step"

def rmsnorm(x, g):
    xf = x.astype(jnp.float32)
    y = xf * lax.rsqrt(jnp.mean(xf * xf, axis=-1, keepdims=True) + EPS)
    return (y * g.astype(jnp.float32)).astype(x.dtype)

def adaln(cond, w, b):
    m = jax.nn.silu(cond) @ w + b
    return jnp.split(m[:, None, :], 6, axis=-1)

def modulate(x, g, shift, scale):
    return rmsnorm(x, g) * (1 + scale) + shift

def axial_rope(x):
    T = x.shape[1]
    rows = T // GRID_W
    row = jnp.repeat(jnp.arange(rows), GRID_W).astype(jnp.float32)
    col = jnp.tile(jnp.arange(GRID_W), rows).astype(jnp.float32)
    half = HEAD_DIM // 2
    nf = half // 2
    freqs = ROPE_THETA ** (-jnp.arange(nf, dtype=jnp.float32) / nf)
    xf = x.astype(jnp.float32)

    def rot(xh, pos):
        ang = pos[:, None] * freqs[None, :]
        cos = jnp.cos(ang)[None, :, None, :]
        sin = jnp.sin(ang)[None, :, None, :]
        x1, x2 = xh[..., :nf], xh[..., nf:]
        return jnp.concatenate([x1 * cos - x2 * sin, x1 * sin + x2 * cos], axis=-1)

    out = jnp.concatenate([rot(xf[..., :half], row), rot(xf[..., half:], col)], axis=-1)
    return out.astype(x.dtype)

def sink_softmax(s, sink):
    sk = sink.astype(jnp.float32).reshape(1, N_KV_HEADS, KV_GROUPS, 1, 1)
    m = jnp.maximum(jnp.max(s, axis=-1, keepdims=True), sk)
    p = jnp.exp(s - m)
    return p / (jnp.sum(p, axis=-1, keepdims=True) + jnp.exp(sk - m))

def context_attention(q, k, v, sink):
    B, L = q.shape[:2]
    nb = L // Q_BLOCK
    scale = HEAD_DIM ** -0.5
    qb = q.reshape(B, nb, Q_BLOCK, N_KV_HEADS, KV_GROUPS, HEAD_DIM).transpose(1, 0, 2, 3, 4, 5)

    def block(qblk):
        s = jnp.einsum('bqkgd,bskd->bkgqs', qblk, k).astype(jnp.float32) * scale
        p = sink_softmax(s, sink).astype(v.dtype)
        return jnp.einsum('bkgqs,bskd->bqkgd', p, v)

    o = lax.map(block, qb)
    return o.transpose(1, 0, 2, 3, 4, 5).reshape(B, L, ATTN_WIDTH)

def latent_attention(q, k, v, k_ctx, v_ctx, sink):
    B, T = q.shape[:2]
    nb = T // Q_BLOCK
    span = Q_BLOCK + 2 * WINDOW
    scale = HEAD_DIM ** -0.5
    pad = ((0, 0), (WINDOW, WINDOW), (0, 0), (0, 0))
    kp = jnp.pad(k, pad)
    vp = jnp.pad(v, pad)
    qg = q.reshape(B, T, N_KV_HEADS, KV_GROUPS, HEAD_DIM)

    def block(b):
        start = b * Q_BLOCK
        qblk = lax.dynamic_slice_in_dim(qg, start, Q_BLOCK, axis=1)
        kw = lax.dynamic_slice_in_dim(kp, start, span, axis=1)
        vw = lax.dynamic_slice_in_dim(vp, start, span, axis=1)
        qpos = start + jnp.arange(Q_BLOCK)
        kpos = start - WINDOW + jnp.arange(span)
        valid = (kpos[None, :] >= 0) & (kpos[None, :] < T) & (jnp.abs(qpos[:, None] - kpos[None, :]) <= WINDOW)
        s_win = jnp.einsum('bqkgd,bskd->bkgqs', qblk, kw).astype(jnp.float32) * scale
        s_win = jnp.where(valid[None, None, None], s_win, NEG)
        s_ctx = jnp.einsum('bqkgd,bskd->bkgqs', qblk, k_ctx).astype(jnp.float32) * scale
        p = sink_softmax(jnp.concatenate([s_win, s_ctx], axis=-1), sink).astype(v.dtype)
        return (jnp.einsum('bkgqs,bskd->bqkgd', p[..., :span], vw)
                + jnp.einsum('bkgqs,bskd->bqkgd', p[..., span:], v_ctx))

    o = lax.map(block, jnp.arange(nb))
    return o.transpose(1, 0, 2, 3, 4, 5).reshape(B, T, ATTN_WIDTH)

def multiscale_pool(u, pool_w, pool_scale):
    B, T, _ = u.shape
    uf = u.reshape(B, T, POOL_GROUPS, POOL_GROUP_DIM).astype(jnp.float32)
    cs = jnp.concatenate([jnp.zeros((B, 1, POOL_GROUPS, POOL_GROUP_DIM), jnp.float32),
                          jnp.cumsum(uf, axis=1)], axis=1)
    half = jnp.asarray(np.array(POOL_WINDOWS) // 2)[None, :]
    t = jnp.arange(T)[:, None]
    lo = jnp.clip(t - half, 0, T)
    hi = jnp.clip(t + half, 0, T)
    gidx = jnp.arange(POOL_GROUPS)[None, :]
    ssum = cs[:, hi, gidx, :] - cs[:, lo, gidx, :]
    cnt = (hi - lo).astype(jnp.float32)[None, :, :, None]
    pooled = (ssum / cnt - uf).astype(u.dtype)
    y = jnp.einsum('btgc,gcd->btgd', pooled, pool_w)
    return y.reshape(B, T, POOL_WIDTH) * pool_scale

def fourier_mix(u):
    B, T, _ = u.shape
    ug = u.reshape(B, T, FOURIER_GROUPS, FOURIER_GROUP_DIM).astype(jnp.float32)
    f = jnp.fft.fft2(ug, axes=(1, 3), norm='ortho').real
    return f.astype(u.dtype).reshape(B, T, FOURIER_WIDTH)

def attn_pool_project(h, w_in, q_g, k_g):
    B, T, _ = h.shape
    z = h @ w_in
    q, k, v, u = jnp.split(z, [ATTN_WIDTH, ATTN_WIDTH + KV_WIDTH, ATTN_WIDTH + 2 * KV_WIDTH], axis=-1)
    q = rmsnorm(q.reshape(B, T, N_HEADS, HEAD_DIM), q_g)
    k = rmsnorm(k.reshape(B, T, N_KV_HEADS, HEAD_DIM), k_g)
    v = v.reshape(B, T, N_KV_HEADS, HEAD_DIM)
    return q, k, v, u

def hier_moe(h, wg, bg, we, be, w1, w3, w2):
    B, T, D = h.shape
    x = h.reshape(-1, D)
    pg = jax.nn.softmax((x @ wg).astype(jnp.float32) + bg.astype(jnp.float32), axis=-1)
    pg_top, g_idx = lax.top_k(pg, 1)
    le = ((x @ we).astype(jnp.float32) + be.astype(jnp.float32)).reshape(-1, N_EXPERT_GROUPS, EXPERTS_PER_GROUP)
    le_g = jnp.einsum('ng,nge->ne', jax.nn.one_hot(g_idx[:, 0], N_EXPERT_GROUPS, dtype=jnp.float32), le)
    pe = jax.nn.softmax(le_g, axis=-1)
    pe_top, e_idx = lax.top_k(pe, TOP_K)
    wts = pg_top * pe_top / jnp.sum(pe_top, axis=-1, keepdims=True)
    ids = g_idx * EXPERTS_PER_GROUP + e_idx
    comb = jnp.einsum('nk,nke->ne', wts, jax.nn.one_hot(ids, N_EXPERTS, dtype=jnp.float32)).astype(x.dtype)
    h1 = jnp.einsum('nd,edf->nef', x, w1)
    h3 = jnp.einsum('nd,edf->nef', x, w3)
    a = jax.nn.silu(h1) * h3 * comb[:, :, None]
    return jnp.einsum('nef,efd->nd', a, w2).reshape(B, T, D)

def setup_inputs(seed: int = 0) -> dict:
    key = jax.random.key(seed)
    ks = jax.random.split(key, 26)
    n = jax.random.normal
    D = D_MODEL
    return {
        'x_prompt': n(ks[0], (BATCH, SEQ, D), jnp.float32),
        'x_sample': n(ks[1], (DEC_BATCH, DEC_SEQ, D), jnp.float32),
        'cache_k': n(ks[2], (DEC_BATCH, N_ATTN_LAYERS, PAST_LEN, N_KV_HEADS, HEAD_DIM), jnp.float32),
        'cache_v': n(ks[3], (DEC_BATCH, N_ATTN_LAYERS, PAST_LEN, N_KV_HEADS, HEAD_DIM), jnp.float32),
        'c': n(ks[4], (DEC_BATCH, D), jnp.float32),
        'c_ctx': n(ks[5], (D,), jnp.float32),
        'ada_w': n(ks[6], (DEPTH, D, 6 * D), jnp.float32) * (0.5 * D ** -0.5),
        'ada_b': n(ks[7], (DEPTH, 6 * D), jnp.float32) * 0.01,
        'norm_mix': 1.0 + 0.02 * n(ks[8], (DEPTH, D), jnp.float32),
        'norm_ffn': 1.0 + 0.02 * n(ks[9], (DEPTH, D), jnp.float32),
        'a_w_in': n(ks[10], (N_ATTN_LAYERS, D, MIX_IN_A), jnp.float32) * D ** -0.5,
        'a_q_norm': 1.0 + 0.02 * n(ks[11], (N_ATTN_LAYERS, HEAD_DIM), jnp.float32),
        'a_k_norm': 1.0 + 0.02 * n(ks[12], (N_ATTN_LAYERS, HEAD_DIM), jnp.float32),
        'a_sink': 0.5 * n(ks[13], (N_ATTN_LAYERS, N_HEADS), jnp.float32),
        'pool_w': n(ks[14], (N_ATTN_LAYERS, POOL_GROUPS, POOL_GROUP_DIM, POOL_GROUP_DIM), jnp.float32) * POOL_GROUP_DIM ** -0.5,
        'pool_scale': 1.0 + 0.1 * n(ks[15], (N_ATTN_LAYERS, POOL_WIDTH), jnp.float32),
        'a_w_out': n(ks[16], (N_ATTN_LAYERS, MIX_OUT_A, D), jnp.float32) * MIX_OUT_A ** -0.5,
        'f_w_in': n(ks[17], (N_FOURIER_LAYERS, D, FOURIER_WIDTH), jnp.float32) * D ** -0.5,
        'f_w_out': n(ks[18], (N_FOURIER_LAYERS, FOURIER_WIDTH, D), jnp.float32) * FOURIER_WIDTH ** -0.5,
        'router_g_w': n(ks[19], (DEPTH, D, N_EXPERT_GROUPS), jnp.float32) * D ** -0.5,
        'router_g_b': n(ks[20], (DEPTH, N_EXPERT_GROUPS), jnp.float32) * 0.01,
        'router_e_w': n(ks[21], (DEPTH, D, N_EXPERTS), jnp.float32) * D ** -0.5,
        'router_e_b': n(ks[22], (DEPTH, N_EXPERTS), jnp.float32) * 0.01,
        'moe_w1': n(ks[23], (DEPTH, N_EXPERTS, D, D_EXPERT), jnp.float32) * D ** -0.5,
        'moe_w3': n(ks[24], (DEPTH, N_EXPERTS, D, D_EXPERT), jnp.float32) * D ** -0.5,
        'moe_w2': n(ks[25], (DEPTH, N_EXPERTS, D_EXPERT, D), jnp.float32) * D_EXPERT ** -0.5,
    }

def reference(x_prompt, x_sample, cache_k, cache_v, c, c_ctx, ada_w, ada_b, norm_mix, norm_ffn,
              a_w_in, a_q_norm, a_k_norm, a_sink, pool_w, pool_scale, a_w_out, f_w_in, f_w_out,
              router_g_w, router_g_b, router_e_w, router_e_b, moe_w1, moe_w3, moe_w2):
    xp, xs = x_prompt, x_sample
    cond_ctx = c_ctx[None, :]
    new_k, new_v = [], []
    for l in range(DEPTH):
        i = l // 2
        mp = adaln(cond_ctx, ada_w[l], ada_b[l])
        ms = adaln(c, ada_w[l], ada_b[l])
        hp = modulate(xp, norm_mix[l], mp[0], mp[1])
        hs = modulate(xs, norm_mix[l], ms[0], ms[1])
        if l % 2 == 0:
            qp, kp, vp, up = attn_pool_project(hp, a_w_in[i], a_q_norm[i], a_k_norm[i])
            new_k.append(kp)
            new_v.append(vp)
            op = jnp.concatenate([context_attention(qp, kp, vp, a_sink[i]),
                                  multiscale_pool(up, pool_w[i], pool_scale[i])], axis=-1) @ a_w_out[i]
            qs, ks_, vs, us = attn_pool_project(hs, a_w_in[i], a_q_norm[i], a_k_norm[i])
            qs = axial_rope(qs)
            ks_ = axial_rope(ks_)
            os_ = jnp.concatenate([latent_attention(qs, ks_, vs, cache_k[:, i], cache_v[:, i], a_sink[i]),
                                   multiscale_pool(us, pool_w[i], pool_scale[i])], axis=-1) @ a_w_out[i]
        else:
            op = fourier_mix(hp @ f_w_in[i]) @ f_w_out[i]
            os_ = fourier_mix(hs @ f_w_in[i]) @ f_w_out[i]
        xp = xp + mp[2] * op
        xs = xs + ms[2] * os_
        hp = modulate(xp, norm_ffn[l], mp[3], mp[4])
        hs = modulate(xs, norm_ffn[l], ms[3], ms[4])
        xp = xp + mp[5] * hier_moe(hp, router_g_w[l], router_g_b[l], router_e_w[l], router_e_b[l],
                                   moe_w1[l], moe_w3[l], moe_w2[l])
        xs = xs + ms[5] * hier_moe(hs, router_g_w[l], router_g_b[l], router_e_w[l], router_e_b[l],
                                   moe_w1[l], moe_w3[l], moe_w2[l])
    new_cache_k = jnp.stack(new_k, axis=1)
    new_cache_v = jnp.stack(new_v, axis=1)
    return (xp, xs, new_cache_k, new_cache_v)


_drawn_inputs = setup_inputs


def setup_inputs(seed=0):
    import zlib

    import numpy as np

    out = dict(_drawn_inputs(seed))
    spreads = {}
    factors = {'cache_k': 4.015,
     'cache_v': 3.495,
     'ada_b': 3.368,
     'norm_mix': 2.96,
     'norm_ffn': 3.689,
     'a_q_norm': 8.0,
     'a_k_norm': 3.168,
     'a_sink': 8.0,
     'router_g_b': 7.449,
     'router_e_b': 8.0}
    for name, (base, spread) in spreads.items():
        noise = np.random.default_rng([zlib.crc32(name.encode()), seed]).standard_normal(out[name].shape)
        drawn = base * np.exp(spread * noise) if base else spread * noise
        out[name] = __import__('jax').numpy.asarray(drawn.astype(out[name].dtype))
    for name, factor in factors.items():
        out[name] = (out[name] * factor).astype(out[name].dtype)
    return out
```

```python
from contextlib import ExitStack

import concourse.bass as bass
from concourse import mybir
import numpy as np

F32 = mybir.dt.float32
I32 = mybir.dt.int32
ALU = mybir.AluOpType
ACT = mybir.ActivationFunctionType
AX = mybir.AxisListType

P = 128
D = 1024
KT = D // P
L = 2
SEQ = 128
DEC = 256
TOK = SEQ + DEC
NT = TOK // P
PAST = 128
HD = 64
NH = 8
NKV = 2
AW = NH * HD
KVW = NKV * HD
PW = 512
NPG = 4
ZW = AW + 2 * KVW + PW
QKW = AW + KVW
NQK = NH + NKV
NE = 16
NG = 4
EPG = 4
DE = 512
FC = DE // P
FG = 4
FD = D // FG
HALF = 512
BLK = 64
PAIRS = 2 * TOK
NOV = (PAIRS - NE) // BLK
NTHR = -(-TOK // BLK) - 1
EPS = 1e-6
GRID_W = 64
WINDOW = 128
LOWEST = -3.0e38

NS = 6
SLOT = KT * HALF
ADA_C = 6 * D // HALF
W_IN_COLS = [512, 512, 256]


def constant_columns():
    out = {}
    p = np.arange(P)
    out["ident"] = np.eye(P)
    out["before"] = (p[:, None] < p[None, :]).astype(float)
    out["ones"] = np.ones((P, P))
    rows = {
        "iota": np.arange(BLK),
        "eps": [EPS],
        "desc": np.arange(NG, 0, -1),
        "limit": BLK * np.arange(1, NTHR + 1),
        "tri": (np.arange(NE)[None, :] < np.arange(NE)[:, None]).astype(float).ravel(),
        "jrow": np.arange(NOV),
        "first": BLK * np.arange(NE),
        "shift": BLK * NE - BLK - BLK * np.arange(NE),
    }
    for k, v in rows.items():
        out[k] = np.broadcast_to(np.asarray(v, float), (P, len(v)))
    return out


def attention_columns():
    out = {}
    tok = np.arange(DEC)
    half, nf = HD // 2, HD // 4
    freqs = (np.float32(10000.0) ** (-np.arange(nf, dtype=np.float32) / np.float32(nf))).astype(np.float32)
    cos, sin = np.zeros((DEC, HD)), np.zeros((DEC, HD))
    for n, pos in enumerate((tok // GRID_W, tok % GRID_W)):
        ang = (pos.astype(np.float32)[:, None] * freqs[None, :]).astype(np.float32)
        c, s = np.cos(ang), np.sin(ang)
        cos[:, half * n:half * (n + 1)] = np.concatenate([c, c], 1)
        sin[:, half * n:half * (n + 1)] = np.concatenate([-s, s], 1)
    out["cos"] = cos.reshape(2, P, HD).transpose(1, 0, 2).reshape(P, -1)
    out["sin"] = sin.reshape(2, P, HD).transpose(1, 0, 2).reshape(P, -1)
    q, k = tok[:, None], tok[None, :]
    mask = np.where(np.abs(q - k) <= WINDOW, 0.0, -1e30)
    mask = np.concatenate([mask, np.zeros((DEC, PAST))], 1)
    out["mask"] = mask.reshape(2, P, DEC + PAST).transpose(1, 0, 2).reshape(P, -1)

    def band(T, w):
        t = np.arange(T)
        lo, hi = np.clip(t - w // 2, 0, T), np.clip(t + w // 2, 0, T)
        s = np.arange(T)[:, None]
        m = ((s >= lo) & (s < hi)) / (hi - lo).astype(float) - np.eye(T)
        return m

    out["band_ctx"] = np.concatenate([band(SEQ, w) for w in (2, 4, 8, 16)], 1)
    lat = np.stack([band(DEC, w) for w in (2, 4, 8, 16)])
    out["band_lat"] = lat.reshape(NPG, 2, P, DEC).transpose(2, 0, 1, 3).reshape(P, -1)
    return out


def fourier_columns():
    out = {}

    def dft(n, scale):
        a = 2 * np.pi * (np.outer(np.arange(n), np.arange(n)) % n) / n
        return np.cos(a) * scale, np.sin(a) * scale

    c, s = dft(FD, FD ** -0.5)
    out["feat"] = np.concatenate([c, s], 1).reshape(2, P, 2 * FD).transpose(1, 0, 2).reshape(P, -1)
    c, s = dft(SEQ, SEQ ** -0.5)
    out["time_ctx"] = np.concatenate([c, -s], 1)
    c, s = dft(DEC, DEC ** -0.5)
    out["time_lat"] = np.concatenate([c, -s], 1).reshape(2, P, 2 * DEC).transpose(1, 0, 2).reshape(P, -1)
    return out


def places(columns):
    at, out = 0, {}
    for k, v in columns.items():
        out[k] = (at, v.shape[1])
        at += v.shape[1]
    return out, at


CONST, N_CONST = places(constant_columns())
ATT, N_ATT = places(attention_columns())
FOUR, N_FOUR = places(fourier_columns())


class Turns:

    def __init__(self, banks):
        self.banks, self.at, self.filled = banks, 0, 0
        self.emptied = {"act": 0, "dve": 0}
        self.last = {}
        self.of = {}

    def add(self, key, who, bank=None):
        if bank is None:
            bank = self.banks[self.at % len(self.banks)]
            self.at += 1
        self.filled += 1
        self.emptied[who] += 1
        self.of[key] = (bank, self.filled, who, self.emptied[who], self.last.get(bank))
        self.last[bank] = (who, self.emptied[who])

    def all_free(self):
        self.last = {}


def plan():
    t = Turns(list(range(7)))
    marks = {}

    def ada(l, c0, c1):
        for c in range(c0, c1):
            t.add(("ada", l, c), "act")
            if c > 0:
                t.add(("adaT", l, c - 1), "dve")
        if c1 == ADA_C:
            t.add(("adaT", l, c1 - 1), "dve")

    def norm(s):
        for j in range(KT):
            t.add(("norm", s, j), "act" if j % 2 else "dve")

    def gate(s):
        for c in range(2):
            for h in range(2):
                t.add(("gate", s, c, h), "act")

    def project(l):
        for h in range(2):
            for i in range(NT):
                t.add(("out", l, h, i), "dve")

    def route(l):
        t.add(("router", l), "dve")
        for i in range(NT):
            for h in range(2):
                t.add(("tokens", l, i, h), "act")
        t.add(("rank", l), "dve")
        gate(2 * l + 1)

    t.add("rows", "dve")
    ada(0, 0, ADA_C)
    norm(0)
    for c in range(len(W_IN_COLS)):
        for i in range(NT):
            t.add(("z", c, i), "act" if i % 2 else "dve")
    for g in range(NPG):
        t.add(("pool", g), "act")
        if g > 0:
            t.add(("pooled", g - 1), "act")
    t.add(("pooled", NPG - 1), "act")
    ada(1, 0, 6)
    for c in range(NH // 2):
        t.add(("qT", c), "act")
    t.add("kT", "act")

    def scores(i):
        for c in range(NH // 2):
            for h in (c, c + NH // 2):
                t.add(("score", i, h), "dve")

    def values(i):
        for h in range(NH):
            t.add(("PT", i, h), "act")
        t.add(("oT", i), "dve", bank=7)

    scores(0)
    scores(1)
    ada(1, 6, 9)
    values(0)
    values(1)
    scores(2)
    ada(1, 9, ADA_C)
    gate(0)
    values(2)
    project(0)
    norm(1)
    route(0)
    marks[0] = dict(t.emptied)
    t.all_free()
    norm(2)
    gate(2)
    for f in range(KT):
        t.add(("uT", f), "act" if f % 2 else "dve")
    for i in range(NT):
        for g in range(FG):
            t.add(("v", i, g), "act" if g % 2 else "dve")
    for f in range(KT):
        t.add(("fT", f), "act" if f % 2 else "dve")
    project(1)
    norm(3)
    route(1)
    marks[1] = dict(t.emptied)
    return t.of, marks


def build(nc, x_prompt, x_sample, cache_k, cache_v, c, c_ctx, ada_w, ada_b, norm_mix, norm_ffn,
          a_w_in, a_q_norm, a_k_norm, a_sink, pool_w, pool_scale, a_w_out, f_w_in, f_w_out,
          router_g_w, router_g_b, router_e_w, router_e_b, moe_w1, moe_w3, moe_w2,
          const, att_const, four_const, y_prompt, y_sample, new_k, new_v):
    turn, marks = plan()

    def cols(w, a, b):
        return w[:, a:b].rearrange("(k p) n -> p k n", p=P)

    ada_items = [[cols(ada_w[l], HALF * n, HALF * (n + 1)) for n in range(ADA_C)] for l in range(L)]
    w_in_items, at = [], 0
    for n in W_IN_COLS:
        w_in_items.append(cols(a_w_in[0], at, at + n))
        at += n
    halves = lambda w: [cols(w, 0, HALF), cols(w, HALF, D)]
    before0 = ada_items[0] + w_in_items + ada_items[1] + halves(a_w_out[0])
    before1 = halves(f_w_in[0]) + halves(f_w_out[0])
    N_ADA0, N_WIN, N_ADA1 = 0, ADA_C, ADA_C + 3
    N_WOUT = N_ADA1 + ADA_C
    N_EXP0 = len(before0)
    N_FIN = N_EXP0 + 3 * NE
    N_FOUT = N_FIN + 2
    N_EXP1 = N_FIN + len(before1)
    n_exp = [N_EXP0, N_EXP1]

    R_MIX, R_FFN, R_CCTX, R_C, R_PS = 0, L * KT, 2 * L * KT, 2 * L * KT + KT, 2 * L * KT + 2 * KT
    N_ROWS = R_PS + NPG
    N_BROWS = L * 6 * KT

    ctx = ExitStack()
    with ctx:
        def sb(name, shape, dt=F32):
            return ctx.enter_context(nc.sbuf_tensor(name, shape, dt))

        def sem(name):
            return ctx.enter_context(nc.semaphore(name))

        ring = sb("ring", [P, NS, SLOT])
        x = sb("x", [P, NT, D])
        h = sb("h", [P, NT, D])
        T = sb("T", [P, KT, TOK])
        Z = sb("Z", [P, 7168])
        gate_b = sb("gate_b", [P, 2, D])
        special = sb("special", [P, max(N_ATT, N_FOUR)])
        cst = sb("cst", [P, N_CONST])
        ada_row = sb("ada_row", [P, 2, HALF])
        diag = sb("diag", [P, 2, HALF])
        rows = sb("rows", [N_ROWS, P])
        rows_silu = sb("rows_silu", [N_ROWS, P])
        brows = sb("brows", [N_BROWS, P])
        colv = sb("colv", [P, N_ROWS])
        bcol = sb("bcol", [P, N_BROWS])
        cond = sb("cond", [P, KT, 32])
        mcol = sb("mcol", [P, L, 6, KT, 2])
        router_w = sb("router_w", [P, L, KT, NG + NE])
        router_b = sb("router_b", [P, L, NG + NE])
        sink = sb("sink", [P, NH])
        qk_gain = sb("qk_gain", [P, 2, HD])
        pool_ws = sb("pool_ws", [P, NPG, P])
        ckT_in = sb("ckT_in", [P, KVW])
        cv = sb("cv", [P, KVW])
        stat = sb("stat", [P, 2, NT])

        z = Z[:, 0:NT * ZW].rearrange("p (t n) -> p t n", t=NT)
        at = NT * ZW
        qT = Z[:, at:at + 4 * TOK].rearrange("p (c n) -> p c n", c=4)
        at += 4 * TOK
        kT = Z[:, at:at + TOK + PAST]
        at += TOK + PAST
        PT = Z[:, at:at + 2 * TOK].rearrange("p (b n) -> p b n", b=2)
        at += 2 * TOK
        small = sb("small", [P, 96])
        ssq, rsq = small[:, 32:62], small[:, 64:94]
        p_ctx = ring_free = None
        PC = sb("PC", [P, NH, P])
        pooled = PC[:, 0:6, :].rearrange("p a n -> p (a n)").rearrange("p (b n) -> p b n", b=2)
        assert at <= 7168
        hflat = h[:, :, :].rearrange("p t n -> p (t n)")
        PL = hflat[:, 0:NH * TOK].rearrange("p (h n) -> p h n", h=NH)
        sq = hflat[:, 0:NT * QKW].rearrange("p (t n) -> p t n", t=NT)
        rot0 = hflat[:, 0:QKW]
        rot1 = PT.rearrange("p b n -> p (b n)")[:, 0:QKW]
        qk = hflat[:, QKW:(1 + NT) * QKW].rearrange("p (t n) -> p t n", t=NT)
        uT = hflat.rearrange("p (c n) -> p c n", c=KT)
        v = Z[:, 0:NT * FG * 2 * FD].rearrange("p (t g n) -> p t g n", t=NT, g=FG)
        at = 0

        def zone(n):
            nonlocal at
            at += n
            return Z[:, at - n:at]

        at = 0
        xT = zone(2 * KT * BLK).rearrange("p (b k s) -> p b k s", b=2, k=KT)
        up_s = zone(2 * DE).rearrange("p (b n) -> p b n", b=2)
        sil = zone(FC * BLK).rearrange("p (k s) -> p k s", k=FC)
        aT = zone(2 * FC * BLK).rearrange("p (b k s) -> p b k s", b=2, k=FC)
        ys = zone(2 * HALF).rearrange("p (b n) -> p b n", b=2)
        S12 = zone(2 * NT * BLK).rearrange("p (a t s) -> p a t s", a=2, t=NT)
        W12 = zone(2 * NT * BLK).rearrange("p (a t s) -> p a t s", a=2, t=NT)
        Sel = zone(2 * NT * BLK).rearrange("p (b t s) -> p b t s", b=2, t=NT)
        CT = zone(2 * NT * 2 * BLK).rearrange("p (b t d s) -> p b t d s", b=2, t=NT, d=2)
        Cs = zone(2 * TOK).rearrange("p (b n) -> p b n", b=2)
        assert at <= 7168, at
        acc = T[:, :, :].rearrange("p k n -> p (k n)").rearrange("p (t n) -> p t n", t=NT)
        scratch = special[:, 0:D]

        rt = PC[:, :, :].rearrange("p h n -> p (h n)")
        rat = [0]

        def rtile(*shape):
            n = int(np.prod(shape))
            a = rt[:, rat[0]:rat[0] + n]
            rat[0] += n
            if len(shape) == 1:
                return a
            names = "abcd"[:len(shape)]
            return a.rearrange(f"p ({' '.join(names)}) -> p {' '.join(names)}",
                               **{k: s for k, s in zip(names[:-1], shape[:-1])})

        lg = rtile(NT, NG + NE)
        mg, sg, pg, ml, se, p1, p2 = (rtile(NT) for _ in range(7))
        eg, og, sc4, le, ee, o1, o2, le2 = (rtile(NT, 4) for _ in range(8))
        prod = rtile(NT, 4, 4)
        M12 = rtile(2, NT, NE)
        Ms = rtile(NT, NE)
        G = rtile(NT, NE)
        ge = rtile(NT, NE)
        Gp = rtile(NT, NE)
        G12 = rtile(2, NT)
        c12 = rtile(2, NT)
        cmp5 = rtile(NE, NTHR)
        ovc, ovb, off, incl = (rtile(NE) for _ in range(4))
        eidf = rtile(NOV + 1)
        tri_p = rtile(NE, NE)
        cmp_j = tri_p[:, 0:NOV, :]
        assert rat[0] <= NH * P
        plan_i = sb("plan_i", [P, NOV + 1], I32)

        def con(name, n=None):
            a, w = CONST[name]
            return cst[:, a:a + w]

        def att(name):
            a, w = ATT[name]
            return special[:, a:a + w]

        def four(name):
            a, w = FOUR[name]
            return special[:, a:a + w]

        ident = con("ident")
        banks = [ctx.enter_context(nc.psum_tensor(f"bank{i}", [P, HALF], F32)) for i in range(8)]
        psX, psU, psT, psD, psC = banks[0:5]
        psK = banks[5:8]

        arrived = [sem(f"arrived{i}") for i in range(NS)]
        small_in = sem("small_in")
        params_in = sem("params_in")
        x_in = sem("x_in")
        special_in = sem("special_in")
        special_free = sem("special_free")
        full = sem("full")
        act_emptied = sem("act_emptied")
        dve_emptied = sem("dve_emptied")
        emptied = {"act": act_emptied, "dve": dve_emptied}
        cond_rows = sem("cond_rows")
        cols_ready = sem("cols_ready")
        zeroed = sem("zeroed")
        normed = sem("normed")
        affine_ready = sem("affine_ready")
        rms_ready = sem("rms_ready")
        qk_squares = sem("qk_squares")
        qk_sums = sem("qk_sums")
        qk_rms_ready = sem("qk_rms_ready")
        qk_ready = sem("qk_ready")
        kv_out_ready = sem("kv_out_ready")
        p_max = sem("p_max")
        p_exp = sem("p_exp")
        p_ready = sem("p_ready")
        pv_done = sem("pv_done")
        diag_ready = sem("diag_ready")
        x_ready = sem("x_ready")
        g_shifted = sem("g_shifted")
        g_exp = sem("g_exp")
        ms_ready = sem("ms_ready")
        plan_ready = sem("plan_ready")
        out_done = sem("out_done")
        kv_out_done = sem("kv_out_done")
        per_layer = []
        for l in range(L):
            per_layer.append({k: sem(f"{k}_{l}") for k in (
                "sel_ready", "gathered", "x_cols", "up_full", "up_out", "mid_full", "silu_out",
                "act_cols", "comb_full", "comb_out", "down_full", "down_out", "back_full",
                "back_out", "over_in", "over_done")})
        from_one = {"act": ("up_out", "comb_out", "down_out"), "dve": ("act_cols", "back_out", "over_done"),
                    "pe": ("comb_full",)}

        def start_at_one(e, who):
            for s in per_layer:
                for name in from_one[who]:
                    e.sem_inc(s[name], 1)

        block = ctx.enter_context(nc.Block())

        def last_use(n):
            for l in range(L):
                q = n - n_exp[l]
                if 0 <= q < 3 * NE:
                    return per_layer[l]["up_full" if q % 3 < 2 else "down_full"], q // 3 + 1
            for first, keys in ((N_ADA0, [("ada", 0, c) for c in range(ADA_C)]),
                                (N_WIN, [("z", c, NT - 1) for c in range(len(W_IN_COLS))]),
                                (N_ADA1, [("ada", 1, c) for c in range(ADA_C)]),
                                (N_WOUT, [("out", 0, c, NT - 1) for c in range(2)]),
                                (N_FIN, [("uT", 4 * c + 3) for c in range(2)]),
                                (N_FOUT, [("out", 1, c, NT - 1) for c in range(2)])):
                if first <= n < first + len(keys):
                    return full, turn[keys[n - first]][1]

        def stage_bank(key, e):
            bank, n, who, k, before = turn[key]
            e.wait_ge(full, n)
            return banks[bank]

        @block.sync
        def _(sp):
            def weights(n, src):
                if n >= NS:
                    sp.wait_ge(*last_use(n - NS))
                w = src.shape[2]
                dst = ring[:, n % NS, 0:KT * w].rearrange("p (k n) -> p k n", k=KT)
                sp.dma_start(dst, src).then_inc(arrived[n % NS], 16)

            for n, src in enumerate(before0):
                weights(n, src)
            for l in range(L):
                n0, s = n_exp[l], per_layer[l]
                if l == 1:
                    for n, src in enumerate(before1):
                        weights(N_FIN + n, src)

                def expert(e, u, m, w):
                    n = n0 + 3 * u + m
                    kk = KT if m < 2 else FC
                    dst = ring[:, n % NS, :].rearrange("p (k n) -> p k n", k=kk)
                    sp.dma_start(dst, w[l, bass.ds(e, 1), :, :].rearrange("a (k p) n -> p (a k) n", p=P))\
                      .then_inc(arrived[n % NS], 16)

                for u in range(2):
                    for m, w in enumerate((moe_w1, moe_w3, moe_w2)):
                        sp.wait_ge(*last_use(n0 + 3 * u + m - NS))
                        expert(u, u, m, w)
                with sp.Fori(1, NE // 2) as i:
                    for u in range(2):
                        for m, w in enumerate((moe_w1, moe_w3, moe_w2)):
                            sp.wait_ge(s["up_full"] if m < 2 else s["down_full"], i * 2 + (u - 1))
                            expert(i * 2 + u, u, m, w)
                sp.wait_ge(plan_ready, l + 1)
                blocks = sp.value_load(plan_i[0:1, NOV:NOV + 1], min_val=0, max_val=NOV)
                with sp.Fori(0, NOV) as j:
                    with sp.If(j < blocks):
                        sp.wait_ge(s["down_full"], NE)
                        sp.wait_ge(s["over_done"], j + 1)
                        ex = sp.value_load(plan_i[0:1, bass.ds(j, 1)], min_val=0, max_val=NE - 1)
                        for m, w in enumerate((moe_w1, moe_w3, moe_w2)):
                            kk = KT if m < 2 else FC
                            dst = ring[:, m, :].rearrange("p (k n) -> p k n", k=kk)
                            sp.dma_start(dst, w[l, bass.ds(ex, 1), :, :].rearrange("a (k p) n -> p (a k) n", p=P))\
                              .then_inc(s["over_in"], 16)
                sp.wait_ge(s["over_done"], blocks + 1)
            sp.wait_ge(x_ready, 4)
            sp.dma_start(y_prompt[0], x[:, 0, :]).then_inc(out_done, 16)
            sp.dma_start(y_sample[0].rearrange("(t p) n -> p t n", p=P), x[:, 1:NT, :]).then_inc(out_done, 16)
            sp.wait_ge(out_done, 32)
            sp.wait_ge(kv_out_done, 32)

        @block.gpsimd
        def _(gp):
            gp.memset(cond[:, :, :], 0.0).then_inc(zeroed, 1)
            gp.wait_ge(kv_out_ready, 1)
            gp.dma_start(new_k[0, 0].rearrange("s h d -> s (h d)"), qk[:, 0, AW:QKW]).then_inc(kv_out_done, 16)
            gp.dma_start(new_v[0, 0].rearrange("s h d -> s (h d)"), z[:, 0, AW + KVW:AW + 2 * KVW]).then_inc(kv_out_done, 16)
            for l in range(L):
                last = turn[("tokens", l, NT - 1, 1)]
                gp.wait_ge(full, last[1])
                gp.memset(Cs[:, 1, :], 0.0)
                gp.memset(ys[:, 1, :], 0.0)
                gp.memset(acc[:, :, :], 0.0).then_inc(zeroed, 1)

        loads = {small_in: 0, params_in: 0}

        @block.scalar
        def _(act):
            def small_load(dst, src, which=small_in):
                loads[which] += 16
                act.dma_start(dst, src).then_inc(which, 16)

            by_chunk = lambda a: a.rearrange("(k p) -> k p", p=P)
            for l in range(L):
                small_load(rows[R_MIX + l * KT:R_MIX + (l + 1) * KT, :], by_chunk(norm_mix[l]))
                small_load(rows[R_FFN + l * KT:R_FFN + (l + 1) * KT, :], by_chunk(norm_ffn[l]))
            small_load(rows[R_CCTX:R_CCTX + KT, :], by_chunk(c_ctx))
            small_load(rows[R_C:R_C + KT, :], by_chunk(c[0]))
            small_load(rows[R_PS:R_PS + NPG, :], by_chunk(pool_scale[0]))
            small_load(brows[:, :], ada_b.rearrange("l (k p) -> (l k) p", p=P))
            small_load(cst[:, :], const)
            act.dma_start(x[:, 0, :], x_prompt[0]).then_inc(x_in, 16)
            act.dma_start(x[:, 1:NT, :], x_sample[0].rearrange("(t p) n -> p t n", p=P)).then_inc(x_in, 16)
            for l in range(L):
                small_load(router_w[:, l, :, 0:NG], router_g_w[l].rearrange("(k p) n -> p k n", p=P), params_in)
                small_load(router_w[:, l, :, NG:], router_e_w[l].rearrange("(k p) n -> p k n", p=P), params_in)
                small_load(router_b[:, l, 0:NG], router_g_b[l:l + 1, :].to_broadcast([P, NG]), params_in)
                small_load(router_b[:, l, NG:], router_e_b[l:l + 1, :].to_broadcast([P, NE]), params_in)
            small_load(sink[:, :], a_sink[0:1, :].to_broadcast([P, NH]), params_in)
            small_load(qk_gain[:, 0, :], a_q_norm[0:1, :].to_broadcast([P, HD]), params_in)
            small_load(qk_gain[:, 1, :], a_k_norm[0:1, :].to_broadcast([P, HD]), params_in)
            small_load(pool_ws[:, :, :], pool_w[0].rearrange("g c d -> c g d"), params_in)
            small_load(ckT_in[:, :], cache_k[0, 0].rearrange("s h d -> s (h d)"), params_in)
            small_load(cv[:, :], cache_v[0, 0].rearrange("s h d -> s (h d)"), params_in)
            act.dma_start(special[:, 0:N_ATT], att_const).then_inc(special_in, 16)

            def emptied_inc(ins):
                ins.then_inc(act_emptied, 1)

            def sum_squares(n):
                for t in range(NT):
                    act.activation(h[:, t, :], x[:, t, :], ACT.Square, accum_out=stat[:, 0, t:t + 1])
                act.drain()
                act.activation(stat[:, 1, :], stat[:, 0, :], ACT.Sqrt, scale=1.0 / D, bias=con("eps")).then_inc(rms_ready, 1)

            def ada(l, c0, c1):
                for cc in range(c0, c1):
                    b = stage_bank(("ada", l, cc), act)
                    if cc >= 2:
                        act.wait_ge(full, turn[("adaT", l, cc - 2)][1])
                    emptied_inc(act.activation(ada_row[:, cc % 2, :], b[:, :], ACT.Copy))

            def norm(s):
                act.wait_ge(affine_ready, s + 1)
                for j in range(KT):
                    if turn[("norm", s, j)][2] == "act":
                        b = stage_bank(("norm", s, j), act)
                        affine(act, s, j, b)

            def affine(act, s, j, b):
                l, f = s // 2, s % 2
                act.activation(T[:, j, 0:SEQ], b[:, 0:SEQ], ACT.Identity,
                               scale=mcol[:, l, 3 * f + 1, j, 0:1], bias=mcol[:, l, 3 * f, j, 0:1])
                emptied_inc(act.activation(T[:, j, SEQ:TOK], b[:, SEQ:TOK], ACT.Identity,
                                           scale=mcol[:, l, 3 * f + 1, j, 1:2], bias=mcol[:, l, 3 * f, j, 1:2]))

            def gate(s):
                for k in range(2):
                    for hh in range(2):
                        b = stage_bank(("gate", s, k, hh), act)
                        emptied_inc(act.activation(gate_b[:, k, HALF * hh:HALF * (hh + 1)], b[:, :], ACT.Copy))

            def exps(i):
                act.wait_ge(p_max, i + 1)
                w = SEQ if i == 0 else TOK
                for hd in range(NH):
                    pr = PC[:, hd, :] if i == 0 else PL[:, hd, :]
                    act.activation(pr[:, 0:w], pr[:, 0:w], ACT.Exp, bias=small[:, 8 + hd:9 + hd],
                                   accum_out=small[:, 16 + hd:17 + hd])
                act.activation(small[:, 24:32], small[:, 24:32], ACT.Exp).then_inc(p_exp, 1)

            def turned(i):
                w = SEQ if i == 0 else TOK
                for hd in range(NH):
                    b = stage_bank(("PT", i, hd), act)
                    if NH * i + hd >= 2:
                        act.wait_ge(pv_done, NH * i + hd - 1)
                    emptied_inc(act.activation(PT[:, hd % 2, 0:w], b[:, 0:w], ACT.Copy))

            start_at_one(act, "act")
            act.wait_ge(small_in, loads[small_in])
            act.activation(rows_silu[:, :], rows[:, :], ACT.Silu).then_inc(cond_rows, 1)
            act.wait_ge(x_in, 32)
            sum_squares(0)
            ada(0, 0, ADA_C)
            norm(0)
            for cc in range(len(W_IN_COLS)):
                for i in range(NT):
                    if turn[("z", cc, i)][2] == "act":
                        b = stage_bank(("z", cc, i), act)
                        w, a = W_IN_COLS[cc], sum(W_IN_COLS[:cc])
                        emptied_inc(act.activation(z[:, i, a:a + w], b[:, 0:w], ACT.Copy))
            act.wait_ge(dve_emptied, turn[("z", 2, 2)][3])
            act.wait_ge(act_emptied, turn[("z", 2, 1)][3])
            act.activation(sq[:, :, :], z[:, :, 0:QKW], ACT.Square).then_inc(qk_squares, 1)
            act.wait_ge(qk_sums, 1)
            act.activation(rsq, ssq, ACT.Sqrt, scale=1.0 / HD, bias=con("eps")).then_inc(qk_rms_ready, 1)
            for g in range(NPG + 1):
                if g < NPG:
                    b = stage_bank(("pool", g), act)
                    if g >= 2:
                        act.wait_ge(full, turn[("pooled", g - 2)][1])
                    emptied_inc(act.activation(pooled[:, g % 2, :], b[:, 0:TOK], ACT.Copy))
                if g > 0:
                    b = stage_bank(("pooled", g - 1), act)
                    emptied_inc(act.activation(T[:, 4 + g - 1, :], b[:, 0:TOK], ACT.Identity,
                                               scale=colv[:, R_PS + g - 1:R_PS + g]))
            ada(1, 0, 6)
            for cc in range(NH // 2):
                b = stage_bank(("qT", cc), act)
                emptied_inc(act.activation(qT[:, cc, :], b[:, 0:TOK], ACT.Copy))
            b = stage_bank("kT", act)
            emptied_inc(act.activation(kT, b[:, 0:TOK + PAST], ACT.Copy))
            exps(0)
            exps(1)
            ada(1, 6, 9)
            turned(0)
            turned(1)
            ada(1, 9, ADA_C)
            gate(0)
            exps(2)
            turned(2)

            def routing_act(l):
                for i in range(NT):
                    for hh in range(2):
                        b = stage_bank(("tokens", l, i, hh), act)
                        emptied_inc(act.activation(h[:, i, HALF * hh:HALF * (hh + 1)], b[:, :], ACT.Copy))

            def moe(l):
                s = per_layer[l]

                def one(e, b, over):
                    act.wait_ge(s["up_full"], e + 1)
                    act.activation(up_s[:, b, :], psU[:, :], ACT.Copy).then_inc(s["up_out"], 1)
                    act.wait_ge(s["mid_full"], e + 1)
                    mid = psT[:, :].rearrange("p (k s) -> p k s", k=FC)
                    act.activation(sil, mid[:, :, 0:BLK], ACT.Silu).then_inc(s["silu_out"], 1)
                    act.wait_ge(s["comb_full"], e + 2)
                    act.activation(Cs[:, b, :], psC[:, 0:TOK], ACT.Copy).then_inc(s["comb_out"], 1)
                    act.wait_ge(s["down_full"], e + 1)
                    act.activation(ys[:, b, :], psD[:, :], ACT.Copy).then_inc(s["down_out"], 1)

                with act.Fori(0, NE // 2) as i:
                    for u in range(2):
                        one(i * 2 + u, u, False)
                act.wait_ge(plan_ready, l + 1)
                blocks = act.value_load(plan_i[0:1, NOV:NOV + 1], min_val=0, max_val=NOV)
                with act.Fori(0, NOV) as j:
                    with act.If(j < blocks):
                        one(j + NE, 0, True)

            for l in range(L):
                if l == 1:
                    act.wait_ge(x_ready, 2)
                    sum_squares(2)
                    norm(2)
                    gate(2)
                    for f in range(KT):
                        if turn[("uT", f)][2] == "act":
                            b = stage_bank(("uT", f), act)
                            emptied_inc(act.activation(uT[:, f, :], b[:, 0:TOK], ACT.Copy))
                    for i in range(NT):
                        for g in range(FG):
                            if turn[("v", i, g)][2] == "act":
                                b = stage_bank(("v", i, g), act)
                                emptied_inc(act.activation(v[:, i, g, :], b[:, :], ACT.Copy))
                    for f in range(KT):
                        if turn[("fT", f)][2] == "act":
                            b = stage_bank(("fT", f), act)
                            emptied_inc(act.activation(T[:, f, :], b[:, 0:TOK], ACT.Copy))
                act.wait_ge(x_ready, 2 * l + 1)
                sum_squares(2 * l + 1)
                norm(2 * l + 1)
                act.wait_ge(g_shifted, 2 * l + 1)
                act.activation(eg, eg, ACT.Exp).then_inc(g_exp, 1)
                act.wait_ge(g_shifted, 2 * l + 2)
                act.activation(ee, ee, ACT.Exp).then_inc(g_exp, 1)
                routing_act(l)
                gate(2 * l + 1)
                if l == 0:
                    act.wait_ge(special_free, 1)
                    act.dma_start(special[:, 0:N_FOUR], four_const).then_inc(special_in, 16)
                moe(l)

        @block.vector
        def _(dve):
            def settle():
                dve.drain()

            def emptied_inc(ins):
                ins.then_inc(dve_emptied, 1)

            def bc(ap, *shape):
                return ap.to_broadcast([P, *shape])

            def norm(s):
                l, f = s // 2, s % 2
                dve.wait_ge(rms_ready, s + 1)
                dve.reciprocal(stat[:, 0, :], stat[:, 1, :])
                settle()
                for t in range(NT):
                    last = dve.tensor_scalar(h[:, t, :], x[:, t, :], stat[:, 0, t:t + 1], None, ALU.mult)
                last.then_inc(normed, 1)

            def affine(s):
                for j in range(KT):
                    if turn[("norm", s, j)][2] == "dve":
                        b = stage_bank(("norm", s, j), dve)
                        l, f = s // 2, s % 2
                        for k, (a, e) in enumerate(((0, SEQ), (SEQ, TOK))):
                            last = dve.tensor_scalar(T[:, j, a:e], b[:, a:e], mcol[:, l, 3 * f + 1, j, k:k + 1],
                                                     mcol[:, l, 3 * f, j, k:k + 1], ALU.mult, ALU.add)
                        emptied_inc(last)

            def ada_cols(l, cc):
                b = stage_bank(("adaT", l, cc), dve)
                src = b[:, :].rearrange("p (s q r) -> p s r q", s=4, q=4)[:, :, 0:2, :]
                k0 = 4 * (cc % 2)
                emptied_inc(dve.tensor_reduce(mcol[:, l, cc // 2, k0:k0 + 4, :], src, AX.X, ALU.add))

            def ada(l, c0, c1):
                for cc in range(c0, c1):
                    if cc > 0:
                        ada_cols(l, cc - 1)
                if c1 == ADA_C:
                    ada_cols(l, c1 - 1)
                    settle()
                    bias = bcol[:, l * 6 * KT:(l + 1) * 6 * KT]
                    m = mcol[:, l].rearrange("p v k c -> p (v k) c")
                    dve.tensor_tensor(m, m, bias.unsqueeze(2).to_broadcast([P, 6 * KT, 2]), ALU.add)
                    settle()
                    for f, r in ((0, R_MIX), (1, R_FFN)):
                        gain = colv[:, r + l * KT:r + (l + 1) * KT].unsqueeze(2).to_broadcast([P, KT, 2])
                        sc = mcol[:, l, 3 * f + 1]
                        last = dve.scalar_tensor_tensor(sc, sc, 1.0, gain, ALU.add, ALU.mult)
                    last.then_inc(affine_ready, 2)
                    settle()

            def diagonals(s):
                l, f = s // 2, s % 2
                for n in range(4):
                    k, hh = n // 2, n % 2
                    if n >= 2:
                        dve.wait_ge(full, turn[("gate", s, (n - 2) // 2, (n - 2) % 2)][1])
                    for q in range(4):
                        last = dve.tensor_scalar(diag[:, n % 2, q * P:(q + 1) * P], ident,
                                                 mcol[:, l, 3 * f + 2, 4 * hh + q, k:k + 1], None, ALU.mult)
                    last.then_inc(diag_ready, 1)

            def gated_add(l):
                dve.wait_ge(act_emptied, turn[("gate", 2 * l, 1, 1)][3])
                for hh in range(2):
                    for i in range(NT):
                        b = stage_bank(("out", l, hh, i), dve)
                        cs = slice(HALF * hh, HALF * (hh + 1))
                        n = NT * hh + i
                        gated = scratch[:, HALF * (n % 2):HALF * (n % 2 + 1)]
                        emptied_inc(dve.tensor_tensor(gated, b[:, :], gate_b[:, min(i, 1), cs], ALU.mult))
                        settle()
                        last = dve.tensor_tensor(x[:, i, cs], x[:, i, cs], gated, ALU.add)
                last.then_inc(x_ready, 1)

            def add_reduce(out, in_):
                return dve.tensor_reduce(out, in_, AX.X, ALU.add)

            def first_largest(one, val, top):
                dve.tensor_tensor(sc4, val, bc(top.unsqueeze(2), NT, 4), ALU.is_equal)
                settle()
                dve.tensor_tensor(sc4, sc4, bc(con("desc").unsqueeze(1), NT, 4), ALU.mult)
                settle()
                dve.tensor_reduce(sg, sc4, AX.X, ALU.max)
                settle()
                dve.tensor_tensor(one, sc4, bc(sg.unsqueeze(2), NT, 4), ALU.is_equal)
                settle()

            def route(l):
                b = stage_bank(("router", l), dve)
                lo = b[:, 0:NT * (NG + NE)].rearrange("p (t n) -> p t n", t=NT)
                emptied_inc(dve.tensor_tensor(lg, lo, bc(router_b[:, l, :].unsqueeze(1), NT, NG + NE), ALU.add))
                settle()
                dve.tensor_reduce(mg, lg[:, :, 0:NG], AX.X, ALU.max)
                settle()
                dve.tensor_tensor(eg, lg[:, :, 0:NG], bc(mg.unsqueeze(2), NT, NG), ALU.subtract).then_inc(g_shifted, 1)
                first_largest(og, lg[:, :, 0:NG], mg)
                dve.tensor_tensor(prod, lg[:, :, NG:].rearrange("p t (g e) -> p t e g", g=NG),
                                  bc(og.unsqueeze(2), NT, EPG, NG), ALU.mult)
                settle()
                add_reduce(le, prod)
                settle()
                dve.tensor_reduce(ml, le, AX.X, ALU.max)
                settle()
                dve.tensor_tensor(ee, le, bc(ml.unsqueeze(2), NT, EPG), ALU.subtract).then_inc(g_shifted, 1)
                first_largest(o1, le, ml)
                dve.scalar_tensor_tensor(le2, o1, LOWEST, le, ALU.mult, ALU.add)
                settle()
                dve.tensor_reduce(ml, le2, AX.X, ALU.max)
                settle()
                first_largest(o2, le2, ml)
                for n, o in enumerate((o1, o2)):
                    dve.tensor_tensor(M12[:, n].rearrange("p t (g e) -> p t g e", g=NG),
                                      bc(og.unsqueeze(3), NT, NG, EPG), bc(o.unsqueeze(2), NT, NG, EPG), ALU.mult)
                settle()
                dve.tensor_tensor(Ms, M12[:, 0], M12[:, 1], ALU.add).then_inc(ms_ready, 1)
                dve.wait_ge(g_exp, 2 * l + 2)
                add_reduce(sg, eg)
                add_reduce(se, ee)
                settle()
                dve.reciprocal(pg, sg)
                dve.reciprocal(se, se)
                settle()
                dve.tensor_tensor(ee, ee, bc(se.unsqueeze(2), NT, EPG), ALU.mult)
                settle()
                dve.tensor_tensor(prod[:, :, 0, :], ee, o1, ALU.mult)
                dve.tensor_tensor(prod[:, :, 1, :], ee, o2, ALU.mult)
                settle()
                add_reduce(c12[:, 0, :], prod[:, :, 0, :])
                add_reduce(c12[:, 1, :], prod[:, :, 1, :])
                settle()
                dve.tensor_tensor(p1, c12[:, 0, :], c12[:, 1, :], ALU.add)
                settle()
                dve.reciprocal(p1, p1)
                settle()
                dve.tensor_tensor(p1, p1, pg, ALU.mult)
                settle()
                dve.tensor_tensor(c12, c12, bc(p1.unsqueeze(1), 2, NT), ALU.mult)
                diagonals(2 * l + 1)
                b = stage_bank(("rank", l), dve)
                rank = b[:, 0:NT * NE].rearrange("p (t e) -> p t e", t=NT)
                count = b[:, NT * NE:(NT + 1) * NE]
                dve.tensor_scalar(ge, rank, float(BLK), None, ALU.is_ge)
                dve.tensor_copy(G, rank)
                emptied_inc(dve.tensor_tensor(cmp5, bc(count.unsqueeze(2), NE, NTHR),
                                              bc(con("limit").unsqueeze(1), NE, NTHR), ALU.is_gt))
                settle()
                add_reduce(ovc, cmp5)
                settle()
                dve.tensor_tensor(tri_p, bc(ovc.unsqueeze(1), NE, NE),
                                  con("tri").rearrange("p (e f) -> p e f", e=NE), ALU.mult)
                settle()
                add_reduce(ovb, tri_p)
                add_reduce(eidf[:, NOV:NOV + 1], ovc)
                settle()
                dve.tensor_tensor(incl, ovb, ovc, ALU.add)
                dve.scalar_tensor_tensor(off, ovb, float(BLK), con("shift"), ALU.mult, ALU.add)
                settle()
                dve.tensor_tensor(cmp_j, bc(incl.unsqueeze(1), NOV, NE), bc(con("jrow").unsqueeze(2), NOV, NE), ALU.is_le)
                dve.tensor_tensor(ge, ge, bc(off.unsqueeze(1), NT, NE), ALU.mult)
                settle()
                add_reduce(eidf[:, 0:NOV], cmp_j)
                dve.tensor_tensor(G, G, ge, ALU.add)
                settle()
                dve.tensor_scalar(eidf[:, 0:NOV], eidf[:, 0:NOV], float(NE - 1), None, ALU.min)
                dve.tensor_tensor(G, G, bc(con("first").unsqueeze(1), NT, NE), ALU.add)
                settle()
                dve.tensor_copy(plan_i[:, :], eidf).then_inc(plan_ready, 1)
                dve.tensor_tensor(Gp, M12[:, 0], G, ALU.mult)
                dve.tensor_tensor(ge, M12[:, 1], G, ALU.mult)
                settle()
                add_reduce(G12[:, 0, :], Gp)
                add_reduce(G12[:, 1, :], ge)
                settle()

            g6 = G12.rearrange("p a t -> p (a t)")
            c6 = c12.rearrange("p a t -> p (a t)")
            S6 = S12.rearrange("p a t s -> p (a t) s")
            W6 = W12.rearrange("p a t s -> p (a t) s")

            def select(s, b):
                dve.tensor_tensor(S6, bc(con("iota").unsqueeze(1), 2 * NT, BLK), bc(g6.unsqueeze(2), 2 * NT, BLK), ALU.is_equal)
                settle()
                dve.tensor_tensor(Sel[:, b], S12[:, 0], S12[:, 1], ALU.add)
                dve.tensor_tensor(W6, S6, bc(c6.unsqueeze(2), 2 * NT, BLK), ALU.mult)
                dve.tensor_scalar(g6, g6, -float(BLK), None, ALU.add)
                settle()
                dve.tensor_tensor(CT[:, b], bc(W12[:, 0].unsqueeze(2), NT, 2, BLK), bc(W12[:, 1].unsqueeze(2), NT, 2, BLK),
                                  ALU.add).then_inc(s["sel_ready"], 1)
                settle()

            def moe(l):
                s = per_layer[l]

                def gather_out(e, b):
                    dve.wait_ge(s["gathered"], e + 1)
                    dve.tensor_copy(xT[:, b].rearrange("p k s -> p (k s)"), psX[:, :]).then_inc(s["x_cols"], 1)

                def hidden(e, b):
                    dve.wait_ge(s["silu_out"], e + 1)
                    mid = psT[:, :].rearrange("p (k s) -> p k s", k=FC)
                    dve.tensor_tensor(aT[:, b], sil, mid[:, :, BLK:2 * BLK], ALU.mult).then_inc(s["act_cols"], 1)

                def add_back(e):
                    for n in range(2 * NT):
                        dve.wait_ge(s["back_full"], e * (2 * NT) + (n + 1))
                        i, hh = n // 2, n % 2
                        a = acc[:, i, HALF * hh:HALF * (hh + 1)]
                        dve.tensor_tensor(a, a, psK[n % 3][:, :], ALU.add).then_inc(s["back_out"], 1)

                select(s, 0)
                gather_out(0, 0)
                dve.wait_ge(zeroed, l + 2)
                with dve.Fori(0, NE // 2) as i:
                    for u in range(2):
                        dve.wait_ge(s["comb_full"], i * 2 + (u + 1))
                        select(s, 1 - u)
                        gather_out(i * 2 + (u + 1), 1 - u)
                        hidden(i * 2 + u, u)
                        add_back(i * 2 + u)
                add_back(NE)
                dve.wait_ge(plan_ready, l + 1)
                blocks = dve.value_load(plan_i[0:1, NOV:NOV + 1], min_val=0, max_val=NOV)
                with dve.Fori(0, NOV) as j:
                    with dve.If(j < blocks):
                        e = j + NE
                        hidden(e, 0)
                        dve.wait_ge(s["comb_full"], e + 2)
                        select(s, 0)
                        gather_out(e + 1, 0)
                        add_back(e + 1)
                        dve.drain().then_inc(s["over_done"], 1)
                settle()
                dve.wait_ge(act_emptied, turn[("gate", 2 * l + 1, 1, 1)][3])
                for i in range(NT):
                    dve.tensor_tensor(acc[:, i, :], acc[:, i, :], gate_b[:, min(i, 1), :], ALU.mult)
                settle()
                for i in range(NT):
                    last = dve.tensor_tensor(x[:, i, :], x[:, i, :], acc[:, i, :], ALU.add)
                last.then_inc(x_ready, 1)

            start_at_one(dve, "dve")
            b = stage_bank("rows", dve)
            dve.wait_ge(zeroed, 1)
            dve.tensor_copy(colv[:, :], b[:, 0:N_ROWS])
            dve.tensor_copy(bcol[:, :], b[:, P:P + N_BROWS])
            for k, r in enumerate((R_CCTX, R_C)):
                last = dve.tensor_copy(cond[:, :, k], b[:, 2 * P + r:2 * P + r + KT])
            emptied_inc(last)
            norm(0)
            ada(0, 0, ADA_C)
            affine(0)
            for cc in range(len(W_IN_COLS)):
                for i in range(NT):
                    if turn[("z", cc, i)][2] == "dve":
                        b = stage_bank(("z", cc, i), dve)
                        w, a = W_IN_COLS[cc], sum(W_IN_COLS[:cc])
                        emptied_inc(dve.tensor_copy(z[:, i, a:a + w], b[:, 0:w]))
            dve.wait_ge(params_in, loads[params_in])
            dve.wait_ge(qk_squares, 1)
            dve.tensor_reduce(ssq, sq[:, :, :].rearrange("p t (h d) -> p (t h) d", d=HD), AX.X, ALU.add)\
               .then_inc(qk_sums, 1)
            dve.wait_ge(qk_rms_ready, 1)
            dve.reciprocal(rsq, rsq)
            settle()
            zq = z[:, :, 0:QKW].rearrange("p t (h d) -> p t h d", d=HD)
            rq = rsq.rearrange("p (t h) -> p t h", t=NT).unsqueeze(3)
            dve.tensor_tensor(zq, zq, bc(rq, NT, NQK, HD), ALU.mult)
            settle()
            for i in range(NT):
                dve.tensor_tensor(qk[:, i, 0:AW].rearrange("p (c k d) -> p k c d", k=NKV, d=HD),
                                  z[:, i, 0:AW].rearrange("p (k c d) -> p k c d", k=NKV, d=HD),
                                  bc(qk_gain[:, 0, :].unsqueeze(1).unsqueeze(1), NKV, NH // NKV, HD), ALU.mult)
            kz = zq[:, :, NH:NQK]
            dve.tensor_tensor(qk[:, :, AW:QKW].rearrange("p t (h d) -> p t h d", d=HD), kz,
                              bc(qk_gain[:, 1, :].unsqueeze(1).unsqueeze(1), NT, NKV, HD), ALU.mult)\
               .then_inc(kv_out_ready, 1)
            settle()
            dve.wait_ge(special_in, 16)
            for i in (1, 2):
                zi = qk[:, i, :].rearrange("p (h d) -> p h d", d=HD)
                cosr = att("cos")[:, (i - 1) * HD:i * HD].unsqueeze(1)
                r0 = rot0.rearrange("p (h d) -> p h d", d=HD)
                dve.tensor_tensor(r0, zi, bc(cosr, NQK, HD), ALU.mult)
                z5 = qk[:, i, :].rearrange("p (h a b f) -> p h a b f", a=2, b=2, f=HD // 4)
                r5 = rot1.rearrange("p (h a b f) -> p h a b f", a=2, b=2, f=HD // 4)
                s5 = att("sin")[:, (i - 1) * HD:i * HD].rearrange("p (a b f) -> p a b f", a=2, b=2)
                for b2 in range(2):
                    sn = s5[:, :, b2, :].unsqueeze(1)
                    dve.tensor_tensor(r5[:, :, :, b2, :], z5[:, :, :, 1 - b2, :], bc(sn, NQK, 2, HD // 4), ALU.mult)
                settle()
                last = dve.tensor_tensor(zi, r0, rot1.rearrange("p (h d) -> p h d", d=HD), ALU.add)
                settle()
            last.then_inc(qk_ready, 1)
            ada(1, 0, 6)

            mx, nmx, den, es = small[:, 0:8], small[:, 8:16], small[:, 16:24], small[:, 24:32]

            def scores(i):
                w = SEQ if i == 0 else TOK
                for cc in range(NH // 2):
                    for hd in (cc, cc + NH // 2):
                        b = stage_bank(("score", i, hd), dve)
                        if i == 0:
                            emptied_inc(dve.tensor_scalar(PC[:, hd, :], b[:, 0:w], HD ** -0.5, None, ALU.mult))
                        else:
                            m = att("mask")[:, (i - 1) * TOK:i * TOK]
                            emptied_inc(dve.scalar_tensor_tensor(PL[:, hd, :], b[:, 0:w], HD ** -0.5, m, ALU.mult, ALU.add))
                settle()
                pr = PC if i == 0 else PL
                dve.tensor_reduce(mx, pr[:, :, 0:w], AX.X, ALU.max)
                settle()
                dve.tensor_tensor(mx, mx, sink[:, :], ALU.max)
                settle()
                dve.tensor_scalar(nmx, mx, -1.0, None, ALU.mult)
                dve.tensor_tensor(es, sink[:, :], mx, ALU.subtract).then_inc(p_max, 1)

            def normalize(i):
                w = SEQ if i == 0 else TOK
                dve.wait_ge(p_exp, i + 1)
                dve.tensor_tensor(den, den, es, ALU.add)
                settle()
                dve.reciprocal(den, den)
                settle()
                pr = PC if i == 0 else PL
                for hd in range(NH):
                    last = dve.tensor_scalar(pr[:, hd, 0:w], pr[:, hd, 0:w], den[:, hd:hd + 1], None, ALU.mult)
                last.then_inc(p_ready, 1)

            def attended(i):
                b = stage_bank(("oT", i), dve)
                emptied_inc(dve.tensor_copy(T[:, 0:4, i * P:(i + 1) * P], b[:, :].rearrange("p (c n) -> p c n", c=4)))

            scores(0)
            normalize(0)
            dve.wait_ge(kv_out_done, 32)
            scores(1)
            normalize(1)
            ada(1, 6, 9)
            attended(0)
            attended(1)
            scores(2)
            ada(1, 9, ADA_C)
            diagonals(0)
            normalize(2)
            attended(2)
            gated_add(0)
            dve.drain().then_inc(special_free, 1)
            norm(1)
            affine(1)
            route(0)
            moe(0)
            norm(2)
            affine(2)
            diagonals(2)
            for f in range(KT):
                if turn[("uT", f)][2] == "dve":
                    b = stage_bank(("uT", f), dve)
                    emptied_inc(dve.tensor_copy(uT[:, f, :], b[:, 0:TOK]))
            for i in range(NT):
                for g in range(FG):
                    if turn[("v", i, g)][2] == "dve":
                        b = stage_bank(("v", i, g), dve)
                        emptied_inc(dve.tensor_copy(v[:, i, g, :], b[:, :]))
            for f in range(KT):
                if turn[("fT", f)][2] == "dve":
                    b = stage_bank(("fT", f), dve)
                    emptied_inc(dve.tensor_copy(T[:, f, :], b[:, 0:TOK]))
            gated_add(1)
            norm(3)
            affine(3)
            route(1)
            moe(1)

        @block.tensor
        def _(pe):
            def begin(key):
                bank, n, who, k, before = turn[key]
                if before is not None:
                    pe.wait_ge(emptied[before[0]], before[1])
                return banks[bank]

            def done_by(*keys):
                for key in keys:
                    pe.wait_ge(emptied[turn[key][2]], turn[key][3])

            def item(n, w=HALF):
                pe.wait_ge(arrived[n % NS], 16 * (n // NS + 1))
                return ring[:, n % NS, 0:KT * w].rearrange("p (k n) -> p k n", k=KT)

            def ada(l, n0, c0, c1):
                def columns(cc):
                    done_by(("ada", l, cc))
                    b = begin(("adaT", l, cc))
                    for q in range(4):
                        last = pe.transpose(b[:, q * P:(q + 1) * P], ada_row[:, cc % 2, q * P:(q + 1) * P], ident)
                    last.then_inc(full, 1)

                for cc in range(c0, c1):
                    w = item(n0 + cc)
                    b = begin(("ada", l, cc))
                    for k in range(KT):
                        q = k % 4
                        last = pe.matmul(b[32 * q:32 * q + 32, :], cond[:, k, :], w[:, k, :],
                                         start=(k < 4), stop=(k >= 4), skip_group_check=True)
                    last.then_inc(full, 1)
                    if cc > 0:
                        columns(cc - 1)
                if c1 == ADA_C:
                    columns(c1 - 1)

            def norm(s):
                pe.wait_ge(normed, s + 1)
                for j in range(KT):
                    b = begin(("norm", s, j))
                    for t in range(NT):
                        last = pe.transpose(b[:, t * P:(t + 1) * P], h[:, t, j * P:(j + 1) * P], ident)
                    last.then_inc(full, 1)

            def normed_cols(s):
                done_by(("norm", s, KT - 1), ("norm", s, KT - 2))

            def gate(s):
                for k in range(2):
                    for hh in range(2):
                        n = 2 * k + hh
                        b = begin(("gate", s, k, hh))
                        pe.wait_ge(diag_ready, 4 * s + n + 1)
                        pe.matmul(b[:, :], con("ones"), diag[:, n % 2, :], start=True, stop=True).then_inc(full, 1)

            def project(l, n0):
                for hh in range(2):
                    w = item(n0 + hh)
                    for i in range(NT):
                        b = begin(("out", l, hh, i))
                        for k in range(KT):
                            last = pe.matmul(b[:, :], T[:, k, i * P:(i + 1) * P], w[:, k, :], start=(k == 0), stop=(k == KT - 1))
                        last.then_inc(full, 1)

            def route(l):
                normed_cols(2 * l + 1)
                pe.wait_ge(params_in, loads[params_in])
                b = begin(("router", l))
                for t in range(NT):
                    for k in range(KT):
                        last = pe.matmul(b[:, t * (NG + NE):(t + 1) * (NG + NE)], T[:, k, t * P:(t + 1) * P],
                                         router_w[:, l, k, :], start=(k == 0), stop=(k == KT - 1))
                last.then_inc(full, 1)
                for t in range(NT):
                    for hh in range(2):
                        b = begin(("tokens", l, t, hh))
                        for q in range(4):
                            last = pe.transpose(b[:, q * P:(q + 1) * P], T[:, 4 * hh + q, t * P:(t + 1) * P], ident)
                        last.then_inc(full, 1)
                b = begin(("rank", l))
                pe.wait_ge(ms_ready, l + 1)
                for t in range(NT + 1):
                    out = b[:, t * NE:(t + 1) * NE]
                    for q in range(min(t + 1, NT)):
                        own = q == t
                        last = pe.matmul(out, con("before") if own else con("ones"), Ms[:, q, :],
                                         start=(q == 0), stop=(q == min(t, NT - 1)))
                last.then_inc(full, 1)
                gate(2 * l + 1)

            def moe(l):
                s = per_layer[l]
                n0 = n_exp[l]
                pe.wait_ge(zeroed, l + 2)
                pe.wait_ge(act_emptied, marks[l]["act"])
                pe.wait_ge(dve_emptied, marks[l]["dve"])

                def gather(e, b):
                    pe.wait_ge(s["sel_ready"], e + 1)
                    for k in range(KT):
                        for t in range(NT):
                            last = pe.matmul(psX[:, k * BLK:(k + 1) * BLK], h[:, t, k * P:(k + 1) * P], Sel[:, b, t, :],
                                             start=(t == 0), stop=(t == NT - 1))
                    last.then_inc(s["gathered"], 1)

                def up(e, b, w1, w3):
                    pe.wait_ge(s["x_cols"], e + 1)
                    pe.wait_ge(s["up_out"], e + 1)
                    for k in range(KT):
                        for q, w in enumerate((w1, w3)):
                            last = pe.matmul(psU[BLK * q:BLK * (q + 1), :], xT[:, b, k, :], w[:, k, :],
                                             start=(k == 0), stop=(k == KT - 1), skip_group_check=True)
                    last.then_inc(s["up_full"], 1)

                def middle(e, b):
                    pe.wait_ge(s["up_out"], e + 2)
                    pe.wait_ge(s["act_cols"], e + 1)
                    for k in range(FC):
                        last = pe.transpose(psT[:, k * P:(k + 1) * P], up_s[:, b, k * P:(k + 1) * P], ident)
                    last.then_inc(s["mid_full"], 1)
                    pe.wait_ge(s["comb_out"], e + 1)
                    for t in range(NT):
                        last = pe.transpose(psC[:, t * P:(t + 1) * P], CT[:, b, t].rearrange("p d s -> p (d s)"), ident)
                    last.then_inc(s["comb_full"], 1)

                def down(b, w2, k):
                    for hh in range(2):
                        last = pe.matmul(psD[BLK * hh:BLK * (hh + 1), :], aT[:, b, k, :], w2[:, k, HALF * hh:HALF * (hh + 1)],
                                         start=(k == 0), stop=(k == FC - 1), skip_group_check=True)
                    return last

                def back(e, b, t):
                    for hh in range(2):
                        n = 2 * t + hh
                        pe.wait_ge(s["back_out"], e * (2 * NT) + (max(n - 2, 0) + 1))
                        pe.matmul(psK[n % 3][:, :], Cs[BLK * hh:BLK * (hh + 1), b, t * P:(t + 1) * P],
                                  ys[BLK * hh:BLK * (hh + 1), b, :], start=True, stop=True).then_inc(s["back_full"], 1)

                gather(0, 0)
                with pe.Fori(0, NE // 2) as i:
                    for u in range(2):
                        e = i * 2 + u
                        ws = []
                        for m in range(3):
                            n = n0 + 3 * u + m
                            ws.append((n % NS, n // NS))
                        w1 = ring[:, ws[0][0], :].rearrange("p (k n) -> p k n", k=KT)
                        w3 = ring[:, ws[1][0], :].rearrange("p (k n) -> p k n", k=KT)
                        w2 = ring[:, ws[2][0], :].rearrange("p (k n) -> p k n", k=FC)
                        for m in range(2):
                            pe.wait_ge(arrived[ws[m][0]], i * 16 + 16 * (ws[m][1] + 1))
                        up(e, u, w1, w3)
                        gather(e + 1, 1 - u)
                        middle(e, u)
                        pe.wait_ge(arrived[ws[2][0]], i * 16 + 16 * (ws[2][1] + 1))
                        for k in range(FC):
                            if k == 0:
                                pe.wait_ge(s["down_out"], e + 1)
                            if k < NT:
                                back(e, 1 - u, k)
                            if k == 0:
                                pe.wait_ge(s["act_cols"], e + 2)
                            last = down(u, w2, k)
                        last.then_inc(s["down_full"], 1)
                pe.wait_ge(s["comb_out"], NE + 1)
                pe.wait_ge(s["down_out"], NE + 1)
                for t in range(NT):
                    back(NE, 1, t)
                pe.wait_ge(plan_ready, l + 1)
                blocks = pe.value_load(plan_i[0:1, NOV:NOV + 1], min_val=0, max_val=NOV)
                with pe.Fori(0, NOV) as j:
                    with pe.If(j < blocks):
                        e = j + NE
                        pe.wait_ge(s["over_in"], j * 48 + 48)
                        up(e, 0, ring[:, 0, :].rearrange("p (k n) -> p k n", k=KT),
                           ring[:, 1, :].rearrange("p (k n) -> p k n", k=KT))
                        middle(e, 0)
                        pe.wait_ge(s["act_cols"], e + 2)
                        pe.wait_ge(s["down_out"], e + 1)
                        for k in range(FC):
                            last = down(0, ring[:, 2, :].rearrange("p (k n) -> p k n", k=FC), k)
                        last.then_inc(s["down_full"], 1)
                        gather(e + 1, 0)
                        pe.wait_ge(s["down_out"], e + 2)
                        pe.wait_ge(s["comb_out"], e + 2)
                        for t in range(NT):
                            back(e + 1, 0, t)

            start_at_one(pe, "pe")
            pe.wait_ge(small_in, loads[small_in])
            pe.wait_ge(cond_rows, 1)
            b = begin("rows")
            pe.transpose(b[:, 0:N_ROWS], rows[:, :], ident[0:N_ROWS, 0:N_ROWS])
            pe.transpose(b[:, P:P + N_BROWS], brows[:, :], ident[0:N_BROWS, 0:N_BROWS])
            pe.transpose(b[:, 2 * P:2 * P + N_ROWS], rows_silu[:, :], ident[0:N_ROWS, 0:N_ROWS]).then_inc(full, 1)
            done_by("rows")
            ada(0, N_ADA0, 0, ADA_C)
            norm(0)
            normed_cols(0)
            for cc in range(len(W_IN_COLS)):
                wd = W_IN_COLS[cc]
                w = item(N_WIN + cc, wd)
                for i in range(NT):
                    b = begin(("z", cc, i))
                    for k in range(KT):
                        last = pe.matmul(b[:, 0:wd], T[:, k, i * P:(i + 1) * P], w[:, k, :], start=(k == 0), stop=(k == KT - 1))
                    last.then_inc(full, 1)
            done_by(("z", 2, 2), ("z", 2, 1))
            pe.wait_ge(special_in, 16)
            pe.wait_ge(params_in, loads[params_in])
            U0 = AW + 2 * KVW

            def pooled_map(g):
                done_by(("pool", g))
                b = begin(("pooled", g))
                pe.matmul(b[:, 0:TOK], pool_ws[:, g, :], pooled[:, g % 2, :], start=True, stop=True).then_inc(full, 1)

            for g in range(NPG):
                b = begin(("pool", g))
                cs = slice(U0 + g * P, U0 + (g + 1) * P)
                pe.matmul(b[:, 0:SEQ], z[:, 0, cs], att("band_ctx")[:, g * P:(g + 1) * P], start=True, stop=True)
                bl = att("band_lat").rearrange("p (g s t) -> p g s t", g=NPG, s=2)
                for q in range(2):
                    last = pe.matmul(b[:, SEQ:TOK], z[:, 1 + q, cs], bl[:, g, q, :], start=(q == 0), stop=(q == 1))
                last.then_inc(full, 1)
                if g > 0:
                    pooled_map(g - 1)
            pooled_map(NPG - 1)
            ada(1, N_ADA1, 0, 6)
            pe.wait_ge(qk_ready, 1)
            for cc in range(NH // 2):
                b = begin(("qT", cc))
                for i in range(NT):
                    last = pe.transpose(b[:, i * P:(i + 1) * P], qk[:, i, cc * P:(cc + 1) * P], ident)
                last.then_inc(full, 1)
            b = begin("kT")
            for i in range(NT):
                pe.transpose(b[:, i * P:(i + 1) * P], qk[:, i, AW:QKW], ident)
            pe.transpose(b[:, TOK:TOK + PAST], ckT_in[:, :], ident).then_inc(full, 1)
            done_by("kT")

            def scores(i):
                for cc in range(NH // 2):
                    for kv in range(2):
                        b = begin(("score", i, cc + 4 * kv))
                        rows_ = slice(HD * kv, HD * (kv + 1))
                        q = qT[rows_, cc, i * P:(i + 1) * P]
                        if i == 0:
                            last = pe.matmul(b[:, 0:SEQ], q, kT[rows_, 0:SEQ], start=True, stop=True)
                        else:
                            last = pe.matmul(b[:, 0:TOK], q, kT[rows_, SEQ:TOK + PAST], start=True, stop=True)
                        last.then_inc(full, 1)

            def values(i):
                pe.wait_ge(p_ready, i + 1)
                keys = [0] if i == 0 else [1, 2, NT]

                def turn_head(hd):
                    b = begin(("PT", i, hd))
                    for n in range(len(keys)):
                        pr = PC[:, hd, :] if i == 0 else PL[:, hd, n * P:(n + 1) * P]
                        last = pe.transpose(b[:, n * P:(n + 1) * P], pr, ident)
                    last.then_inc(full, 1)

                if turn[("oT", i)][4] is not None:
                    pe.wait_ge(emptied[turn[("oT", i)][4][0]], turn[("oT", i)][4][1])
                ob = banks[7]

                def product(hd):
                    done_by(("PT", i, hd))
                    kv, r0 = hd // 4, HD * (hd % 2)
                    out = ob[r0:r0 + HD, (hd // 2) * P:(hd // 2 + 1) * P]
                    for n, kt in enumerate(keys):
                        vals = cv[:, HD * kv:HD * (kv + 1)] if kt == NT else \
                            z[:, kt, AW + KVW + HD * kv:AW + KVW + HD * (kv + 1)]
                        last = pe.matmul(out, vals, PT[:, hd % 2, n * P:(n + 1) * P],
                                         start=(n == 0), stop=(n == len(keys) - 1), skip_group_check=True)
                    last.then_inc(pv_done, 1)

                for hd in range(NH):
                    turn_head(hd)
                    if hd > 0:
                        product(hd - 1)
                product(NH - 1)
                pe.drain().then_inc(full, 1)

            scores(0)
            scores(1)
            ada(1, N_ADA1, 6, 9)
            values(0)
            values(1)
            scores(2)
            ada(1, N_ADA1, 9, ADA_C)
            gate(0)
            values(2)
            done_by(("oT", 2), ("pooled", NPG - 1))
            project(0, N_WOUT)
            norm(1)
            route(0)
            moe(0)
            pe.wait_ge(x_ready, 2)
            norm(2)
            gate(2)
            normed_cols(2)
            for cc in range(2):
                w = item(N_FIN + cc)
                for q in range(4):
                    b = begin(("uT", 4 * cc + q))
                    for k in range(KT):
                        last = pe.matmul(b[:, 0:TOK], w[:, k, q * P:(q + 1) * P], T[:, k, :], start=(k == 0), stop=(k == KT - 1))
                    last.then_inc(full, 1)
            pe.wait_ge(special_in, 32)
            done_by(("uT", KT - 1), ("uT", KT - 2))
            for i in range(NT):
                for g in range(FG):
                    b = begin(("v", i, g))
                    for q in range(2):
                        last = pe.matmul(b[:, :], uT[:, 2 * g + q, i * P:(i + 1) * P],
                                         four("feat")[:, q * 2 * FD:(q + 1) * 2 * FD], start=(q == 0), stop=(q == 1))
                    last.then_inc(full, 1)
            done_by(("v", NT - 1, FG - 1), ("v", NT - 1, FG - 2))
            for f in range(KT):
                g, q0 = f // 2, (f % 2) * P
                b = begin(("fT", f))
                for part in range(2):
                    pe.matmul(b[:, 0:SEQ], v[:, 0, g, part * FD + q0:part * FD + q0 + P],
                              four("time_ctx")[:, part * SEQ:(part + 1) * SEQ], start=(part == 0), stop=(part == 1))
                tl = four("time_lat").rearrange("p (s c t) -> p s c t", s=2, c=2)
                for n in range(4):
                    q, part = n // 2, n % 2
                    last = pe.matmul(b[:, SEQ:TOK], v[:, 1 + q, g, part * FD + q0:part * FD + q0 + P],
                                     tl[:, q, part, :], start=(n == 0), stop=(n == 3))
                last.then_inc(full, 1)
            done_by(("fT", KT - 1), ("fT", KT - 2))
            project(1, N_FOUT)
            norm(3)
            route(1)
            moe(1)


NAMES = ["x_prompt", "x_sample", "cache_k", "cache_v", "c", "c_ctx", "ada_w", "ada_b", "norm_mix",
         "norm_ffn", "a_w_in", "a_q_norm", "a_k_norm", "a_sink", "pool_w", "pool_scale", "a_w_out",
         "f_w_in", "f_w_out", "router_g_w", "router_g_b", "router_e_w", "router_e_b", "moe_w1",
         "moe_w3", "moe_w2"]


def kernel(**inputs):
    import concourse.bacc as bacc
    from concourse.bass_utils import run_bass_kernel_spmd

    nc = bacc.Bacc("TRN2", target_bir_lowering=False, num_devices=1)
    arrays, args = {}, []
    for name in NAMES:
        arrays[name] = np.ascontiguousarray(inputs[name])
    for name, columns in (("const", constant_columns()), ("att_const", attention_columns()),
                          ("four_const", fourier_columns())):
        arrays[name] = np.concatenate([np.asarray(v, np.float32) for v in columns.values()], 1)
    for name, a in arrays.items():
        args.append(nc.dram_tensor(f"in_{name}", a.shape, F32, kind="ExternalInput").ap())
    outs = {"y_prompt": (1, SEQ, D), "y_sample": (1, DEC, D),
            "new_cache_k": (1, 1, SEQ, NKV, HD), "new_cache_v": (1, 1, SEQ, NKV, HD)}
    for name, shape in outs.items():
        args.append(nc.dram_tensor(name, shape, F32, kind="ExternalOutput").ap())
    build(nc, *args)
    got = run_bass_kernel_spmd(nc, [{f"in_{k}": a for k, a in arrays.items()}], core_ids=[0]).results[0]
    return tuple(got[name] for name in outs)
```

```python
from contextlib import ExitStack

import concourse.bass as bass
from concourse import mybir
import numpy as np

F32 = mybir.dt.float32
I32 = mybir.dt.int32
ALU = mybir.AluOpType
ACT = mybir.ActivationFunctionType
AX = mybir.AxisListType

P = 128
D = 1024
KT = D // P
L = 2
SEQ = 128
DEC = 256
TOK = SEQ + DEC
NT = TOK // P
PAST = 128
HD = 64
NH = 8
NKV = 2
AW = NH * HD
KVW = NKV * HD
PW = 512
NPG = 4
ZW = AW + 2 * KVW + PW
QKW = AW + KVW
NQK = NH + NKV
NE = 16
NG = 4
EPG = 4
DE = 512
FC = DE // P
FG = 4
FD = D // FG
HALF = 512
BLK = 64
PAIRS = 2 * TOK
NPAIR = NE // 2
NOV = (PAIRS - NE) // BLK
NTHR = -(-TOK // BLK) - 1
EPS = 1e-6
GRID_W = 64
WINDOW = 128
LOWEST = -3.0e38

NS = 6
SLOT = KT * HALF
ADA_C = 6 * D // HALF
W_IN_COLS = [512, 512, 256]


def constant_columns():
    out = {}
    p = np.arange(P)
    out["ident"] = np.eye(P)
    out["before"] = (p[:, None] < p[None, :]).astype(float)
    out["ones"] = np.ones((P, P))
    rows = {
        "iota": np.arange(2 * BLK),
        "eps": [EPS],
        "desc": np.arange(NG, 0, -1),
        "limit": BLK * np.arange(1, NTHR + 1),
        "tri": (np.arange(NE)[None, :] < np.arange(NE)[:, None]).astype(float).ravel(),
        "jrow": np.arange(NOV),
        "first": BLK * np.arange(NE),
        "shift": BLK * NE - BLK - BLK * np.arange(NE),
    }
    for k, v in rows.items():
        out[k] = np.broadcast_to(np.asarray(v, float), (P, len(v)))
    return out


def attention_columns():
    out = {}
    tok = np.arange(DEC)
    half, nf = HD // 2, HD // 4
    freqs = (np.float32(10000.0) ** (-np.arange(nf, dtype=np.float32) / np.float32(nf))).astype(np.float32)
    cos, sin = np.zeros((DEC, HD)), np.zeros((DEC, HD))
    for n, pos in enumerate((tok // GRID_W, tok % GRID_W)):
        ang = (pos.astype(np.float32)[:, None] * freqs[None, :]).astype(np.float32)
        c, s = np.cos(ang), np.sin(ang)
        cos[:, half * n:half * (n + 1)] = np.concatenate([c, c], 1)
        sin[:, half * n:half * (n + 1)] = np.concatenate([-s, s], 1)
    out["cos"] = cos.reshape(2, P, HD).transpose(1, 0, 2).reshape(P, -1)
    out["sin"] = sin.reshape(2, P, HD).transpose(1, 0, 2).reshape(P, -1)
    q, k = tok[:, None], tok[None, :]
    mask = np.where(np.abs(q - k) <= WINDOW, 0.0, -1e30)
    mask = np.concatenate([mask, np.zeros((DEC, PAST))], 1)
    out["mask"] = mask.reshape(2, P, DEC + PAST).transpose(1, 0, 2).reshape(P, -1)

    def band(T, w):
        t = np.arange(T)
        lo, hi = np.clip(t - w // 2, 0, T), np.clip(t + w // 2, 0, T)
        s = np.arange(T)[:, None]
        m = ((s >= lo) & (s < hi)) / (hi - lo).astype(float) - np.eye(T)
        return m

    out["band_ctx"] = np.concatenate([band(SEQ, w) for w in (2, 4, 8, 16)], 1)
    lat = np.stack([band(DEC, w) for w in (2, 4, 8, 16)])
    out["band_lat"] = lat.reshape(NPG, 2, P, DEC).transpose(2, 0, 1, 3).reshape(P, -1)
    return out


def fourier_columns():
    out = {}

    def dft(n, scale):
        a = 2 * np.pi * (np.outer(np.arange(n), np.arange(n)) % n) / n
        return np.cos(a) * scale, np.sin(a) * scale

    c, s = dft(FD, FD ** -0.5)
    out["feat"] = np.concatenate([c, s], 1).reshape(2, P, 2 * FD).transpose(1, 0, 2).reshape(P, -1)
    c, s = dft(SEQ, SEQ ** -0.5)
    out["time_ctx"] = np.concatenate([c, -s], 1)
    c, s = dft(DEC, DEC ** -0.5)
    out["time_lat"] = np.concatenate([c, -s], 1).reshape(2, P, 2 * DEC).transpose(1, 0, 2).reshape(P, -1)
    return out


def places(columns):
    at, out = 0, {}
    for k, v in columns.items():
        out[k] = (at, v.shape[1])
        at += v.shape[1]
    return out, at


CONST, N_CONST = places(constant_columns())
ATT, N_ATT = places(attention_columns())
FOUR, N_FOUR = places(fourier_columns())


class Turns:

    def __init__(self, banks):
        self.banks, self.at, self.filled = banks, 0, 0
        self.emptied = {"act": 0, "dve": 0}
        self.last = {}
        self.of = {}

    def add(self, key, who, bank=None):
        if bank is None:
            bank = self.banks[self.at % len(self.banks)]
            self.at += 1
        self.filled += 1
        self.emptied[who] += 1
        self.of[key] = (bank, self.filled, who, self.emptied[who], self.last.get(bank))
        self.last[bank] = (who, self.emptied[who])

    def all_free(self):
        self.last = {}


def plan():
    t = Turns(list(range(7)))
    marks = {}

    def ada(l, c0, c1):
        for c in range(c0, c1):
            t.add(("ada", l, c), "act")
            if c > 0:
                t.add(("adaT", l, c - 1), "dve")
        if c1 == ADA_C:
            t.add(("adaT", l, c1 - 1), "dve")

    def norm(s):
        for j in range(KT):
            t.add(("norm", s, j), "act" if j % 2 else "dve")

    def gate(s):
        for c in range(2):
            for h in range(2):
                t.add(("gate", s, c, h), "act")

    def project(l):
        for h in range(2):
            for i in range(NT):
                t.add(("out", l, h, i), "dve")

    def route(l):
        t.add(("router", l), "dve")
        for i in range(NT):
            for h in range(2):
                t.add(("tokens", l, i, h), "act")
        t.add(("rank", l), "dve")
        gate(2 * l + 1)

    t.add("rows", "dve")
    ada(0, 0, ADA_C)
    norm(0)
    for c in range(len(W_IN_COLS)):
        for i in range(NT):
            t.add(("z", c, i), "act" if i % 2 else "dve")
    for g in range(NPG):
        t.add(("pool", g), "act")
        if g > 0:
            t.add(("pooled", g - 1), "act")
    t.add(("pooled", NPG - 1), "act")
    ada(1, 0, 6)
    for c in range(NH // 2):
        t.add(("qT", c), "act")
    t.add("kT", "act")

    def scores(i):
        for c in range(NH // 2):
            for h in (c, c + NH // 2):
                t.add(("score", i, h), "dve")

    def values(i):
        for h in range(NH):
            t.add(("PT", i, h), "act")
        t.add(("oT", i), "dve", bank=7)

    scores(0)
    scores(1)
    ada(1, 6, 9)
    values(0)
    values(1)
    scores(2)
    ada(1, 9, ADA_C)
    gate(0)
    values(2)
    project(0)
    norm(1)
    route(0)
    marks[0] = dict(t.emptied)
    t.all_free()
    norm(2)
    gate(2)
    for f in range(KT):
        t.add(("uT", f), "act" if f % 2 else "dve")
    for i in range(NT):
        for g in range(FG):
            t.add(("v", i, g), "act" if g % 2 else "dve")
    for f in range(KT):
        t.add(("fT", f), "act" if f % 2 else "dve")
    project(1)
    norm(3)
    route(1)
    marks[1] = dict(t.emptied)
    return t.of, marks


def build(nc, x_prompt, x_sample, cache_k, cache_v, c, c_ctx, ada_w, ada_b, norm_mix, norm_ffn,
          a_w_in, a_q_norm, a_k_norm, a_sink, pool_w, pool_scale, a_w_out, f_w_in, f_w_out,
          router_g_w, router_g_b, router_e_w, router_e_b, moe_w1, moe_w3, moe_w2,
          const, att_const, four_const, y_prompt, y_sample, new_k, new_v):
    turn, marks = plan()

    def cols(w, a, b):
        return w[:, a:b].rearrange("(k p) n -> p k n", p=P)

    ada_items = [[cols(ada_w[l], HALF * n, HALF * (n + 1)) for n in range(ADA_C)] for l in range(L)]
    w_in_items, at = [], 0
    for n in W_IN_COLS:
        w_in_items.append(cols(a_w_in[0], at, at + n))
        at += n
    halves = lambda w: [cols(w, 0, HALF), cols(w, HALF, D)]
    before0 = ada_items[0] + w_in_items + ada_items[1] + halves(a_w_out[0])
    before1 = halves(f_w_in[0]) + halves(f_w_out[0])
    N_ADA0, N_WIN, N_ADA1 = 0, ADA_C, ADA_C + 3
    N_WOUT = N_ADA1 + ADA_C
    N_EXP0 = len(before0)
    N_FIN = N_EXP0 + 3 * NE
    N_FOUT = N_FIN + 2
    N_EXP1 = N_FIN + len(before1)
    n_exp = [N_EXP0, N_EXP1]

    R_MIX, R_FFN, R_CCTX, R_C, R_PS = 0, L * KT, 2 * L * KT, 2 * L * KT + KT, 2 * L * KT + 2 * KT
    N_ROWS = R_PS + NPG
    N_BROWS = L * 6 * KT

    ctx = ExitStack()
    with ctx:
        def sb(name, shape, dt=F32):
            return ctx.enter_context(nc.sbuf_tensor(name, shape, dt))

        def sem(name):
            return ctx.enter_context(nc.semaphore(name))

        ring = sb("ring", [P, NS, SLOT])
        x = sb("x", [P, NT, D])
        h = sb("h", [P, NT, D])
        T = sb("T", [P, KT, TOK])
        Z = sb("Z", [P, 7168])
        gate_b = sb("gate_b", [P, 2, D])
        special = sb("special", [P, max(N_ATT, N_FOUR)])
        cst = sb("cst", [P, N_CONST])
        ada_row = sb("ada_row", [P, 2, HALF])
        diag = sb("diag", [P, 2, HALF])
        rows = sb("rows", [N_ROWS, P])
        rows_silu = sb("rows_silu", [N_ROWS, P])
        brows = sb("brows", [N_BROWS, P])
        colv = sb("colv", [P, N_ROWS])
        bcol = sb("bcol", [P, N_BROWS])
        cond = sb("cond", [P, KT, 32])
        mcol = sb("mcol", [P, L, 6, KT, 2])
        router_w = sb("router_w", [P, L, KT, NG + NE])
        router_b = sb("router_b", [P, L, NG + NE])
        sink = sb("sink", [P, NH])
        qk_gain = sb("qk_gain", [P, 2, HD])
        pool_ws = sb("pool_ws", [P, NPG, P])
        ckT_in = sb("ckT_in", [P, KVW])
        cv = sb("cv", [P, KVW])
        stat = sb("stat", [P, 2, NT])

        z = Z[:, 0:NT * ZW].rearrange("p (t n) -> p t n", t=NT)
        at = NT * ZW
        qT = Z[:, at:at + 4 * TOK].rearrange("p (c n) -> p c n", c=4)
        at += 4 * TOK
        kT = Z[:, at:at + TOK + PAST]
        at += TOK + PAST
        PT = Z[:, at:at + 2 * TOK].rearrange("p (b n) -> p b n", b=2)
        at += 2 * TOK
        small = sb("small", [P, 96])
        ssq, rsq = small[:, 32:62], small[:, 64:94]
        p_ctx = ring_free = None
        PC = sb("PC", [P, NH, P])
        pooled = PC[:, 0:6, :].rearrange("p a n -> p (a n)").rearrange("p (b n) -> p b n", b=2)
        assert at <= 7168
        hflat = h[:, :, :].rearrange("p t n -> p (t n)")
        PL = hflat[:, 0:NH * TOK].rearrange("p (h n) -> p h n", h=NH)
        sq = hflat[:, 0:NT * QKW].rearrange("p (t n) -> p t n", t=NT)
        rot0 = hflat[:, 0:QKW]
        rot1 = PT.rearrange("p b n -> p (b n)")[:, 0:QKW]
        qk = hflat[:, QKW:(1 + NT) * QKW].rearrange("p (t n) -> p t n", t=NT)
        uT = hflat.rearrange("p (c n) -> p c n", c=KT)
        v = Z[:, 0:NT * FG * 2 * FD].rearrange("p (t g n) -> p t g n", t=NT, g=FG)
        at = 0

        def zone(n):
            nonlocal at
            at += n
            return Z[:, at - n:at]

        at = 0
        B2 = 2 * BLK
        xT = zone(2 * KT * B2).rearrange("p (b k s) -> p b k s", b=2, k=KT)
        up_s = zone(2 * DE).rearrange("p (b n) -> p b n", b=2)
        sil = zone(FC * BLK).rearrange("p (k s) -> p k s", k=FC)
        aT = zone(2 * FC * BLK).rearrange("p (u k s) -> p u k s", u=2, k=FC)
        ys = zone(D)
        Sel = zone(NT * B2).rearrange("p (t s) -> p t s", t=NT)
        CT = zone(2 * NT * B2).rearrange("p (b t s) -> p b t s", b=2, t=NT)
        Cs = zone(2 * TOK).rearrange("p (b n) -> p b n", b=2)
        S12 = special[:, N_FOUR:N_FOUR + 2 * NT * B2].rearrange("p (a t s) -> p a t s", a=2, t=NT)
        assert at <= 7168 and N_FOUR + 2 * NT * B2 <= N_ATT
        acc = T[:, :, :].rearrange("p k n -> p (k n)").rearrange("p (t n) -> p t n", t=NT)
        scratch = special[:, 0:D]

        rt = PC[:, :, :].rearrange("p h n -> p (h n)")
        rat = [0]

        def rtile(*shape):
            n = int(np.prod(shape))
            a = rt[:, rat[0]:rat[0] + n]
            rat[0] += n
            if len(shape) == 1:
                return a
            names = "abcd"[:len(shape)]
            return a.rearrange(f"p ({' '.join(names)}) -> p {' '.join(names)}",
                               **{k: s for k, s in zip(names[:-1], shape[:-1])})

        lg = rtile(NT, NG + NE)
        mg, sg, pg, ml, se, p1, p2 = (rtile(NT) for _ in range(7))
        eg, og, sc4, le, ee, o1, o2, le2 = (rtile(NT, 4) for _ in range(8))
        prod = rtile(NT, 4, 4)
        M12 = rtile(2, NT, NE)
        Ms = rtile(NT, NE)
        G = rtile(NT, NE)
        ge = rtile(NT, NE)
        Gp = rtile(NT, NE)
        G12 = rtile(2, NT)
        c12 = rtile(2, NT)
        cmp5 = rtile(NE, NTHR)
        ovc, ovb, off, incl = (rtile(NE) for _ in range(4))
        eidf = rtile(NOV + 1)
        tri_p = rtile(NE, NE)
        cmp_j = tri_p[:, 0:NOV, :]
        assert rat[0] <= NH * P
        plan_i = sb("plan_i", [P, NOV + 1], I32)

        def con(name, n=None):
            a, w = CONST[name]
            return cst[:, a:a + w]

        def att(name):
            a, w = ATT[name]
            return special[:, a:a + w]

        def four(name):
            a, w = FOUR[name]
            return special[:, a:a + w]

        ident = con("ident")
        banks = [ctx.enter_context(nc.psum_tensor(f"bank{i}", [P, HALF], F32)) for i in range(8)]
        psU, psT = banks[0:2]
        psC = psU
        psX, psD, psK = banks[2:4], banks[4:6], banks[6:8]

        arrived = [sem(f"arrived{i}") for i in range(NS)]
        small_in = sem("small_in")
        params_in = sem("params_in")
        x_in = sem("x_in")
        special_in = sem("special_in")
        special_free = sem("special_free")
        full = sem("full")
        act_emptied = sem("act_emptied")
        dve_emptied = sem("dve_emptied")
        emptied = {"act": act_emptied, "dve": dve_emptied}
        cond_rows = sem("cond_rows")
        cols_ready = sem("cols_ready")
        zeroed = sem("zeroed")
        normed = sem("normed")
        affine_ready = sem("affine_ready")
        rms_ready = sem("rms_ready")
        qk_squares = sem("qk_squares")
        qk_sums = sem("qk_sums")
        qk_rms_ready = sem("qk_rms_ready")
        qk_ready = sem("qk_ready")
        kv_out_ready = sem("kv_out_ready")
        p_max = sem("p_max")
        p_exp = sem("p_exp")
        p_ready = sem("p_ready")
        pv_done = sem("pv_done")
        diag_ready = sem("diag_ready")
        x_ready = sem("x_ready")
        g_shifted = sem("g_shifted")
        g_exp = sem("g_exp")
        ms_ready = sem("ms_ready")
        plan_ready = sem("plan_ready")
        out_done = sem("out_done")
        kv_out_done = sem("kv_out_done")
        steps = ("sel_ready",
                 "gathered",
                 "x_cols",
                 "up_full",
                 "up_out",
                 "mid_full",
                 "silu_out",
                 "act_cols",
                 "comb_full",
                 "comb_out",
                 "down_full",
                 "down_out",
                 "back_full",
                 "back_out")
        pairs = [{k: sem(f"{k}_{l}") for k in steps} for l in range(L)]
        overs = [{k: sem(f"over_{k}_{l}") for k in steps + ("weights", "done")} for l in range(L)]

        block = ctx.enter_context(nc.Block())

        def last_use(n):
            for l in range(L):
                q = n - n_exp[l]
                if 0 <= q < 3 * NE:
                    p, m = q // 6, q % 6
                    if m < 4:
                        return pairs[l]["up_full"], 2 * p + m // 2 + 1
                    return pairs[l]["down_full"], p + 1
            for first, keys in ((N_ADA0, [("ada", 0, c) for c in range(ADA_C)]),
                                (N_WIN, [("z", c, NT - 1) for c in range(len(W_IN_COLS))]),
                                (N_ADA1, [("ada", 1, c) for c in range(ADA_C)]),
                                (N_WOUT, [("out", 0, c, NT - 1) for c in range(2)]),
                                (N_FIN, [("uT", 4 * c + 3) for c in range(2)]),
                                (N_FOUT, [("out", 1, c, NT - 1) for c in range(2)])):
                if first <= n < first + len(keys):
                    return full, turn[keys[n - first]][1]

        def stage_bank(key, e):
            bank, n, who, k, before = turn[key]
            e.wait_ge(full, n)
            return banks[bank]

        @block.sync
        def _(sp):
            def weights(n, src):
                if n >= NS:
                    sp.wait_ge(*last_use(n - NS))
                w = src.shape[2]
                dst = ring[:, n % NS, 0:KT * w].rearrange("p (k n) -> p k n", k=KT)
                sp.dma_start(dst, src).then_inc(arrived[n % NS], 16)

            for n, src in enumerate(before0):
                weights(n, src)
            for l in range(L):
                n0, s, o = n_exp[l], pairs[l], overs[l]
                if l == 1:
                    for n, src in enumerate(before1):
                        weights(N_FIN + n, src)

                def expert(e, k, w):
                    n = n0 + k
                    kk = KT if k < 4 else FC
                    dst = ring[:, n % NS, :].rearrange("p (k n) -> p k n", k=kk)
                    sp.dma_start(dst, w[l, bass.ds(e, 1), :, :].rearrange("a (k p) n -> p (a k) n", p=P))\
                      .then_inc(arrived[n % NS], 16)

                items = [(0, moe_w1), (0, moe_w3), (1, moe_w1), (1, moe_w3), (0, moe_w2), (1, moe_w2)]
                for k, (u, w) in enumerate(items):
                    sp.wait_ge(*last_use(n0 + k - NS))
                    expert(u, k, w)
                with sp.Fori(1, NPAIR) as i:
                    for k, (u, w) in enumerate(items):
                        if k < 4:
                            sp.wait_ge(s["up_full"], i * 2 + (k // 2 - 1))
                        else:
                            sp.wait_ge(s["down_full"], i)
                        expert(i * 2 + u, k, w)
                sp.wait_ge(plan_ready, l + 1)
                blocks = sp.value_load(plan_i[0:1, NOV:NOV + 1], min_val=0, max_val=NOV)
                with sp.Fori(0, NOV) as j:
                    with sp.If(j < blocks):
                        sp.wait_ge(s["down_full"], NPAIR)
                        sp.wait_ge(o["done"], j + 1)
                        ex = sp.value_load(plan_i[0:1, bass.ds(j, 1)], min_val=0, max_val=NE - 1)
                        for m, w in enumerate((moe_w1, moe_w3, moe_w2)):
                            kk = KT if m < 2 else FC
                            dst = ring[:, m, :].rearrange("p (k n) -> p k n", k=kk)
                            sp.dma_start(dst, w[l, bass.ds(ex, 1), :, :].rearrange("a (k p) n -> p (a k) n", p=P))\
                              .then_inc(o["weights"], 16)
                sp.wait_ge(o["done"], blocks + 1)
            sp.wait_ge(x_ready, 4)
            sp.dma_start(y_prompt[0], x[:, 0, :]).then_inc(out_done, 16)
            sp.dma_start(y_sample[0].rearrange("(t p) n -> p t n", p=P), x[:, 1:NT, :]).then_inc(out_done, 16)
            sp.wait_ge(out_done, 32)
            sp.wait_ge(kv_out_done, 32)

        @block.gpsimd
        def _(gp):
            gp.memset(cond[:, :, :], 0.0).then_inc(zeroed, 1)
            gp.wait_ge(kv_out_ready, 1)
            gp.dma_start(new_k[0, 0].rearrange("s h d -> s (h d)"), qk[:, 0, AW:QKW]).then_inc(kv_out_done, 16)
            gp.dma_start(new_v[0, 0].rearrange("s h d -> s (h d)"), z[:, 0, AW + KVW:AW + 2 * KVW]).then_inc(kv_out_done, 16)
            for l in range(L):
                last = turn[("tokens", l, NT - 1, 1)]
                gp.wait_ge(full, last[1])
                gp.memset(acc[:, :, :], 0.0).then_inc(zeroed, 1)

        loads = {small_in: 0, params_in: 0}

        @block.scalar
        def _(act):
            def small_load(dst, src, which=small_in):
                loads[which] += 16
                act.dma_start(dst, src).then_inc(which, 16)

            by_chunk = lambda a: a.rearrange("(k p) -> k p", p=P)
            for l in range(L):
                small_load(rows[R_MIX + l * KT:R_MIX + (l + 1) * KT, :], by_chunk(norm_mix[l]))
                small_load(rows[R_FFN + l * KT:R_FFN + (l + 1) * KT, :], by_chunk(norm_ffn[l]))
            small_load(rows[R_CCTX:R_CCTX + KT, :], by_chunk(c_ctx))
            small_load(rows[R_C:R_C + KT, :], by_chunk(c[0]))
            small_load(rows[R_PS:R_PS + NPG, :], by_chunk(pool_scale[0]))
            small_load(brows[:, :], ada_b.rearrange("l (k p) -> (l k) p", p=P))
            small_load(cst[:, :], const)
            act.dma_start(x[:, 0, :], x_prompt[0]).then_inc(x_in, 16)
            act.dma_start(x[:, 1:NT, :], x_sample[0].rearrange("(t p) n -> p t n", p=P)).then_inc(x_in, 16)
            for l in range(L):
                small_load(router_w[:, l, :, 0:NG], router_g_w[l].rearrange("(k p) n -> p k n", p=P), params_in)
                small_load(router_w[:, l, :, NG:], router_e_w[l].rearrange("(k p) n -> p k n", p=P), params_in)
                small_load(router_b[:, l, 0:NG], router_g_b[l:l + 1, :].to_broadcast([P, NG]), params_in)
                small_load(router_b[:, l, NG:], router_e_b[l:l + 1, :].to_broadcast([P, NE]), params_in)
            small_load(sink[:, :], a_sink[0:1, :].to_broadcast([P, NH]), params_in)
            small_load(qk_gain[:, 0, :], a_q_norm[0:1, :].to_broadcast([P, HD]), params_in)
            small_load(qk_gain[:, 1, :], a_k_norm[0:1, :].to_broadcast([P, HD]), params_in)
            small_load(pool_ws[:, :, :], pool_w[0].rearrange("g c d -> c g d"), params_in)
            small_load(ckT_in[:, :], cache_k[0, 0].rearrange("s h d -> s (h d)"), params_in)
            small_load(cv[:, :], cache_v[0, 0].rearrange("s h d -> s (h d)"), params_in)
            act.dma_start(special[:, 0:N_ATT], att_const).then_inc(special_in, 16)

            def emptied_inc(ins):
                ins.then_inc(act_emptied, 1)

            def sum_squares(n):
                for t in range(NT):
                    act.activation(h[:, t, :], x[:, t, :], ACT.Square, accum_out=stat[:, 0, t:t + 1])
                act.drain()
                act.activation(stat[:, 1, :], stat[:, 0, :], ACT.Sqrt, scale=1.0 / D, bias=con("eps")).then_inc(rms_ready, 1)

            def ada(l, c0, c1):
                for cc in range(c0, c1):
                    b = stage_bank(("ada", l, cc), act)
                    if cc >= 2:
                        act.wait_ge(full, turn[("adaT", l, cc - 2)][1])
                    emptied_inc(act.activation(ada_row[:, cc % 2, :], b[:, :], ACT.Copy))

            def norm(s):
                act.wait_ge(affine_ready, s + 1)
                for j in range(KT):
                    if turn[("norm", s, j)][2] == "act":
                        b = stage_bank(("norm", s, j), act)
                        affine(act, s, j, b)

            def affine(act, s, j, b):
                l, f = s // 2, s % 2
                act.activation(T[:, j, 0:SEQ], b[:, 0:SEQ], ACT.Identity,
                               scale=mcol[:, l, 3 * f + 1, j, 0:1], bias=mcol[:, l, 3 * f, j, 0:1])
                emptied_inc(act.activation(T[:, j, SEQ:TOK], b[:, SEQ:TOK], ACT.Identity,
                                           scale=mcol[:, l, 3 * f + 1, j, 1:2], bias=mcol[:, l, 3 * f, j, 1:2]))

            def gate(s):
                for k in range(2):
                    for hh in range(2):
                        b = stage_bank(("gate", s, k, hh), act)
                        emptied_inc(act.activation(gate_b[:, k, HALF * hh:HALF * (hh + 1)], b[:, :], ACT.Copy))

            def exps(i):
                act.wait_ge(p_max, i + 1)
                w = SEQ if i == 0 else TOK
                for hd in range(NH):
                    pr = PC[:, hd, :] if i == 0 else PL[:, hd, :]
                    act.activation(pr[:, 0:w], pr[:, 0:w], ACT.Exp, bias=small[:, 8 + hd:9 + hd],
                                   accum_out=small[:, 16 + hd:17 + hd])
                act.activation(small[:, 24:32], small[:, 24:32], ACT.Exp).then_inc(p_exp, 1)

            def turned(i):
                w = SEQ if i == 0 else TOK
                for hd in range(NH):
                    b = stage_bank(("PT", i, hd), act)
                    if NH * i + hd >= 2:
                        act.wait_ge(pv_done, NH * i + hd - 1)
                    emptied_inc(act.activation(PT[:, hd % 2, 0:w], b[:, 0:w], ACT.Copy))

            act.wait_ge(small_in, loads[small_in])
            act.activation(rows_silu[:, :], rows[:, :], ACT.Silu).then_inc(cond_rows, 1)
            act.wait_ge(x_in, 32)
            sum_squares(0)
            ada(0, 0, ADA_C)
            norm(0)
            for cc in range(len(W_IN_COLS)):
                for i in range(NT):
                    if turn[("z", cc, i)][2] == "act":
                        b = stage_bank(("z", cc, i), act)
                        w, a = W_IN_COLS[cc], sum(W_IN_COLS[:cc])
                        emptied_inc(act.activation(z[:, i, a:a + w], b[:, 0:w], ACT.Copy))
            act.wait_ge(dve_emptied, turn[("z", 2, 2)][3])
            act.wait_ge(act_emptied, turn[("z", 2, 1)][3])
            act.activation(sq[:, :, :], z[:, :, 0:QKW], ACT.Square).then_inc(qk_squares, 1)
            act.wait_ge(qk_sums, 1)
            act.activation(rsq, ssq, ACT.Sqrt, scale=1.0 / HD, bias=con("eps")).then_inc(qk_rms_ready, 1)
            for g in range(NPG + 1):
                if g < NPG:
                    b = stage_bank(("pool", g), act)
                    if g >= 2:
                        act.wait_ge(full, turn[("pooled", g - 2)][1])
                    emptied_inc(act.activation(pooled[:, g % 2, :], b[:, 0:TOK], ACT.Copy))
                if g > 0:
                    b = stage_bank(("pooled", g - 1), act)
                    emptied_inc(act.activation(T[:, 4 + g - 1, :], b[:, 0:TOK], ACT.Identity,
                                               scale=colv[:, R_PS + g - 1:R_PS + g]))
            ada(1, 0, 6)
            for cc in range(NH // 2):
                b = stage_bank(("qT", cc), act)
                emptied_inc(act.activation(qT[:, cc, :], b[:, 0:TOK], ACT.Copy))
            b = stage_bank("kT", act)
            emptied_inc(act.activation(kT, b[:, 0:TOK + PAST], ACT.Copy))
            exps(0)
            exps(1)
            ada(1, 6, 9)
            turned(0)
            turned(1)
            ada(1, 9, ADA_C)
            gate(0)
            exps(2)
            turned(2)

            def routing_act(l):
                for i in range(NT):
                    for hh in range(2):
                        b = stage_bank(("tokens", l, i, hh), act)
                        emptied_inc(act.activation(h[:, i, HALF * hh:HALF * (hh + 1)], b[:, :], ACT.Copy))

            def moe(l):
                def up_copy(s, e, u):
                    act.wait_ge(s["up_full"], e + 1)
                    act.activation(up_s[:, u, :], psU[:, :], ACT.Copy).then_inc(s["up_out"], 1)

                def silu(s, e):
                    act.wait_ge(s["mid_full"], e + 1)
                    mid = psT[:, :].rearrange("p (k s) -> p k s", k=FC)
                    act.activation(sil, mid[:, :, 0:BLK], ACT.Silu).then_inc(s["silu_out"], 1)

                def comb_copy(s, p, b, w):
                    act.wait_ge(s["comb_full"], p + 1)
                    act.activation(Cs[0:w, b, :], psC[0:w, 0:TOK], ACT.Copy).then_inc(s["comb_out"], 1)

                def down_copy(s, p, w):
                    act.wait_ge(s["down_full"], p + 1)
                    for hh in range(2):
                        last = act.activation(ys[0:w, HALF * hh:HALF * (hh + 1)], psD[hh][0:w, :], ACT.Copy)
                    last.then_inc(s["down_out"], 1)

                def pair(p, b):
                    for u in range(2):
                        up_copy(pairs[l], p * 2 + u, u)
                        silu(pairs[l], p * 2 + u)
                    comb_copy(pairs[l], p, b, 2 * BLK)
                    down_copy(pairs[l], p, 2 * BLK)

                with act.Fori(0, NPAIR // 2) as i:
                    for b in range(2):
                        pair(i * 2 + b, b)
                act.wait_ge(plan_ready, l + 1)
                blocks = act.value_load(plan_i[0:1, NOV:NOV + 1], min_val=0, max_val=NOV)
                with act.Fori(0, NOV) as j:
                    with act.If(j < blocks):
                        up_copy(overs[l], j, 0)
                        silu(overs[l], j)
                        comb_copy(overs[l], j, 0, BLK)
                        down_copy(overs[l], j, BLK)

            for l in range(L):
                if l == 1:
                    act.wait_ge(x_ready, 2)
                    sum_squares(2)
                    norm(2)
                    gate(2)
                    for f in range(KT):
                        if turn[("uT", f)][2] == "act":
                            b = stage_bank(("uT", f), act)
                            emptied_inc(act.activation(uT[:, f, :], b[:, 0:TOK], ACT.Copy))
                    for i in range(NT):
                        for g in range(FG):
                            if turn[("v", i, g)][2] == "act":
                                b = stage_bank(("v", i, g), act)
                                emptied_inc(act.activation(v[:, i, g, :], b[:, :], ACT.Copy))
                    for f in range(KT):
                        if turn[("fT", f)][2] == "act":
                            b = stage_bank(("fT", f), act)
                            emptied_inc(act.activation(T[:, f, :], b[:, 0:TOK], ACT.Copy))
                act.wait_ge(x_ready, 2 * l + 1)
                sum_squares(2 * l + 1)
                norm(2 * l + 1)
                act.wait_ge(g_shifted, 2 * l + 1)
                act.activation(eg, eg, ACT.Exp).then_inc(g_exp, 1)
                act.wait_ge(g_shifted, 2 * l + 2)
                act.activation(ee, ee, ACT.Exp).then_inc(g_exp, 1)
                routing_act(l)
                gate(2 * l + 1)
                if l == 0:
                    act.wait_ge(special_free, 1)
                    act.dma_start(special[:, 0:N_FOUR], four_const).then_inc(special_in, 16)
                moe(l)

        @block.vector
        def _(dve):
            def settle():
                dve.drain()

            def emptied_inc(ins):
                ins.then_inc(dve_emptied, 1)

            def bc(ap, *shape):
                return ap.to_broadcast([P, *shape])

            def norm(s):
                l, f = s // 2, s % 2
                dve.wait_ge(rms_ready, s + 1)
                dve.reciprocal(stat[:, 0, :], stat[:, 1, :])
                settle()
                for t in range(NT):
                    last = dve.tensor_scalar(h[:, t, :], x[:, t, :], stat[:, 0, t:t + 1], None, ALU.mult)
                last.then_inc(normed, 1)

            def affine(s):
                for j in range(KT):
                    if turn[("norm", s, j)][2] == "dve":
                        b = stage_bank(("norm", s, j), dve)
                        l, f = s // 2, s % 2
                        for k, (a, e) in enumerate(((0, SEQ), (SEQ, TOK))):
                            last = dve.tensor_scalar(T[:, j, a:e], b[:, a:e], mcol[:, l, 3 * f + 1, j, k:k + 1],
                                                     mcol[:, l, 3 * f, j, k:k + 1], ALU.mult, ALU.add)
                        emptied_inc(last)

            def ada_cols(l, cc):
                b = stage_bank(("adaT", l, cc), dve)
                src = b[:, :].rearrange("p (s q r) -> p s r q", s=4, q=4)[:, :, 0:2, :]
                k0 = 4 * (cc % 2)
                emptied_inc(dve.tensor_reduce(mcol[:, l, cc // 2, k0:k0 + 4, :], src, AX.X, ALU.add))

            def ada(l, c0, c1):
                for cc in range(c0, c1):
                    if cc > 0:
                        ada_cols(l, cc - 1)
                if c1 == ADA_C:
                    ada_cols(l, c1 - 1)
                    settle()
                    bias = bcol[:, l * 6 * KT:(l + 1) * 6 * KT]
                    m = mcol[:, l].rearrange("p v k c -> p (v k) c")
                    dve.tensor_tensor(m, m, bias.unsqueeze(2).to_broadcast([P, 6 * KT, 2]), ALU.add)
                    settle()
                    for f, r in ((0, R_MIX), (1, R_FFN)):
                        gain = colv[:, r + l * KT:r + (l + 1) * KT].unsqueeze(2).to_broadcast([P, KT, 2])
                        sc = mcol[:, l, 3 * f + 1]
                        last = dve.scalar_tensor_tensor(sc, sc, 1.0, gain, ALU.add, ALU.mult)
                    last.then_inc(affine_ready, 2)
                    settle()

            def diagonals(s):
                l, f = s // 2, s % 2
                for n in range(4):
                    k, hh = n // 2, n % 2
                    if n >= 2:
                        dve.wait_ge(full, turn[("gate", s, (n - 2) // 2, (n - 2) % 2)][1])
                    for q in range(4):
                        last = dve.tensor_scalar(diag[:, n % 2, q * P:(q + 1) * P], ident,
                                                 mcol[:, l, 3 * f + 2, 4 * hh + q, k:k + 1], None, ALU.mult)
                    last.then_inc(diag_ready, 1)

            def gated_add(l):
                dve.wait_ge(act_emptied, turn[("gate", 2 * l, 1, 1)][3])
                for hh in range(2):
                    for i in range(NT):
                        b = stage_bank(("out", l, hh, i), dve)
                        cs = slice(HALF * hh, HALF * (hh + 1))
                        n = NT * hh + i
                        gated = scratch[:, HALF * (n % 2):HALF * (n % 2 + 1)]
                        emptied_inc(dve.tensor_tensor(gated, b[:, :], gate_b[:, min(i, 1), cs], ALU.mult))
                        settle()
                        last = dve.tensor_tensor(x[:, i, cs], x[:, i, cs], gated, ALU.add)
                last.then_inc(x_ready, 1)

            def add_reduce(out, in_):
                return dve.tensor_reduce(out, in_, AX.X, ALU.add)

            def first_largest(one, val, top):
                dve.tensor_tensor(sc4, val, bc(top.unsqueeze(2), NT, 4), ALU.is_equal)
                settle()
                dve.tensor_tensor(sc4, sc4, bc(con("desc").unsqueeze(1), NT, 4), ALU.mult)
                settle()
                dve.tensor_reduce(sg, sc4, AX.X, ALU.max)
                settle()
                dve.tensor_tensor(one, sc4, bc(sg.unsqueeze(2), NT, 4), ALU.is_equal)
                settle()

            def route(l):
                b = stage_bank(("router", l), dve)
                lo = b[:, 0:NT * (NG + NE)].rearrange("p (t n) -> p t n", t=NT)
                emptied_inc(dve.tensor_tensor(lg, lo, bc(router_b[:, l, :].unsqueeze(1), NT, NG + NE), ALU.add))
                settle()
                dve.tensor_reduce(mg, lg[:, :, 0:NG], AX.X, ALU.max)
                settle()
                dve.tensor_tensor(eg, lg[:, :, 0:NG], bc(mg.unsqueeze(2), NT, NG), ALU.subtract).then_inc(g_shifted, 1)
                first_largest(og, lg[:, :, 0:NG], mg)
                dve.tensor_tensor(prod, lg[:, :, NG:].rearrange("p t (g e) -> p t e g", g=NG),
                                  bc(og.unsqueeze(2), NT, EPG, NG), ALU.mult)
                settle()
                add_reduce(le, prod)
                settle()
                dve.tensor_reduce(ml, le, AX.X, ALU.max)
                settle()
                dve.tensor_tensor(ee, le, bc(ml.unsqueeze(2), NT, EPG), ALU.subtract).then_inc(g_shifted, 1)
                first_largest(o1, le, ml)
                dve.scalar_tensor_tensor(le2, o1, LOWEST, le, ALU.mult, ALU.add)
                settle()
                dve.tensor_reduce(ml, le2, AX.X, ALU.max)
                settle()
                first_largest(o2, le2, ml)
                for n, o in enumerate((o1, o2)):
                    dve.tensor_tensor(M12[:, n].rearrange("p t (g e) -> p t g e", g=NG),
                                      bc(og.unsqueeze(3), NT, NG, EPG), bc(o.unsqueeze(2), NT, NG, EPG), ALU.mult)
                settle()
                dve.tensor_tensor(Ms, M12[:, 0], M12[:, 1], ALU.add).then_inc(ms_ready, 1)
                dve.wait_ge(g_exp, 2 * l + 2)
                add_reduce(sg, eg)
                add_reduce(se, ee)
                settle()
                dve.reciprocal(pg, sg)
                dve.reciprocal(se, se)
                settle()
                dve.tensor_tensor(ee, ee, bc(se.unsqueeze(2), NT, EPG), ALU.mult)
                settle()
                dve.tensor_tensor(prod[:, :, 0, :], ee, o1, ALU.mult)
                dve.tensor_tensor(prod[:, :, 1, :], ee, o2, ALU.mult)
                settle()
                add_reduce(c12[:, 0, :], prod[:, :, 0, :])
                add_reduce(c12[:, 1, :], prod[:, :, 1, :])
                settle()
                dve.tensor_tensor(p1, c12[:, 0, :], c12[:, 1, :], ALU.add)
                settle()
                dve.reciprocal(p1, p1)
                settle()
                dve.tensor_tensor(p1, p1, pg, ALU.mult)
                settle()
                dve.tensor_tensor(c12, c12, bc(p1.unsqueeze(1), 2, NT), ALU.mult)
                diagonals(2 * l + 1)
                b = stage_bank(("rank", l), dve)
                rank = b[:, 0:NT * NE].rearrange("p (t e) -> p t e", t=NT)
                count = b[:, NT * NE:(NT + 1) * NE]
                dve.tensor_scalar(ge, rank, float(BLK), None, ALU.is_ge)
                dve.tensor_copy(G, rank)
                emptied_inc(dve.tensor_tensor(cmp5, bc(count.unsqueeze(2), NE, NTHR),
                                              bc(con("limit").unsqueeze(1), NE, NTHR), ALU.is_gt))
                settle()
                add_reduce(ovc, cmp5)
                settle()
                dve.tensor_tensor(tri_p, bc(ovc.unsqueeze(1), NE, NE),
                                  con("tri").rearrange("p (e f) -> p e f", e=NE), ALU.mult)
                settle()
                add_reduce(ovb, tri_p)
                add_reduce(eidf[:, NOV:NOV + 1], ovc)
                settle()
                dve.tensor_tensor(incl, ovb, ovc, ALU.add)
                dve.scalar_tensor_tensor(off, ovb, float(BLK), con("shift"), ALU.mult, ALU.add)
                settle()
                dve.tensor_tensor(cmp_j, bc(incl.unsqueeze(1), NOV, NE), bc(con("jrow").unsqueeze(2), NOV, NE), ALU.is_le)
                dve.tensor_tensor(ge, ge, bc(off.unsqueeze(1), NT, NE), ALU.mult)
                settle()
                add_reduce(eidf[:, 0:NOV], cmp_j)
                dve.tensor_tensor(G, G, ge, ALU.add)
                settle()
                dve.tensor_scalar(eidf[:, 0:NOV], eidf[:, 0:NOV], float(NE - 1), None, ALU.min)
                dve.tensor_tensor(G, G, bc(con("first").unsqueeze(1), NT, NE), ALU.add)
                settle()
                dve.tensor_copy(plan_i[:, :], eidf).then_inc(plan_ready, 1)
                dve.tensor_tensor(Gp, M12[:, 0], G, ALU.mult)
                dve.tensor_tensor(ge, M12[:, 1], G, ALU.mult)
                settle()
                add_reduce(G12[:, 0, :], Gp)
                add_reduce(G12[:, 1, :], ge)
                settle()

            g6 = G12.rearrange("p a t -> p (a t)")
            c6 = c12.rearrange("p a t -> p (a t)")
            S6 = S12.rearrange("p a t s -> p (a t) s")

            def select(s, b, w):
                dve.tensor_tensor(S6[:, :, 0:w], bc(con("iota")[:, 0:w].unsqueeze(1), 2 * NT, w),
                                  bc(g6.unsqueeze(2), 2 * NT, w), ALU.is_equal)
                settle()
                dve.tensor_tensor(Sel[:, :, 0:w], S12[:, 0, :, 0:w], S12[:, 1, :, 0:w], ALU.add)
                dve.tensor_scalar(g6, g6, -float(w), None, ALU.add)
                settle()
                dve.tensor_tensor(S6[:, :, 0:w], S6[:, :, 0:w], bc(c6.unsqueeze(2), 2 * NT, w), ALU.mult)
                settle()
                dve.tensor_tensor(CT[:, b, :, 0:w], S12[:, 0, :, 0:w], S12[:, 1, :, 0:w], ALU.add)\
                   .then_inc(s["sel_ready"], 1)
                settle()

            def moe(l):
                def gather_out(s, n, b, q, w):
                    dve.wait_ge(s["gathered"], n + 1)
                    dve.tensor_copy(xT[:, b, 4 * q:4 * q + 4, 0:w], psX[q][:, 0:4 * w].rearrange("p (k s) -> p k s", k=4))\
                       .then_inc(s["x_cols"], 1)

                def hidden(s, e, u):
                    dve.wait_ge(s["silu_out"], e + 1)
                    mid = psT[:, :].rearrange("p (k s) -> p k s", k=FC)
                    dve.tensor_tensor(aT[:, u], sil, mid[:, :, BLK:2 * BLK], ALU.mult).then_inc(s["act_cols"], 1)

                def add_back(s, p):
                    for n in range(2 * NT):
                        dve.wait_ge(s["back_full"], p * (2 * NT) + (n + 1))
                        a = acc[:, n // 2, HALF * (n % 2):HALF * (n % 2 + 1)]
                        dve.tensor_tensor(a, a, psK[n % 2][:, :], ALU.add).then_inc(s["back_out"], 1)

                def pair(s, p, b, first=False, last=False):
                    w = 2 * BLK
                    if not last:
                        if not first:
                            dve.wait_ge(s["comb_full"], p)
                        select(s, 1 - b, w)
                        gather_out(s, p * 2 + 2, 1 - b, 0, w)
                    hidden(s, p * 2, 0)
                    if not last:
                        gather_out(s, p * 2 + 3, 1 - b, 1, w)
                    hidden(s, p * 2 + 1, 1)
                    if not first:
                        add_back(s, p - 1)

                s, o = pairs[l], overs[l]
                select(s, 0, 2 * BLK)
                for q in range(2):
                    gather_out(s, q, 0, q, 2 * BLK)
                dve.wait_ge(zeroed, l + 2)
                pair(s, 0, 0, first=True)
                pair(s, 1, 1)
                with dve.Fori(1, NPAIR // 2 - 1) as i:
                    for b in range(2):
                        pair(s, i * 2 + b, b)
                pair(s, NPAIR - 2, 0)
                pair(s, NPAIR - 1, 1, last=True)
                add_back(s, NPAIR - 1)
                dve.wait_ge(plan_ready, l + 1)
                dve.sem_inc(o["done"], 1)
                blocks = dve.value_load(plan_i[0:1, NOV:NOV + 1], min_val=0, max_val=NOV)
                with dve.Fori(0, NOV) as j:
                    with dve.If(j < blocks):
                        select(o, 0, BLK)
                        for q in range(2):
                            gather_out(o, j * 2 + q, 0, q, BLK)
                        hidden(o, j, 0)
                        add_back(o, j)
                        dve.drain().then_inc(o["done"], 1)
                settle()
                dve.wait_ge(act_emptied, turn[("gate", 2 * l + 1, 1, 1)][3])
                for i in range(NT):
                    dve.tensor_tensor(acc[:, i, :], acc[:, i, :], gate_b[:, min(i, 1), :], ALU.mult)
                settle()
                for i in range(NT):
                    last = dve.tensor_tensor(x[:, i, :], x[:, i, :], acc[:, i, :], ALU.add)
                last.then_inc(x_ready, 1)

            b = stage_bank("rows", dve)
            dve.wait_ge(zeroed, 1)
            dve.tensor_copy(colv[:, :], b[:, 0:N_ROWS])
            dve.tensor_copy(bcol[:, :], b[:, P:P + N_BROWS])
            for k, r in enumerate((R_CCTX, R_C)):
                last = dve.tensor_copy(cond[:, :, k], b[:, 2 * P + r:2 * P + r + KT])
            emptied_inc(last)
            norm(0)
            ada(0, 0, ADA_C)
            affine(0)
            for cc in range(len(W_IN_COLS)):
                for i in range(NT):
                    if turn[("z", cc, i)][2] == "dve":
                        b = stage_bank(("z", cc, i), dve)
                        w, a = W_IN_COLS[cc], sum(W_IN_COLS[:cc])
                        emptied_inc(dve.tensor_copy(z[:, i, a:a + w], b[:, 0:w]))
            dve.wait_ge(params_in, loads[params_in])
            dve.wait_ge(qk_squares, 1)
            dve.tensor_reduce(ssq, sq[:, :, :].rearrange("p t (h d) -> p (t h) d", d=HD), AX.X, ALU.add)\
               .then_inc(qk_sums, 1)
            dve.wait_ge(qk_rms_ready, 1)
            dve.reciprocal(rsq, rsq)
            settle()
            zq = z[:, :, 0:QKW].rearrange("p t (h d) -> p t h d", d=HD)
            rq = rsq.rearrange("p (t h) -> p t h", t=NT).unsqueeze(3)
            dve.tensor_tensor(zq, zq, bc(rq, NT, NQK, HD), ALU.mult)
            settle()
            for i in range(NT):
                dve.tensor_tensor(qk[:, i, 0:AW].rearrange("p (c k d) -> p k c d", k=NKV, d=HD),
                                  z[:, i, 0:AW].rearrange("p (k c d) -> p k c d", k=NKV, d=HD),
                                  bc(qk_gain[:, 0, :].unsqueeze(1).unsqueeze(1), NKV, NH // NKV, HD), ALU.mult)
            kz = zq[:, :, NH:NQK]
            dve.tensor_tensor(qk[:, :, AW:QKW].rearrange("p t (h d) -> p t h d", d=HD), kz,
                              bc(qk_gain[:, 1, :].unsqueeze(1).unsqueeze(1), NT, NKV, HD), ALU.mult)\
               .then_inc(kv_out_ready, 1)
            settle()
            dve.wait_ge(special_in, 16)
            for i in (1, 2):
                zi = qk[:, i, :].rearrange("p (h d) -> p h d", d=HD)
                cosr = att("cos")[:, (i - 1) * HD:i * HD].unsqueeze(1)
                r0 = rot0.rearrange("p (h d) -> p h d", d=HD)
                dve.tensor_tensor(r0, zi, bc(cosr, NQK, HD), ALU.mult)
                z5 = qk[:, i, :].rearrange("p (h a b f) -> p h a b f", a=2, b=2, f=HD // 4)
                r5 = rot1.rearrange("p (h a b f) -> p h a b f", a=2, b=2, f=HD // 4)
                s5 = att("sin")[:, (i - 1) * HD:i * HD].rearrange("p (a b f) -> p a b f", a=2, b=2)
                for b2 in range(2):
                    sn = s5[:, :, b2, :].unsqueeze(1)
                    dve.tensor_tensor(r5[:, :, :, b2, :], z5[:, :, :, 1 - b2, :], bc(sn, NQK, 2, HD // 4), ALU.mult)
                settle()
                last = dve.tensor_tensor(zi, r0, rot1.rearrange("p (h d) -> p h d", d=HD), ALU.add)
                settle()
            last.then_inc(qk_ready, 1)
            ada(1, 0, 6)

            mx, nmx, den, es = small[:, 0:8], small[:, 8:16], small[:, 16:24], small[:, 24:32]

            def scores(i):
                w = SEQ if i == 0 else TOK
                for cc in range(NH // 2):
                    for hd in (cc, cc + NH // 2):
                        b = stage_bank(("score", i, hd), dve)
                        if i == 0:
                            emptied_inc(dve.tensor_scalar(PC[:, hd, :], b[:, 0:w], HD ** -0.5, None, ALU.mult))
                        else:
                            m = att("mask")[:, (i - 1) * TOK:i * TOK]
                            emptied_inc(dve.scalar_tensor_tensor(PL[:, hd, :], b[:, 0:w], HD ** -0.5, m, ALU.mult, ALU.add))
                settle()
                pr = PC if i == 0 else PL
                dve.tensor_reduce(mx, pr[:, :, 0:w], AX.X, ALU.max)
                settle()
                dve.tensor_tensor(mx, mx, sink[:, :], ALU.max)
                settle()
                dve.tensor_scalar(nmx, mx, -1.0, None, ALU.mult)
                dve.tensor_tensor(es, sink[:, :], mx, ALU.subtract).then_inc(p_max, 1)

            def normalize(i):
                w = SEQ if i == 0 else TOK
                dve.wait_ge(p_exp, i + 1)
                dve.tensor_tensor(den, den, es, ALU.add)
                settle()
                dve.reciprocal(den, den)
                settle()
                pr = PC if i == 0 else PL
                for hd in range(NH):
                    last = dve.tensor_scalar(pr[:, hd, 0:w], pr[:, hd, 0:w], den[:, hd:hd + 1], None, ALU.mult)
                last.then_inc(p_ready, 1)

            def attended(i):
                b = stage_bank(("oT", i), dve)
                emptied_inc(dve.tensor_copy(T[:, 0:4, i * P:(i + 1) * P], b[:, :].rearrange("p (c n) -> p c n", c=4)))

            scores(0)
            normalize(0)
            dve.wait_ge(kv_out_done, 32)
            scores(1)
            normalize(1)
            ada(1, 6, 9)
            attended(0)
            attended(1)
            scores(2)
            ada(1, 9, ADA_C)
            diagonals(0)
            normalize(2)
            attended(2)
            gated_add(0)
            dve.drain().then_inc(special_free, 1)
            norm(1)
            affine(1)
            route(0)
            moe(0)
            norm(2)
            affine(2)
            diagonals(2)
            for f in range(KT):
                if turn[("uT", f)][2] == "dve":
                    b = stage_bank(("uT", f), dve)
                    emptied_inc(dve.tensor_copy(uT[:, f, :], b[:, 0:TOK]))
            for i in range(NT):
                for g in range(FG):
                    if turn[("v", i, g)][2] == "dve":
                        b = stage_bank(("v", i, g), dve)
                        emptied_inc(dve.tensor_copy(v[:, i, g, :], b[:, :]))
            for f in range(KT):
                if turn[("fT", f)][2] == "dve":
                    b = stage_bank(("fT", f), dve)
                    emptied_inc(dve.tensor_copy(T[:, f, :], b[:, 0:TOK]))
            gated_add(1)
            norm(3)
            affine(3)
            route(1)
            moe(1)

        @block.tensor
        def _(pe):
            def begin(key):
                bank, n, who, k, before = turn[key]
                if before is not None:
                    pe.wait_ge(emptied[before[0]], before[1])
                return banks[bank]

            def done_by(*keys):
                for key in keys:
                    pe.wait_ge(emptied[turn[key][2]], turn[key][3])

            def item(n, w=HALF):
                pe.wait_ge(arrived[n % NS], 16 * (n // NS + 1))
                return ring[:, n % NS, 0:KT * w].rearrange("p (k n) -> p k n", k=KT)

            def ada(l, n0, c0, c1):
                def columns(cc):
                    done_by(("ada", l, cc))
                    b = begin(("adaT", l, cc))
                    for q in range(4):
                        last = pe.transpose(b[:, q * P:(q + 1) * P], ada_row[:, cc % 2, q * P:(q + 1) * P], ident)
                    last.then_inc(full, 1)

                for cc in range(c0, c1):
                    w = item(n0 + cc)
                    b = begin(("ada", l, cc))
                    for k in range(KT):
                        q = k % 4
                        last = pe.matmul(b[32 * q:32 * q + 32, :], cond[:, k, :], w[:, k, :],
                                         start=(k < 4), stop=(k >= 4), skip_group_check=True)
                    last.then_inc(full, 1)
                    if cc > 0:
                        columns(cc - 1)
                if c1 == ADA_C:
                    columns(c1 - 1)

            def norm(s):
                pe.wait_ge(normed, s + 1)
                for j in range(KT):
                    b = begin(("norm", s, j))
                    for t in range(NT):
                        last = pe.transpose(b[:, t * P:(t + 1) * P], h[:, t, j * P:(j + 1) * P], ident)
                    last.then_inc(full, 1)

            def normed_cols(s):
                done_by(("norm", s, KT - 1), ("norm", s, KT - 2))

            def gate(s):
                for k in range(2):
                    for hh in range(2):
                        n = 2 * k + hh
                        b = begin(("gate", s, k, hh))
                        pe.wait_ge(diag_ready, 4 * s + n + 1)
                        pe.matmul(b[:, :], con("ones"), diag[:, n % 2, :], start=True, stop=True).then_inc(full, 1)

            def project(l, n0):
                for hh in range(2):
                    w = item(n0 + hh)
                    for i in range(NT):
                        b = begin(("out", l, hh, i))
                        for k in range(KT):
                            last = pe.matmul(b[:, :], T[:, k, i * P:(i + 1) * P], w[:, k, :], start=(k == 0), stop=(k == KT - 1))
                        last.then_inc(full, 1)

            def route(l):
                normed_cols(2 * l + 1)
                pe.wait_ge(params_in, loads[params_in])
                b = begin(("router", l))
                for t in range(NT):
                    for k in range(KT):
                        last = pe.matmul(b[:, t * (NG + NE):(t + 1) * (NG + NE)], T[:, k, t * P:(t + 1) * P],
                                         router_w[:, l, k, :], start=(k == 0), stop=(k == KT - 1))
                last.then_inc(full, 1)
                for t in range(NT):
                    for hh in range(2):
                        b = begin(("tokens", l, t, hh))
                        for q in range(4):
                            last = pe.transpose(b[:, q * P:(q + 1) * P], T[:, 4 * hh + q, t * P:(t + 1) * P], ident)
                        last.then_inc(full, 1)
                b = begin(("rank", l))
                pe.wait_ge(ms_ready, l + 1)
                for t in range(NT + 1):
                    out = b[:, t * NE:(t + 1) * NE]
                    for q in range(min(t + 1, NT)):
                        own = q == t
                        last = pe.matmul(out, con("before") if own else con("ones"), Ms[:, q, :],
                                         start=(q == 0), stop=(q == min(t, NT - 1)))
                last.then_inc(full, 1)
                gate(2 * l + 1)

            def moe(l):
                s, o = pairs[l], overs[l]
                n0 = n_exp[l]
                pe.wait_ge(act_emptied, marks[l]["act"])
                pe.wait_ge(dve_emptied, marks[l]["dve"])

                def gather(q, w, s):
                    for k in range(4):
                        for t in range(NT):
                            kk = 4 * q + k
                            last = pe.matmul(psX[q][:, k * w:(k + 1) * w], h[:, t, kk * P:(kk + 1) * P], Sel[:, t, 0:w],
                                             start=(t == 0), stop=(t == NT - 1))
                    last.then_inc(s["gathered"], 1)

                def up(s, b, s0, w1, w3):
                    for k in range(KT):
                        for q, w in enumerate((w1, w3)):
                            last = pe.matmul(psU[BLK * q:BLK * (q + 1), :], xT[:, b, k, s0:s0 + BLK], w[:, k, :],
                                             start=(k == 0), stop=(k == KT - 1), skip_group_check=True)
                    last.then_inc(s["up_full"], 1)

                def middle(s, u):
                    for k in range(FC):
                        last = pe.transpose(psT[:, k * P:(k + 1) * P], up_s[:, u, k * P:(k + 1) * P], ident)
                    last.then_inc(s["mid_full"], 1)

                def combine_rows(s, b, w):
                    for t in range(NT):
                        last = pe.transpose(psC[0:w, t * P:(t + 1) * P], CT[:, b, t, 0:w], ident)
                    last.then_inc(s["comb_full"], 1)

                def down(k, hh, ws):
                    for u, w2 in enumerate(ws):
                        last = pe.matmul(psD[hh][BLK * u:BLK * (u + 1), :], aT[:, u, k, :], w2[:, k, HALF * hh:HALF * (hh + 1)],
                                         start=(k == 0), stop=(k == FC - 1), skip_group_check=True)
                    return last

                def back(s, n, b, w):
                    t, hh = n // 2, n % 2
                    pe.matmul(psK[n % 2][:, :], Cs[0:w, b, t * P:(t + 1) * P], ys[0:w, HALF * hh:HALF * (hh + 1)],
                              start=True, stop=True).then_inc(s["back_full"], 1)

                def slot(k, kk):
                    return ring[:, (n0 + k) % NS, :].rearrange("p (k n) -> p k n", k=kk)

                def pair(i, p, b, first=False, last=False):
                    def weights(*ks):
                        for k in ks:
                            n = n0 + k
                            pe.wait_ge(arrived[n % NS], i * 16 + 16 * (n // NS + 1))

                    for u in range(2):
                        if u == 0:
                            pe.wait_ge(s["x_cols"], p * 2 + 2)
                            if not first:
                                pe.wait_ge(s["comb_out"], p)
                        else:
                            pe.wait_ge(s["up_out"], p * 2 + 1)
                        weights(2 * u, 2 * u + 1)
                        up(s, b, BLK * u, slot(2 * u, KT), slot(2 * u + 1, KT))
                        if not last:
                            if u == 0:
                                pe.wait_ge(s["sel_ready"], p + 2)
                                pe.wait_ge(s["x_cols"], p * 2 + 2)
                            gather(u, 2 * BLK, s)
                        pe.wait_ge(s["up_out"], p * 2 + (u + 1))
                        if u == 1 or not first:
                            pe.wait_ge(s["act_cols"], p * 2 + u)
                        middle(s, u)
                    combine_rows(s, b, 2 * BLK)
                    order = []
                    for n in range(2 * FC):
                        if n < 2 * NT and not first:
                            order.append(("back", n))
                        if n > 0:
                            order.append(("down", n - 1))
                    order.append(("down", 2 * FC - 1))
                    for n, (what, m) in enumerate(order):
                        if (what, m) == ("back", 0):
                            pe.wait_ge(s["down_out"], p)
                            pe.wait_ge(s["comb_out"], p)
                        if (what, m) == ("down", 0):
                            pe.wait_ge(s["act_cols"], p * 2 + 2)
                            if not first:
                                pe.wait_ge(s["down_out"], p)
                            weights(4, 5)
                        if what == "back":
                            if isinstance(p, int) and p == 1:
                                if m >= 2:
                                    pe.wait_ge(s["back_out"], m - 1)
                            else:
                                pe.wait_ge(s["back_out"], p * (2 * NT) + (m - 1 - 2 * NT))
                            back(s, m, 1 - b, 2 * BLK)
                        else:
                            done = down(m // 2, m % 2, (slot(4, FC), slot(5, FC)))
                    done.then_inc(s["down_full"], 1)

                pe.wait_ge(s["sel_ready"], 1)
                gather(0, 2 * BLK, s)
                gather(1, 2 * BLK, s)
                pair(0, 0, 0, first=True)
                pair(1, 1, 1)
                with pe.Fori(1, NPAIR // 2 - 1) as i:
                    for b in range(2):
                        pair(i * 2 + b, i * 2 + b, b)
                pair(NPAIR - 2, NPAIR - 2, 0)
                pair(NPAIR - 1, NPAIR - 1, 1, last=True)
                pe.wait_ge(s["comb_out"], NPAIR)
                pe.wait_ge(s["down_out"], NPAIR)
                for n in range(2 * NT):
                    pe.wait_ge(s["back_out"], (NPAIR - 1) * 2 * NT + n - 1)
                    back(s, n, 1, 2 * BLK)
                pe.wait_ge(plan_ready, l + 1)
                blocks = pe.value_load(plan_i[0:1, NOV:NOV + 1], min_val=0, max_val=NOV)
                with pe.Fori(0, NOV) as j:
                    with pe.If(j < blocks):
                        pe.wait_ge(o["sel_ready"], j + 1)
                        gather(0, BLK, o)
                        gather(1, BLK, o)
                        pe.wait_ge(o["x_cols"], j * 2 + 2)
                        pe.wait_ge(o["weights"], j * 48 + 48)
                        ow = [ring[:, m, :].rearrange("p (k n) -> p k n", k=KT if m < 2 else FC) for m in range(3)]
                        up(o, 0, 0, ow[0], ow[1])
                        pe.wait_ge(o["up_out"], j + 1)
                        middle(o, 0)
                        combine_rows(o, 0, BLK)
                        pe.wait_ge(o["act_cols"], j + 1)
                        for n in range(2 * FC):
                            done = down(n // 2, n % 2, ow[2:])
                        done.then_inc(o["down_full"], 1)
                        pe.wait_ge(o["comb_out"], j + 1)
                        pe.wait_ge(o["down_out"], j + 1)
                        for n in range(2 * NT):
                            if n >= 2:
                                pe.wait_ge(o["back_out"], j * (2 * NT) + (n - 1))
                            back(o, n, 0, BLK)

            pe.wait_ge(small_in, loads[small_in])
            pe.wait_ge(cond_rows, 1)
            b = begin("rows")
            pe.transpose(b[:, 0:N_ROWS], rows[:, :], ident[0:N_ROWS, 0:N_ROWS])
            pe.transpose(b[:, P:P + N_BROWS], brows[:, :], ident[0:N_BROWS, 0:N_BROWS])
            pe.transpose(b[:, 2 * P:2 * P + N_ROWS], rows_silu[:, :], ident[0:N_ROWS, 0:N_ROWS]).then_inc(full, 1)
            done_by("rows")
            ada(0, N_ADA0, 0, ADA_C)
            norm(0)
            normed_cols(0)
            for cc in range(len(W_IN_COLS)):
                wd = W_IN_COLS[cc]
                w = item(N_WIN + cc, wd)
                for i in range(NT):
                    b = begin(("z", cc, i))
                    for k in range(KT):
                        last = pe.matmul(b[:, 0:wd], T[:, k, i * P:(i + 1) * P], w[:, k, :], start=(k == 0), stop=(k == KT - 1))
                    last.then_inc(full, 1)
            done_by(("z", 2, 2), ("z", 2, 1))
            pe.wait_ge(special_in, 16)
            pe.wait_ge(params_in, loads[params_in])
            U0 = AW + 2 * KVW

            def pooled_map(g):
                done_by(("pool", g))
                b = begin(("pooled", g))
                pe.matmul(b[:, 0:TOK], pool_ws[:, g, :], pooled[:, g % 2, :], start=True, stop=True).then_inc(full, 1)

            for g in range(NPG):
                b = begin(("pool", g))
                cs = slice(U0 + g * P, U0 + (g + 1) * P)
                pe.matmul(b[:, 0:SEQ], z[:, 0, cs], att("band_ctx")[:, g * P:(g + 1) * P], start=True, stop=True)
                bl = att("band_lat").rearrange("p (g s t) -> p g s t", g=NPG, s=2)
                for q in range(2):
                    last = pe.matmul(b[:, SEQ:TOK], z[:, 1 + q, cs], bl[:, g, q, :], start=(q == 0), stop=(q == 1))
                last.then_inc(full, 1)
                if g > 0:
                    pooled_map(g - 1)
            pooled_map(NPG - 1)
            ada(1, N_ADA1, 0, 6)
            pe.wait_ge(qk_ready, 1)
            for cc in range(NH // 2):
                b = begin(("qT", cc))
                for i in range(NT):
                    last = pe.transpose(b[:, i * P:(i + 1) * P], qk[:, i, cc * P:(cc + 1) * P], ident)
                last.then_inc(full, 1)
            b = begin("kT")
            for i in range(NT):
                pe.transpose(b[:, i * P:(i + 1) * P], qk[:, i, AW:QKW], ident)
            pe.transpose(b[:, TOK:TOK + PAST], ckT_in[:, :], ident).then_inc(full, 1)
            done_by("kT")

            def scores(i):
                for cc in range(NH // 2):
                    for kv in range(2):
                        b = begin(("score", i, cc + 4 * kv))
                        rows_ = slice(HD * kv, HD * (kv + 1))
                        q = qT[rows_, cc, i * P:(i + 1) * P]
                        if i == 0:
                            last = pe.matmul(b[:, 0:SEQ], q, kT[rows_, 0:SEQ], start=True, stop=True)
                        else:
                            last = pe.matmul(b[:, 0:TOK], q, kT[rows_, SEQ:TOK + PAST], start=True, stop=True)
                        last.then_inc(full, 1)

            def values(i):
                pe.wait_ge(p_ready, i + 1)
                keys = [0] if i == 0 else [1, 2, NT]

                def turn_head(hd):
                    b = begin(("PT", i, hd))
                    for n in range(len(keys)):
                        pr = PC[:, hd, :] if i == 0 else PL[:, hd, n * P:(n + 1) * P]
                        last = pe.transpose(b[:, n * P:(n + 1) * P], pr, ident)
                    last.then_inc(full, 1)

                if turn[("oT", i)][4] is not None:
                    pe.wait_ge(emptied[turn[("oT", i)][4][0]], turn[("oT", i)][4][1])
                ob = banks[7]

                def product(hd):
                    done_by(("PT", i, hd))
                    kv, r0 = hd // 4, HD * (hd % 2)
                    out = ob[r0:r0 + HD, (hd // 2) * P:(hd // 2 + 1) * P]
                    for n, kt in enumerate(keys):
                        vals = cv[:, HD * kv:HD * (kv + 1)] if kt == NT else \
                            z[:, kt, AW + KVW + HD * kv:AW + KVW + HD * (kv + 1)]
                        last = pe.matmul(out, vals, PT[:, hd % 2, n * P:(n + 1) * P],
                                         start=(n == 0), stop=(n == len(keys) - 1), skip_group_check=True)
                    last.then_inc(pv_done, 1)

                for hd in range(NH):
                    turn_head(hd)
                    if hd > 0:
                        product(hd - 1)
                product(NH - 1)
                pe.drain().then_inc(full, 1)

            scores(0)
            scores(1)
            ada(1, N_ADA1, 6, 9)
            values(0)
            values(1)
            scores(2)
            ada(1, N_ADA1, 9, ADA_C)
            gate(0)
            values(2)
            done_by(("oT", 2), ("pooled", NPG - 1))
            project(0, N_WOUT)
            norm(1)
            route(0)
            moe(0)
            pe.wait_ge(x_ready, 2)
            norm(2)
            gate(2)
            normed_cols(2)
            for cc in range(2):
                w = item(N_FIN + cc)
                for q in range(4):
                    b = begin(("uT", 4 * cc + q))
                    for k in range(KT):
                        last = pe.matmul(b[:, 0:TOK], w[:, k, q * P:(q + 1) * P], T[:, k, :], start=(k == 0), stop=(k == KT - 1))
                    last.then_inc(full, 1)
            pe.wait_ge(special_in, 32)
            done_by(("uT", KT - 1), ("uT", KT - 2))
            for i in range(NT):
                for g in range(FG):
                    b = begin(("v", i, g))
                    for q in range(2):
                        last = pe.matmul(b[:, :], uT[:, 2 * g + q, i * P:(i + 1) * P],
                                         four("feat")[:, q * 2 * FD:(q + 1) * 2 * FD], start=(q == 0), stop=(q == 1))
                    last.then_inc(full, 1)
            done_by(("v", NT - 1, FG - 1), ("v", NT - 1, FG - 2))
            for f in range(KT):
                g, q0 = f // 2, (f % 2) * P
                b = begin(("fT", f))
                for part in range(2):
                    pe.matmul(b[:, 0:SEQ], v[:, 0, g, part * FD + q0:part * FD + q0 + P],
                              four("time_ctx")[:, part * SEQ:(part + 1) * SEQ], start=(part == 0), stop=(part == 1))
                tl = four("time_lat").rearrange("p (s c t) -> p s c t", s=2, c=2)
                for n in range(4):
                    q, part = n // 2, n % 2
                    last = pe.matmul(b[:, SEQ:TOK], v[:, 1 + q, g, part * FD + q0:part * FD + q0 + P],
                                     tl[:, q, part, :], start=(n == 0), stop=(n == 3))
                last.then_inc(full, 1)
            done_by(("fT", KT - 1), ("fT", KT - 2))
            project(1, N_FOUT)
            norm(3)
            route(1)
            moe(1)


NAMES = ["x_prompt", "x_sample", "cache_k", "cache_v", "c", "c_ctx", "ada_w", "ada_b", "norm_mix",
         "norm_ffn", "a_w_in", "a_q_norm", "a_k_norm", "a_sink", "pool_w", "pool_scale", "a_w_out",
         "f_w_in", "f_w_out", "router_g_w", "router_g_b", "router_e_w", "router_e_b", "moe_w1",
         "moe_w3", "moe_w2"]


def kernel(**inputs):
    import concourse.bacc as bacc
    from concourse.bass_utils import run_bass_kernel_spmd

    nc = bacc.Bacc("TRN2", target_bir_lowering=False, num_devices=1)
    arrays, args = {}, []
    for name in NAMES:
        arrays[name] = np.ascontiguousarray(inputs[name])
    for name, columns in (("const", constant_columns()), ("att_const", attention_columns()),
                          ("four_const", fourier_columns())):
        arrays[name] = np.concatenate([np.asarray(v, np.float32) for v in columns.values()], 1)
    for name, a in arrays.items():
        args.append(nc.dram_tensor(f"in_{name}", a.shape, F32, kind="ExternalInput").ap())
    outs = {"y_prompt": (1, SEQ, D), "y_sample": (1, DEC, D),
            "new_cache_k": (1, 1, SEQ, NKV, HD), "new_cache_v": (1, 1, SEQ, NKV, HD)}
    for name, shape in outs.items():
        args.append(nc.dram_tensor(name, shape, F32, kind="ExternalOutput").ap())
    build(nc, *args)
    got = run_bass_kernel_spmd(nc, [{f"in_{k}": a for k, a in arrays.items()}], core_ids=[0]).results[0]
    return tuple(got[name] for name in outs)
```

```python
from contextlib import ExitStack

import concourse.bass as bass
from concourse import mybir
import numpy as np

F32 = mybir.dt.float32
BF16 = mybir.dt.bfloat16
I32 = mybir.dt.int32
ALU = mybir.AluOpType
ACT = mybir.ActivationFunctionType
AX = mybir.AxisListType

P = 128
D = 1024
KT = D // P
L = 2
SEQ = 128
DEC = 256
TOK = SEQ + DEC
NT = TOK // P
PAST = 128
HD = 64
NH = 8
NKV = 2
AW = NH * HD
KVW = NKV * HD
PW = 512
NPG = 4
ZW = AW + 2 * KVW + PW
QKW = AW + KVW
NQK = NH + NKV
NE = 16
NG = 4
EPG = 4
DE = 512
FC = DE // P
FG = 4
FD = D // FG
HALF = 512
BLK = 64
PAIRS = 2 * TOK
NPAIR = NE // 2
NOV = (PAIRS - NE) // BLK
NTHR = -(-TOK // BLK) - 1
EPS = 1e-6
GRID_W = 64
WINDOW = 128
LOWEST = -3.0e38

NS = 6
SLOT = KT * HALF
ADA_C = 6 * D // HALF
W_IN_COLS = [256, 512, 512]
ADA = [(0, n) for n in range(10)] + [(1, n) for n in (0, 1, 2, 3, 6, 7, 8, 9)] + [(0, 10), (0, 11)] + \
      [(1, n) for n in (4, 5, 10, 11)]
GATE_CHUNKS = (4, 5, 10, 11)
MIX_GATE = [ADA.index((l, 4)) for l in range(L)]
LAST_GATE = [ADA.index((l, 10)) for l in range(L)]


def constant_columns():
    out = {}
    p = np.arange(P)
    out["ident"] = np.eye(P)
    out["before"] = (p[:, None] < p[None, :]).astype(float)
    out["ones"] = np.ones((P, P))
    for n in range(2):
        out[f"spread{n}"] = np.tile((p[:, None] % 32 == n).astype(float), (1, P))
    rows = {
        "iota": np.arange(2 * BLK),
        "eps": [EPS],
        "desc": np.arange(NG, 0, -1),
        "limit": BLK * np.arange(1, NTHR + 1),
        "tri": (np.arange(NE)[None, :] < np.arange(NE)[:, None]).astype(float).ravel(),
        "jrow": np.arange(NOV),
        "first": BLK * np.arange(NE),
        "shift": BLK * NE - BLK - BLK * np.arange(NE),
    }
    for k, v in rows.items():
        out[k] = np.broadcast_to(np.asarray(v, float), (P, len(v)))
    return out


def attention_columns():
    out = {}
    tok = np.arange(DEC)
    half, nf = HD // 2, HD // 4
    freqs = (np.float32(10000.0) ** (-np.arange(nf, dtype=np.float32) / np.float32(nf))).astype(np.float32)
    cos, sin = np.zeros((DEC, HD)), np.zeros((DEC, HD))
    for n, pos in enumerate((tok // GRID_W, tok % GRID_W)):
        ang = (pos.astype(np.float32)[:, None] * freqs[None, :]).astype(np.float32)
        c, s = np.cos(ang), np.sin(ang)
        cos[:, half * n:half * (n + 1)] = np.concatenate([c, c], 1)
        sin[:, half * n:half * (n + 1)] = np.concatenate([-s, s], 1)
    out["cos"] = cos.reshape(2, P, HD).transpose(1, 0, 2).reshape(P, -1)
    out["sin"] = sin.reshape(2, P, HD).transpose(1, 0, 2).reshape(P, -1)
    q, k = tok[:, None], tok[None, :]
    mask = np.where(np.abs(q - k) <= WINDOW, 0.0, -1e30)
    mask = np.concatenate([mask, np.zeros((DEC, PAST))], 1)
    out["mask"] = mask.reshape(2, P, DEC + PAST).transpose(1, 0, 2).reshape(P, -1)

    def band(T, w):
        t = np.arange(T)
        lo, hi = np.clip(t - w // 2, 0, T), np.clip(t + w // 2, 0, T)
        s = np.arange(T)[:, None]
        m = ((s >= lo) & (s < hi)) / (hi - lo).astype(float) - np.eye(T)
        return m

    out["band_ctx"] = np.concatenate([band(SEQ, w) for w in (2, 4, 8, 16)], 1)
    lat = np.stack([band(DEC, w) for w in (2, 4, 8, 16)])
    out["band_lat"] = lat.reshape(NPG, 2, P, DEC).transpose(2, 0, 1, 3).reshape(P, -1)
    return out


FH = FD // 2
FEATURE_SLOTS = np.arange(FH)
FREQ_SLOTS = np.concatenate([np.arange(0, FH, 2), np.arange(1, FH, 2)])


def slot_order(slots):
    partners = np.where(slots == 0, FH, FD - slots)
    return np.concatenate([g * FD + np.concatenate([slots, partners]) for g in range(FG)])


def fourier_columns():
    out = {}
    n, k = FEATURE_SLOTS[:, None], FREQ_SLOTS[None, :]
    cos = np.cos(2 * np.pi * (n * k % FD) / FD) * FD ** -0.5
    sin = np.sin(2 * np.pi * (n * k % FD) / FD) * FD ** -0.5
    odd = (FREQ_SLOTS % 2 == 1)
    of_sums = cos.copy()
    of_sums[0, odd] = 0
    middle = np.cos(np.pi * FEATURE_SLOTS)[:, None] * FD ** -0.5
    of_differences = np.zeros((FH, FH // 2))
    of_differences[0, :] = FD ** -0.5
    out["sums"] = np.concatenate([middle, of_sums], 1)
    out["odd"] = of_differences
    out["sines"] = sin

    def dft(n, scale):
        a = 2 * np.pi * (np.outer(np.arange(n), np.arange(n)) % n) / n
        return np.cos(a) * scale, np.sin(a) * scale

    out["time_ctx"] = np.concatenate(dft(SEQ, SEQ ** -0.5), 1)
    t = np.concatenate(dft(DEC, DEC ** -0.5), 1)
    out["time_lat"] = t.reshape(2, P, 2 * DEC).transpose(1, 0, 2).reshape(P, -1)
    return out


def places(columns):
    at, out = 0, {}
    for k, v in columns.items():
        out[k] = (at, v.shape[1])
        at += v.shape[1]
    return out, at


CONST, N_CONST = places(constant_columns())
ATT, N_ATT = places(attention_columns())
FOUR, N_FOUR = places(fourier_columns())


class Turns:

    def __init__(self, banks):
        self.banks, self.at, self.filled = banks, 0, 0
        self.emptied = {"act": 0, "dve": 0}
        self.last = {}
        self.of = {}

    def fill(self, key, who, bank=None):
        if bank is None:
            bank = self.banks[self.at % len(self.banks)]
            self.at += 1
        self.filled += 1
        before = None
        if bank in self.last:
            _, _, who0, k0, _ = self.of[self.last[bank]]
            assert k0 is not None
            before = (who0, k0)
        self.of[key] = [bank, self.filled, who, None, before]
        self.last[bank] = key

    def empty(self, key):
        who = self.of[key][2]
        self.emptied[who] += 1
        self.of[key][3] = self.emptied[who]

    def add(self, key, who, bank=None):
        self.fill(key, who, bank)
        self.empty(key)

    def all_free(self):
        self.at = 0
        self.last = {}


def plan():
    t = Turns(list(range(7)))
    marks = {}

    def ada_product(n):
        t.add(("ada", n), "act")

    def ada_read(n):
        if ADA[n][1] in GATE_CHUNKS:
            for k in range(2):
                t.add(("gate", n, k), "act")
        else:
            t.add(("adaT", n), "dve")

    def ada(n0, n1):
        for n in range(n0, n1):
            ada_product(n)
            if n > n0:
                ada_read(n - 1)
        ada_read(n1 - 1)

    def norm(s, *tiles, step=t.add):
        for t_ in tiles:
            for q in range(2):
                step(("norm", s, t_, q), "dve" if q else "act")

    def project(l):
        for hh in range(2):
            for i in range(NT):
                t.add(("out", l, hh, i), "dve")
                if (hh, i) == (1, 1):
                    norm(2 * l + 1, 0)
        norm(2 * l + 1, 1)
        ada_product(LAST_GATE[l])
        norm(2 * l + 1, 2)

    def tokens(l, i):
        for h in range(2):
            t.add(("tokens", l, i, h), "act")

    def route(l):
        n = LAST_GATE[l]
        tokens(l, 0)
        t.add(("logits", l), "act")
        tokens(l, 1)
        t.add(("router", l), "dve")
        tokens(l, 2)
        ada_product(n + 1)
        ada_read(n)
        t.add(("rank", l), "dve")
        ada_read(n + 1)

    t.add("rows", "dve")
    for n in range(3):
        ada_product(n)
        if n > 0:
            ada_read(n - 1)
    norm(0, 0, 1, step=t.fill)
    ada_product(3)
    ada_read(2)
    ada_read(3)
    for i in range(2):
        for q in range(2):
            t.empty(("norm", 0, i, q))
    for c in range(len(W_IN_COLS)):
        for i in range(NT):
            t.add(("z", c, i), "act" if i % 2 or c == 2 else "dve")
            if (c, i) == (0, 0):
                norm(0, 2)
    for g in range(NPG):
        t.add(("pool", g), "act")
        if g > 0:
            t.add(("pooled", g - 1), "act")
    t.add(("pooled", NPG - 1), "act")
    ada(4, 7)
    for c in range(NH // 2):
        t.add(("qT", c), "act")
    t.add("kT", "act")

    def scores(i, half):
        for n in range(4 * half, 4 * half + 4):
            t.add(("score", i, n), "dve")

    def values(i, half):
        for n in range(4 * half, 4 * half + 4):
            t.add(("PT", i, n), "act")
        if half:
            t.add(("oT", i), "dve", bank=7)

    scores(0, 0)
    scores(0, 1)
    ada(7, 9)
    scores(1, 0)
    ada_product(9)
    values(0, 0)
    ada_read(9)
    scores(1, 1)
    ada_product(10)
    values(0, 1)
    ada_read(10)
    scores(2, 0)
    ada(11, 13)
    values(1, 0)
    ada_product(13)
    scores(2, 1)
    ada_read(13)
    ada(14, 16)
    values(1, 1)
    ada_product(16)
    values(2, 0)
    ada_read(16)
    ada_product(17)
    values(2, 1)
    ada_read(17)
    project(0)
    route(0)
    marks[0] = dict(t.emptied)
    t.all_free()
    ada_product(20)
    norm(2, 0)
    ada_product(21)
    norm(2, 1, 2)
    ada_read(20)
    t.add(("uT", 0), "dve")
    ada_read(21)
    for f in range(1, KT):
        t.add(("uT", f), "act" if f % 2 else "dve")
    for g in range(FG):
        for i in range(NT):
            t.add(("v", i, g), "dve" if (g * NT + i) % 2 else "act")
    t.fill("fM", "act", bank=7)
    for f in range(KT):
        t.add(("fT", f), "act" if f % 2 else "dve")
    t.empty("fM")
    project(1)
    route(1)
    marks[1] = dict(t.emptied)
    return t.of, marks


def build(nc, x_prompt, x_sample, cache_k, cache_v, ada_w,
          a_w_in, a_q_norm, a_k_norm, a_sink, pool_w, a_w_out, f_w_in, f_w_out,
          router_g_w, router_g_b, router_e_w, router_e_b, moe_w1, moe_w3, moe_w2,
          row_in, const, att_const, four_const, y_prompt, y_sample, new_k, new_v):
    turn, marks = plan()

    def cols(w, a, b):
        return w[:, a:b].rearrange("(k p) n -> p k n", p=P)

    ada_items = [cols(ada_w[l], HALF * n, HALF * (n + 1)) for l, n in ADA]
    w_in_items, at = [], 0
    for n in W_IN_COLS:
        w_in_items.append(cols(a_w_in[0], at, at + n))
        at += n
    halves = lambda w: [cols(w, 0, HALF), cols(w, HALF, D)]
    before0 = ada_items[0:4] + w_in_items + ada_items[4:18] + halves(a_w_out[0]) + ada_items[18:20]
    before1 = ada_items[20:22] + halves(f_w_in[0]) + halves(f_w_out[0]) + ada_items[22:24]
    N_EXP0 = len(before0)
    N_MIX1 = N_EXP0 + 3 * NE
    N_EXP1 = N_MIX1 + len(before1)
    n_exp = [N_EXP0, N_EXP1]
    N_WIN = 4
    N_WOUT = N_WIN + 3 + 14
    N_FIN = N_MIX1 + 2
    N_FOUT = N_FIN + 2

    def ada_at(n):
        start = 0
        for end, at in ((4, 0), (18, N_WIN + 3), (20, N_WOUT + 2), (22, N_MIX1), (24, N_FOUT + 2)):
            if n < end:
                return at + n - start
            start = end

    R_MIX, R_FFN, R_CCTX, R_C, R_PS = 0, L * KT, 2 * L * KT, 2 * L * KT + KT, 2 * L * KT + 2 * KT
    N_ROWS = R_PS + NPG
    N_BROWS = L * 6 * KT

    ctx = ExitStack()
    with ctx:
        def sb(name, shape, dt=F32):
            return ctx.enter_context(nc.sbuf_tensor(name, shape, dt))

        def sem(name):
            return ctx.enter_context(nc.semaphore(name))

        ring = sb("ring", [P, NS, SLOT])
        x = sb("x", [P, NT, D])
        h = sb("h", [P, NT, D])
        T = sb("T", [P, KT, TOK])
        Z = sb("Z", [P, 7424])
        gate_b = sb("gate_b", [P, 2, D])
        special = sb("special", [P, max(N_ATT, N_FOUR)])
        cst = sb("cst", [P, N_CONST])
        before_bf, ones_bf = (sb(f"{k}_bf", [P, P], BF16)[:, :] for k in ("before", "ones"))
        Ms = sb("Ms", [P, NT + 1, NE], BF16)
        ada_row = sb("ada_row", [P, 2, HALF])
        rows = sb("rows", [N_ROWS, P])
        rows_silu = sb("rows_silu", [N_ROWS, P])
        brows = sb("brows", [N_BROWS, P])
        colv = sb("colv", [P, N_ROWS])
        bcol = sb("bcol", [P, N_BROWS])
        cond = sb("cond", [P, KT, 32])
        mcol = sb("mcol", [P, L, 6, KT, 2])
        router_w = sb("router_w", [P, L, KT, 32])
        router_b = sb("router_b", [P, L, NG + NE])
        sink_in = sb("sink_in", [P, NH])
        sink = sb("sink", [P, NH])
        qk_gain = sb("qk_gain", [P, 2, HD])
        pool_ws = sb("pool_ws", [P, NPG, P])
        ckT_in = sb("ckT_in", [P, KVW])
        cv = sb("cv", [P, KVW])
        stat = sb("stat", [P, 2, NT])

        z = Z[:, 0:NT * ZW].rearrange("p (t n) -> p t n", t=NT)
        at = NT * ZW
        qT = Z[:, at:at + 4 * TOK].rearrange("p (c n) -> p c n", c=4)
        at += 4 * TOK
        kT = Z[:, at:at + TOK + PAST]
        at += TOK + PAST
        PT = Z[:, at:at + 4 * TOK].rearrange("p (b n) -> p b n", b=4)
        at += 4 * TOK
        small = sb("small", [P, 160])
        ssq, rsq = small[:, 96:126], small[:, 128:158]
        PC = sb("PC", [P, NH, P])
        pooled = PC[:, 0:6, :].rearrange("p a n -> p (a n)").rearrange("p (b n) -> p b n", b=2)
        assert at <= 7424
        hflat = h[:, :, :].rearrange("p t n -> p (t n)")
        PL = hflat[:, 0:NH * TOK].rearrange("p (h n) -> p h n", h=NH)
        N_BAND = ATT["band_ctx"][0]
        PB = special[:, N_BAND:N_BAND + 6 * TOK].rearrange("p (h n) -> p h n", h=6)
        assert N_BAND + 6 * TOK <= N_ATT

        def heads(i, a, b):
            if i < 2:
                return (PC if i == 0 else PL)[:, a:b, :]
            assert b <= 6 or a >= 6
            return PB[:, a:b, :] if b <= 6 else z[:, a - 6:b - 6, 0:TOK]

        def stats(i, half):
            at = 32 * i + 4 * half
            return [small[:, at + 8 * k:at + 8 * k + 4] for k in range(4)]

        sq = hflat[:, 0:NT * QKW].rearrange("p (t n) -> p t n", t=NT)
        rot0 = hflat[:, 0:QKW]
        rot1 = PT.rearrange("p b n -> p (b n)")[:, 0:QKW]
        qk = hflat[:, QKW:(1 + NT) * QKW].rearrange("p (t n) -> p t n", t=NT)
        uT = hflat.rearrange("p (c n) -> p c n", c=KT)
        VW = 2 * FH + 1
        v = Z[:, 0:NT * FG * VW].rearrange("p (t g n) -> p t g n", t=NT, g=FG)
        at = 0

        def zone(n):
            nonlocal at
            at += n
            return Z[:, at - n:at]

        at = 0
        B2 = 2 * BLK
        xT = zone(2 * KT * B2).rearrange("p (b k s) -> p b k s", b=2, k=KT)
        up_s = zone(2 * DE).rearrange("p (b n) -> p b n", b=2)
        sil = zone(FC * BLK).rearrange("p (k s) -> p k s", k=FC)
        aT = zone(2 * FC * BLK).rearrange("p (u k s) -> p u k s", u=2, k=FC)
        ys = zone(D)
        ys_over = xT[:, 1].rearrange("p k s -> p (k s)")
        Sel = zone(NT * B2).rearrange("p (t s) -> p t s", t=NT)
        CT = zone(2 * NT * B2).rearrange("p (b t s) -> p b t s", b=2, t=NT)
        Cs = zone(2 * TOK).rearrange("p (b n) -> p b n", b=2)
        S12 = special[:, N_FOUR:N_FOUR + 2 * NT * B2].rearrange("p (a t s) -> p a t s", a=2, t=NT)
        assert at <= 7424 and N_FOUR + 2 * NT * B2 <= N_ATT
        lrow = Cs[:, 0, :]
        acc = T[:, :, :].rearrange("p k n -> p (k n)").rearrange("p (t n) -> p t n", t=NT)
        scratch = special[:, 0:D]

        rt = PC[:, :, :].rearrange("p h n -> p (h n)")
        rat = [0]

        def rtile(*shape):
            n = int(np.prod(shape))
            a = rt[:, rat[0]:rat[0] + n]
            rat[0] += n
            if len(shape) == 1:
                return a
            names = "abcd"[:len(shape)]
            return a.rearrange(f"p ({' '.join(names)}) -> p {' '.join(names)}",
                               **{k: s for k, s in zip(names[:-1], shape[:-1])})

        lg = rtile(NT, NG + NE)
        mg, sg, pg, ml, se, p1 = (rtile(NT) for _ in range(6))
        dg, eg, og, sc4, le, de, ee, o1, o2, le2 = (rtile(NT, 4) for _ in range(10))
        prod = rtile(NT, 4, 4)
        M12 = rtile(2, NT, NE)
        G = rtile(NT, NE)
        ge = rtile(NT, NE)
        MG = rtile(2, NT, NE)
        G12 = rtile(2, NT)
        c12 = rtile(2, NT)
        cmp5 = rtile(NE, NTHR)
        ovc, ovb, off, incl = (rtile(NE) for _ in range(4))
        eidf = rtile(NOV + 1)
        tri_p = rtile(NE, NE)
        cmp_j = tri_p[:, 0:NOV, :]
        assert rat[0] <= NH * P
        plan_i = sb("plan_i", [P, NOV + 1], I32)

        def con(name, n=None):
            a, w = CONST[name]
            return cst[:, a:a + w]

        def att(name):
            a, w = ATT[name]
            return special[:, a:a + w]

        def four(name):
            a, w = FOUR[name]
            return special[:, a:a + w]

        ident = con("ident")
        banks = [ctx.enter_context(nc.psum_tensor(f"bank{i}", [P, HALF], F32)) for i in range(8)]
        psU, psT = banks[0:2]
        psC = psU
        psX, psD, psK = banks[2:4], banks[4:6], banks[6:8]

        arrived = [sem(f"arrived{i}") for i in range(NS)]
        small_in = sem("small_in")
        params_in = sem("params_in")
        x_in = [sem(f"x_in{t}") for t in range(NT)]
        special_in = sem("special_in")
        special_free = sem("special_free")
        full = sem("full")
        act_emptied = sem("act_emptied")
        dve_emptied = sem("dve_emptied")
        emptied = {"act": act_emptied, "dve": dve_emptied}
        cond_rows = sem("cond_rows")
        cols_ready = sem("cols_ready")
        zeroed = sem("zeroed")
        normed = sem("normed")
        affine_ready = sem("affine_ready")
        rms_ready = sem("rms_ready")
        qk_squares = sem("qk_squares")
        qk_sums = sem("qk_sums")
        qk_rms_ready = sem("qk_rms_ready")
        qk_ready = sem("qk_ready")
        kv_out_ready = sem("kv_out_ready")
        p_max = sem("p_max")
        p_exp = sem("p_exp")
        p_ready = sem("p_ready")
        pv_done = sem("pv_done")
        x_ready = sem("x_ready")
        g_shifted = sem("g_shifted")
        g_exp = sem("g_exp")
        ms_ready = sem("ms_ready")
        plan_ready = sem("plan_ready")
        middle_out_done = sem("middle_out_done")
        sums_ready = sem("sums_ready")
        late_half = sem("late_half")
        out_done = sem("out_done")
        kv_out_done = sem("kv_out_done")
        steps = ("sel_ready",
                 "weighted",
                 "gathered",
                 "x_cols",
                 "up_full",
                 "up_out",
                 "mid_full",
                 "silu_out",
                 "act_cols",
                 "comb_full",
                 "comb_out",
                 "down_full",
                 "down_out",
                 "back_full",
                 "back_out")
        pairs = [{k: sem(f"{k}_{l}") for k in steps} for l in range(L)]
        overs = [{k: sem(f"over_{k}_{l}") for k in steps + ("weights", "done")} for l in range(L)]

        block = ctx.enter_context(nc.Block())

        def last_use(n):
            for l in range(L):
                q = n - n_exp[l]
                if 0 <= q < 3 * NE:
                    p, m = q // 6, q % 6
                    if m < 4:
                        return pairs[l]["up_full"], 2 * p + m // 2 + 1
                    return pairs[l]["down_full"], p + 1
            for m in range(len(ADA)):
                if ada_at(m) == n:
                    return full, turn[("ada", m)][1]
            for first, keys in ((N_WIN, [("z", c, NT - 1) for c in range(len(W_IN_COLS))]),
                                (N_WOUT, [("out", 0, c, NT - 1) for c in range(2)]),
                                (N_FIN, [("uT", 4 * c + 3) for c in range(2)]),
                                (N_FOUT, [("out", 1, c, NT - 1) for c in range(2)])):
                if first <= n < first + len(keys):
                    return full, turn[keys[n - first]][1]

        def read_turn(n):
            return turn[("gate", n, 1) if ADA[n][1] in GATE_CHUNKS else ("adaT", n)]

        def stage_bank(key, e):
            bank, n, who, k, before = turn[key]
            taken[who] += 1
            assert k == taken[who], "an engine empties its banks in the plan's order"
            e.wait_ge(full, n)
            return banks[bank]

        taken = {"act": 0, "dve": 0}

        loads = {small_in: 0, params_in: 0}

        def small_load(e, dst, src, which):
            loads[which] += 16
            e.dma_start(dst, src).then_inc(which, 16)

        @block.sync
        def _(sp):
            def weights(n, src):
                if n >= NS:
                    sp.wait_ge(*last_use(n - NS))
                w = src.shape[2]
                dst = ring[:, n % NS, 0:KT * w].rearrange("p (k n) -> p k n", k=KT)
                sp.dma_start(dst, src).then_inc(arrived[n % NS], 16)

            def parameters():
                for l in range(L):
                    small_load(sp, router_w[:, l, :, 0:NG], router_g_w[l].rearrange("(k p) n -> p k n", p=P), params_in)
                    small_load(sp, router_w[:, l, :, NG:NG + NE], router_e_w[l].rearrange("(k p) n -> p k n", p=P), params_in)
                    small_load(sp, router_b[:, l, 0:NG], router_g_b[l:l + 1, :].to_broadcast([P, NG]), params_in)
                    small_load(sp, router_b[:, l, NG:], router_e_b[l:l + 1, :].to_broadcast([P, NE]), params_in)
                small_load(sp, sink_in[:, :], a_sink[0:1, :].to_broadcast([P, NH]), params_in)
                small_load(sp, qk_gain[:, 0, :], a_q_norm[0:1, :].to_broadcast([P, HD]), params_in)
                small_load(sp, qk_gain[:, 1, :], a_k_norm[0:1, :].to_broadcast([P, HD]), params_in)
                small_load(sp, pool_ws[:, :, :], pool_w[0].rearrange("g c d -> c g d"), params_in)
                small_load(sp, ckT_in[:, :], cache_k[0, 0].rearrange("s h d -> s (h d)"), params_in)
                small_load(sp, cv[:, :], cache_v[0, 0].rearrange("s h d -> s (h d)"), params_in)
                sp.dma_start(special[:, 0:N_ATT], att_const).then_inc(special_in, 16)

            small_load(sp, rows[:, :], row_in[0:N_ROWS, :], small_in)
            small_load(sp, brows[:, :], row_in[N_ROWS:N_ROWS + N_BROWS, :], small_in)
            small_load(sp, cst[:, :], const, small_in)
            for n, src in enumerate(before0):
                weights(n, src)
                if n in (2, 3):
                    t = n - 1
                    sp.dma_start(x[:, t, :], x_sample[0, (t - 1) * P:t * P, :]).then_inc(x_in[t], 16)
                if n == NS - 1:
                    sp.wait_ge(zeroed, 1)
                    parameters()
            for l in range(L):
                n0, s, o = n_exp[l], pairs[l], overs[l]
                if l == 1:
                    for n, src in enumerate(before1):
                        weights(N_MIX1 + n, src)

                def expert(e, k, w):
                    n = n0 + k
                    kk = KT if k < 4 else FC
                    dst = ring[:, n % NS, :].rearrange("p (k n) -> p k n", k=kk)
                    sp.dma_start(dst, w[l, bass.ds(e, 1), :, :].rearrange("a (k p) n -> p (a k) n", p=P))\
                      .then_inc(arrived[n % NS], 16)

                items = [(0, moe_w1), (0, moe_w3), (1, moe_w1), (1, moe_w3), (0, moe_w2), (1, moe_w2)]
                for k, (u, w) in enumerate(items):
                    sp.wait_ge(*last_use(n0 + k - NS))
                    expert(u, k, w)
                with sp.Fori(1, NPAIR - 1) as i:
                    for k, (u, w) in enumerate(items):
                        if k < 4:
                            sp.wait_ge(s["up_full"], i * 2 + (k // 2 - 1))
                        else:
                            sp.wait_ge(s["down_full"], i)
                        expert(i * 2 + u, k, w)
                for k, (u, w) in enumerate(items[:5]):
                    if k < 4:
                        sp.wait_ge(s["up_full"], 2 * (NPAIR - 1) + k // 2 - 1)
                    else:
                        sp.wait_ge(s["down_full"], NPAIR - 1)
                    expert(2 * (NPAIR - 1) + u, k, w)
                src = moe_w2[l, NE - 1].rearrange("(k p) n -> p k n", p=P)
                dst = ring[:, (n0 + 5) % NS, :].rearrange("p (k n) -> p k n", k=FC)
                sp.dma_start(dst[:, 0:FC // 2], src[:, 0:FC // 2]).then_inc(arrived[(n0 + 5) % NS], 16)
                sp.dma_start(dst[:, FC // 2:], src[:, FC // 2:]).then_inc(late_half, 16)
                sp.wait_ge(plan_ready, l + 1)
                blocks = sp.value_load(plan_i[0:1, NOV:NOV + 1], min_val=0, max_val=NOV)
                with sp.If(blocks > 0):
                    with sp.Fori(0, NOV) as j:
                        with sp.If(j < blocks):
                            sp.wait_ge(s["up_full"], NE)
                            sp.wait_ge(o["done"], j + 1)
                            ex = sp.value_load(plan_i[0:1, bass.ds(j, 1)], min_val=0, max_val=NE - 1)
                            for m, w in enumerate((moe_w1, moe_w3, moe_w2)):
                                kk = KT if m < 2 else FC
                                dst = ring[:, (n0 + m) % NS, :].rearrange("p (k n) -> p k n", k=kk)
                                sp.dma_start(dst, w[l, bass.ds(ex, 1), :, :].rearrange("a (k p) n -> p (a k) n", p=P))\
                                  .then_inc(o["weights"], 16)
                sp.wait_ge(o["done"], blocks + 1)
            for i in range(NT):
                sp.wait_ge(x_ready, 3 * NT + i + 1)
                dst = y_prompt[0] if i == 0 else y_sample[0, (i - 1) * P:i * P, :]
                sp.dma_start(dst, x[:, i, :]).then_inc(out_done, 16)
            sp.wait_ge(out_done, 16 * NT)
            sp.wait_ge(kv_out_done, 32)

        @block.gpsimd
        def _(gp):
            gp.memset(router_w[:, :, :, :], 0.0)
            gp.memset(cond[:, :, :], 0.0).then_inc(zeroed, 1)
            gp.wait_ge(kv_out_ready, 1)
            gp.dma_start(new_k[0, 0].rearrange("s h d -> s (h d)"), qk[:, 0, AW:QKW]).then_inc(kv_out_done, 16)
            gp.dma_start(new_v[0, 0].rearrange("s h d -> s (h d)"), z[:, 0, AW + KVW:AW + 2 * KVW]).then_inc(kv_out_done, 16)
            for l in range(L):
                last = turn[("tokens", l, NT - 1, 1)]
                gp.wait_ge(full, last[1])
                gp.memset(acc[:, :, :], 0.0).then_inc(zeroed, 1)

        @block.scalar
        def _(act):
            act.dma_start(x[:, 0, :], x_prompt[0]).then_inc(x_in[0], 16)

            def emptied_inc(ins):
                ins.then_inc(act_emptied, 1)

            def rms(s, t):
                if s == 0:
                    act.wait_ge(x_in[t], 16)
                else:
                    act.wait_ge(x_ready, NT * (s - 1) + t + 1)
                act.activation(h[:, t, :], x[:, t, :], ACT.Square, accum_out=stat[:, 0, t:t + 1])
                act.drain()
                act.activation(stat[:, 1, t:t + 1], stat[:, 0, t:t + 1], ACT.Sqrt, scale=1.0 / D, bias=con("eps"))\
                   .then_inc(rms_ready, 1)

            def ada_product(n):
                b = stage_bank(("ada", n), act)
                if n >= 2:
                    act.wait_ge(full, read_turn(n - 2)[1])
                emptied_inc(act.activation(ada_row[:, n % 2, :], b[:, :], ACT.Copy))

            def ada_read(n):
                l, cc = ADA[n]
                if cc in GATE_CHUNKS:
                    s = 2 * l + (cc >= 10)
                    if s > 0:
                        act.wait_ge(x_ready, NT * s)
                    for k in range(2):
                        b = stage_bank(("gate", n, k), act)
                        emptied_inc(act.activation(gate_b[:, k, HALF * (cc % 2):HALF * (cc % 2 + 1)], b[:, :], ACT.Copy))

            def ada(n0, n1):
                for n in range(n0, n1):
                    ada_product(n)
                    if n > n0:
                        ada_read(n - 1)
                ada_read(n1 - 1)

            def affine(s, t):
                l, f = s // 2, s % 2
                act.wait_ge(affine_ready, s + 1)
                b = stage_bank(("norm", s, t, 0), act)
                c = min(t, 1)
                for k in range(4):
                    last = act.activation(T[:, k, t * P:(t + 1) * P], b[:, k * P:(k + 1) * P], ACT.Identity,
                                          scale=mcol[:, l, 3 * f + 1, k, c:c + 1], bias=mcol[:, l, 3 * f, k, c:c + 1])
                emptied_inc(last)

            def norm_ffn_act(l):
                s = 2 * l + 1
                rms(s, 0)
                rms(s, 1)
                affine(s, 0)
                rms(s, 2)
                affine(s, 1)
                ada_product(LAST_GATE[l])
                affine(s, 2)

            def exps(i, half):
                act.wait_ge(p_max, 2 * i + half + 1)
                w = SEQ if i == 0 else TOK
                mx, nmx, den, es = stats(i, half)
                for n in range(4):
                    pr = heads(i, 4 * half + n, 4 * half + n + 1)[:, 0, 0:w]
                    act.activation(pr, pr, ACT.Exp, bias=nmx[:, n:n + 1], accum_out=den[:, n:n + 1])
                act.activation(es, es, ACT.Exp).then_inc(p_exp, 1)

            def turned(i, half):
                w = SEQ if i == 0 else TOK
                for n in range(4 * half, 4 * half + 4):
                    b = stage_bank(("PT", i, n), act)
                    if NH * i + n >= 4:
                        act.wait_ge(pv_done, (NH * i + n) // 2 - 1)
                    emptied_inc(act.activation(PT[:, n % 4, 0:w], b[:, 0:w], ACT.Copy))

            def z_copy(cc, i):
                if turn[("z", cc, i)][2] == "act":
                    b = stage_bank(("z", cc, i), act)
                    w, a = W_IN_COLS[cc], sum(W_IN_COLS[:cc])
                    emptied_inc(act.activation(z[:, i, a:a + w], b[:, 0:w], ACT.Copy))

            act.wait_ge(small_in, loads[small_in])
            act.activation(rows_silu[:, :], rows[:, :], ACT.Silu).then_inc(cond_rows, 1)
            ada_product(0)
            rms(0, 0)
            ada_product(1)
            ada_product(2)
            rms(0, 1)
            ada_product(3)
            rms(0, 2)
            affine(0, 0)
            affine(0, 1)
            z_copy(0, 0)
            affine(0, 2)

            for cc in range(2):
                for i in range(NT):
                    if (cc, i) != (0, 0):
                        z_copy(cc, i)
            act.wait_ge(dve_emptied, turn[("z", 1, 2)][3])
            act.wait_ge(act_emptied, turn[("z", 1, 1)][3])
            act.activation(sq[:, :, :], z[:, :, 0:QKW], ACT.Square).then_inc(qk_squares, 1)
            act.wait_ge(qk_sums, 1)
            act.activation(rsq, ssq, ACT.Sqrt, scale=1.0 / HD, bias=con("eps")).then_inc(qk_rms_ready, 1)
            for i in range(NT):
                z_copy(2, i)
            for g in range(NPG + 1):
                if g < NPG:
                    b = stage_bank(("pool", g), act)
                    if g >= 2:
                        act.wait_ge(full, turn[("pooled", g - 2)][1])
                    emptied_inc(act.activation(pooled[:, g % 2, :], b[:, 0:TOK], ACT.Copy))
                if g > 0:
                    b = stage_bank(("pooled", g - 1), act)
                    emptied_inc(act.activation(T[:, 4 + g - 1, :], b[:, 0:TOK], ACT.Identity,
                                               scale=colv[:, R_PS + g - 1:R_PS + g]))
            ada(4, 7)
            for cc in range(NH // 2):
                b = stage_bank(("qT", cc), act)
                emptied_inc(act.activation(qT[:, cc, :], b[:, 0:TOK], ACT.Copy))
            b = stage_bank("kT", act)
            emptied_inc(act.activation(kT, b[:, 0:TOK + PAST], ACT.Copy))
            exps(0, 0)
            exps(0, 1)
            ada(7, 9)
            ada_product(9)
            turned(0, 0)
            exps(1, 0)
            ada_product(10)
            turned(0, 1)
            exps(1, 1)
            ada(11, 13)
            turned(1, 0)
            exps(2, 0)
            ada_product(13)
            ada(14, 16)
            turned(1, 1)
            exps(2, 1)
            ada_product(16)
            turned(2, 0)
            ada_product(17)
            turned(2, 1)

            def tokens(l, i):
                for hh in range(2):
                    b = stage_bank(("tokens", l, i, hh), act)
                    emptied_inc(act.activation(h[:, i, HALF * hh:HALF * (hh + 1)], b[:, :], ACT.Copy))

            def moe(l):
                def up_copy(s, e, u):
                    act.wait_ge(s["up_full"], e + 1)
                    act.activation(up_s[:, u, :], psU[:, :], ACT.Copy).then_inc(s["up_out"], 1)

                def silu(s, e):
                    act.wait_ge(s["mid_full"], e + 1)
                    mid = psT[:, :].rearrange("p (k s) -> p k s", k=FC)
                    act.activation(sil, mid[:, :, 0:BLK], ACT.Silu).then_inc(s["silu_out"], 1)

                def comb_copy(s, p, b, w):
                    act.wait_ge(s["comb_full"], p + 1)
                    act.activation(Cs[0:w, b, :], psC[0:w, 0:TOK], ACT.Copy).then_inc(s["comb_out"], 1)

                def down_copy(s, p, w):
                    act.wait_ge(s["down_full"], p + 1)
                    out = ys if s is pairs[l] else ys_over
                    for hh in range(2):
                        last = act.activation(out[0:w, HALF * hh:HALF * (hh + 1)], psD[hh][0:w, :], ACT.Copy)
                    last.then_inc(s["down_out"], 1)

                def pair(p, b):
                    for u in range(2):
                        up_copy(pairs[l], p * 2 + u, u)
                        silu(pairs[l], p * 2 + u)
                    comb_copy(pairs[l], p, b, 2 * BLK)
                    down_copy(pairs[l], p, 2 * BLK)

                for q in range(2):
                    act.wait_ge(pairs[l]["gathered"], q + 1)
                    act.activation(xT[:, 0, 4 * q:4 * q + 4, :], psX[q][:, :].rearrange("p (k s) -> p k s", k=4), ACT.Copy)\
                       .then_inc(pairs[l]["x_cols"], 1)
                with act.Fori(0, NPAIR // 2) as i:
                    for b in range(2):
                        pair(i * 2 + b, b)
                act.wait_ge(plan_ready, l + 1)
                blocks = act.value_load(plan_i[0:1, NOV:NOV + 1], min_val=0, max_val=NOV)
                with act.If(blocks > 0):
                    with act.Fori(0, NOV) as j:
                        with act.If(j < blocks):
                            up_copy(overs[l], j, 0)
                            silu(overs[l], j)
                            comb_copy(overs[l], j, 0, BLK)
                            down_copy(overs[l], j, BLK)

            for l in range(L):
                if l == 1:
                    rms(2, 0)
                    ada_product(20)
                    rms(2, 1)
                    affine(2, 0)
                    rms(2, 2)
                    ada_product(21)
                    affine(2, 1)
                    affine(2, 2)
                    ada_read(20)
                    ada_read(21)
                    for g in range(FG):
                        b = stage_bank(("uT", 2 * g + 1), act)
                        emptied_inc(act.activation(uT[:, 2 * g + 1, :], b[:, 0:TOK], ACT.Copy))
                    for g in range(FG):
                        for i in range(NT):
                            if turn[("v", i, g)][2] == "act":
                                b = stage_bank(("v", i, g), act)
                                emptied_inc(act.activation(v[:, i, g, :], b[:, 0:VW], ACT.Copy))
                    middle = banks[turn["fM"][0]]

                    def middle_out(g):
                        act.wait_ge(dve_emptied, turn[("fT", 2 * g)][3])
                        return act.activation(T[0:1, 2 * g + 1, :], middle[32 * g:32 * g + 1, 0:TOK], ACT.Copy)\
                                  .then_inc(middle_out_done, 1)

                    for g in range(FG):
                        b = stage_bank(("fT", 2 * g + 1), act)
                        emptied_inc(act.activation(T[:, 2 * g + 1, :], b[:, 0:TOK], ACT.Copy))
                        if g > 0:
                            middle_out(g - 1)
                    stage_bank("fM", act)
                    middle_out(FG - 1)
                    emptied_inc(act.drain())
                norm_ffn_act(l)
                tokens(l, 0)
                b = stage_bank(("logits", l), act)
                emptied_inc(act.activation(lrow, b[:, 0:TOK], ACT.Copy))
                tokens(l, 1)
                tokens(l, 2)
                n = LAST_GATE[l]
                ada_product(n + 1)
                ada_read(n)
                act.wait_ge(g_shifted, 2 * l + 2)
                act.activation(eg, dg, ACT.Exp)
                act.activation(ee, de, ACT.Exp).then_inc(g_exp, 1)
                ada_read(n + 1)
                if l == 0:
                    act.wait_ge(special_free, 1)
                    act.dma_start(special[:, 0:N_FOUR], four_const).then_inc(special_in, 16)
                moe(l)

        @block.vector
        def _(dve):
            def settle():
                dve.drain()

            def emptied_inc(ins):
                ins.then_inc(dve_emptied, 1)

            def bc(ap, *shape):
                return ap.to_broadcast([P, *shape])

            def norm(s, t):
                dve.wait_ge(rms_ready, NT * s + t + 1)
                dve.reciprocal(stat[:, 0, t:t + 1], stat[:, 1, t:t + 1])
                settle()
                dve.tensor_scalar(h[:, t, :], x[:, t, :], stat[:, 0, t:t + 1], None, ALU.mult).then_inc(normed, 1)

            def affine(s, t):
                l, f = s // 2, s % 2
                b = stage_bank(("norm", s, t, 1), dve)
                c = min(t, 1)
                for k in range(4):
                    last = dve.tensor_scalar(T[:, 4 + k, t * P:(t + 1) * P], b[:, k * P:(k + 1) * P],
                                             mcol[:, l, 3 * f + 1, 4 + k, c:c + 1], mcol[:, l, 3 * f, 4 + k, c:c + 1],
                                             ALU.mult, ALU.add)
                emptied_inc(last)

            def ada_read(n):
                l, cc = ADA[n]
                if cc in GATE_CHUNKS:
                    return
                b = stage_bank(("adaT", n), dve)
                src = b[:, :].rearrange("p (s q r) -> p s r q", s=4, q=4)[:, :, 0:2, :]
                k0 = 4 * (cc % 2)
                emptied_inc(dve.tensor_reduce(mcol[:, l, cc // 2, k0:k0 + 4, :], src, AX.X, ALU.add))
                if cc in (3, 9):
                    f = cc // 6
                    settle()
                    bias = bcol[:, (6 * l + 3 * f) * KT:(6 * l + 3 * f + 2) * KT]
                    m = mcol[:, l, 3 * f:3 * f + 2].rearrange("p v k c -> p (v k) c")
                    dve.tensor_tensor(m, m, bias.unsqueeze(2).to_broadcast([P, 2 * KT, 2]), ALU.add)
                    settle()
                    r = (R_MIX, R_FFN)[f]
                    gain = colv[:, r + l * KT:r + (l + 1) * KT].unsqueeze(2).to_broadcast([P, KT, 2])
                    sc = mcol[:, l, 3 * f + 1]
                    dve.scalar_tensor_tensor(sc, sc, 1.0, gain, ALU.add, ALU.mult).then_inc(affine_ready, 1)
                    settle()

            def ada(n0, n1):
                for n in range(n0, n1):
                    ada_read(n)

            def gated_add(l):
                dve.wait_ge(act_emptied, turn[("gate", MIX_GATE[l] + 1, 1)][3])
                for hh in range(2):
                    for i in range(NT):
                        b = stage_bank(("out", l, hh, i), dve)
                        cs = slice(HALF * hh, HALF * (hh + 1))
                        n = NT * hh + i
                        gated = scratch[:, HALF * (n % 2):HALF * (n % 2 + 1)]
                        emptied_inc(dve.tensor_tensor(gated, b[:, :], gate_b[:, min(i, 1), cs], ALU.mult))
                        settle()
                        last = dve.tensor_tensor(x[:, i, cs], x[:, i, cs], gated, ALU.add)
                        if hh == 1:
                            last.then_inc(x_ready, 1)
                            if i > 0:
                                affine(2 * l + 1, i - 1)
                            norm(2 * l + 1, i)
                affine(2 * l + 1, NT - 1)

            def add_reduce(out, in_):
                return dve.tensor_reduce(out, in_, AX.X, ALU.add)

            def first_largest(one):
                dve.tensor_reduce(sg, sc4, AX.X, ALU.max)
                settle()
                dve.tensor_tensor(one, sc4, bc(sg.unsqueeze(2), NT, 4), ALU.is_equal)
                settle()

            descending = con("desc").unsqueeze(1)
            g6 = G12.rearrange("p a t -> p (a t)")
            c6 = c12.rearrange("p a t -> p (a t)")
            S6 = S12.rearrange("p a t s -> p (a t) s")

            def one_hot(s, w):
                dve.tensor_tensor(S6[:, :, 0:w], bc(con("iota")[:, 0:w].unsqueeze(1), 2 * NT, w),
                                  bc(g6.unsqueeze(2), 2 * NT, w), ALU.is_equal)
                settle()
                dve.tensor_tensor(Sel[:, :, 0:w], S12[:, 0, :, 0:w], S12[:, 1, :, 0:w], ALU.add)\
                   .then_inc(s["sel_ready"], 1)

            def weighted(s, b, w):
                dve.tensor_scalar(g6, g6, -float(w), None, ALU.add)
                dve.tensor_tensor(S6[:, :, 0:w], S6[:, :, 0:w], bc(c6.unsqueeze(2), 2 * NT, w), ALU.mult)
                settle()
                dve.tensor_tensor(CT[:, b, :, 0:w], S12[:, 0, :, 0:w], S12[:, 1, :, 0:w], ALU.add)\
                   .then_inc(s["weighted"], 1)
                settle()

            def slots_of_tokens():
                dve.tensor_tensor(MG, M12, bc(G.unsqueeze(1), 2, NT, NE), ALU.mult)
                settle()
                add_reduce(G12, MG)
                settle()

            def route(l):
                b = stage_bank(("router", l), dve)
                parts = b[:, 0:TOK].rearrange("p (t q n) -> p t n q", t=NT, q=4)[:, :, 0:NG + NE, :]
                emptied_inc(dve.tensor_reduce(lg, parts, AX.X, ALU.add))
                settle()
                dve.tensor_tensor(lg, lg, bc(router_b[:, l, :].unsqueeze(1), NT, NG + NE), ALU.add)
                settle()
                dve.tensor_reduce(mg, lg[:, :, 0:NG], AX.X, ALU.max)
                settle()
                dve.tensor_tensor(dg, lg[:, :, 0:NG], bc(mg.unsqueeze(2), NT, NG), ALU.subtract).then_inc(g_shifted, 1)
                settle()
                dve.scalar_tensor_tensor(sc4, dg, 0.0, bc(descending, NT, NG), ALU.is_equal, ALU.mult)
                settle()
                first_largest(og)
                dve.tensor_tensor(prod, lg[:, :, NG:].rearrange("p t (g e) -> p t e g", g=NG),
                                  bc(og.unsqueeze(2), NT, EPG, NG), ALU.mult)
                settle()
                add_reduce(le, prod)
                settle()
                dve.tensor_reduce(ml, le, AX.X, ALU.max)
                settle()
                dve.tensor_tensor(de, le, bc(ml.unsqueeze(2), NT, EPG), ALU.subtract).then_inc(g_shifted, 1)
                settle()
                dve.scalar_tensor_tensor(sc4, de, 0.0, bc(descending, NT, EPG), ALU.is_equal, ALU.mult)
                settle()
                first_largest(o1)
                dve.scalar_tensor_tensor(le2, o1, LOWEST, le, ALU.mult, ALU.add)
                settle()
                dve.tensor_reduce(ml, le2, AX.X, ALU.max)
                settle()
                dve.tensor_tensor(sc4, le2, bc(ml.unsqueeze(2), NT, EPG), ALU.is_equal)
                settle()
                dve.tensor_tensor(sc4, sc4, bc(descending, NT, EPG), ALU.mult)
                settle()
                first_largest(o2)
                for n, o in enumerate((o1, o2)):
                    dve.tensor_tensor(M12[:, n].rearrange("p t (g e) -> p t g e", g=NG),
                                      bc(og.unsqueeze(3), NT, NG, EPG), bc(o.unsqueeze(2), NT, NG, EPG), ALU.mult)
                settle()
                dve.tensor_tensor(Ms[:, 0:NT, :], M12[:, 0], M12[:, 1], ALU.add).then_inc(ms_ready, 1)
                b = stage_bank(("rank", l), dve)
                rank = b[:, 0:NT * NE].rearrange("p (t e) -> p t e", t=NT)
                count = b[:, NT * NE:(NT + 1) * NE]
                dve.tensor_scalar(ge, rank, float(BLK), float(BLK * NE), ALU.is_ge, ALU.mult)
                dve.tensor_tensor(G, rank, bc(con("first").unsqueeze(1), NT, NE), ALU.add)
                emptied_inc(dve.tensor_tensor(cmp5, bc(count.unsqueeze(2), NE, NTHR),
                                              bc(con("limit").unsqueeze(1), NE, NTHR), ALU.is_gt))
                settle()
                dve.tensor_tensor(G, G, ge, ALU.add)
                settle()
                slots_of_tokens()
                one_hot(pairs[l], 2 * BLK)
                dve.wait_ge(g_exp, l + 1)
                add_reduce(sg, eg)
                add_reduce(se, ee)
                add_reduce(ovc, cmp5)
                settle()
                dve.reciprocal(pg, sg)
                dve.reciprocal(se, se)
                dve.tensor_tensor(tri_p, bc(ovc.unsqueeze(1), NE, NE),
                                  con("tri").rearrange("p (e f) -> p e f", e=NE), ALU.mult)
                settle()
                dve.tensor_tensor(ee, ee, bc(se.unsqueeze(2), NT, EPG), ALU.mult)
                add_reduce(ovb, tri_p)
                add_reduce(eidf[:, NOV:NOV + 1], ovc)
                settle()
                dve.tensor_tensor(prod[:, :, 0, :], ee, o1, ALU.mult)
                dve.tensor_tensor(prod[:, :, 1, :], ee, o2, ALU.mult)
                dve.tensor_tensor(incl, ovb, ovc, ALU.add)
                dve.scalar_tensor_tensor(off, ovb, float(BLK), con("shift"), ALU.mult, ALU.add)
                settle()
                add_reduce(c12[:, 0, :], prod[:, :, 0, :])
                add_reduce(c12[:, 1, :], prod[:, :, 1, :])
                dve.tensor_tensor(cmp_j, bc(incl.unsqueeze(1), NOV, NE), bc(con("jrow").unsqueeze(2), NOV, NE), ALU.is_le)
                dve.tensor_scalar(off, off, -float(BLK * NE), 1.0 / (BLK * NE), ALU.add, ALU.mult)
                settle()
                dve.tensor_tensor(p1, c12[:, 0, :], c12[:, 1, :], ALU.add)
                dve.tensor_tensor(ge, ge, bc(off.unsqueeze(1), NT, NE), ALU.mult)
                add_reduce(eidf[:, 0:NOV], cmp_j)
                settle()
                dve.reciprocal(p1, p1)
                dve.tensor_tensor(G, G, ge, ALU.add)
                dve.tensor_scalar(eidf[:, 0:NOV], eidf[:, 0:NOV], float(NE - 1), None, ALU.min)
                settle()
                dve.tensor_tensor(p1, p1, pg, ALU.mult)
                dve.tensor_copy(plan_i[:, :], eidf).then_inc(plan_ready, 1)
                slots_of_tokens()
                dve.tensor_tensor(c12, c12, bc(p1.unsqueeze(1), 2, NT), ALU.mult)
                settle()
                weighted(pairs[l], 0, 2 * BLK)

            def moe(l):
                def gather_out(s, n, b, q, w):
                    dve.wait_ge(s["gathered"], n + 1)
                    dve.tensor_copy(xT[:, b, 4 * q:4 * q + 4, 0:w], psX[q][:, 0:4 * w].rearrange("p (k s) -> p k s", k=4))\
                       .then_inc(s["x_cols"], 1)

                def hidden(s, e, u):
                    dve.wait_ge(s["silu_out"], e + 1)
                    mid = psT[:, :].rearrange("p (k s) -> p k s", k=FC)
                    dve.tensor_tensor(aT[:, u], sil, mid[:, :, BLK:2 * BLK], ALU.mult).then_inc(s["act_cols"], 1)

                def add_back(s, p, n0=0, n1=2 * NT):
                    for n in range(n0, n1):
                        dve.wait_ge(s["back_full"], p * (2 * NT) + (n + 1))
                        a = acc[:, n // 2, HALF * (n % 2):HALF * (n % 2 + 1)]
                        dve.tensor_tensor(a, a, psK[n % 2][:, :], ALU.add).then_inc(s["back_out"], 1)

                def select(s, b, w, before=None):
                    one_hot(s, w)
                    settle()
                    if before is not None:
                        dve.wait_ge(s["comb_full"], before)
                    weighted(s, b, w)

                def pair(s, p, b, first=False):
                    w = 2 * BLK
                    select(s, 1 - b, w, None if first else p)
                    gather_out(s, p * 2 + 2, 1 - b, 0, w)
                    hidden(s, p * 2, 0)
                    gather_out(s, p * 2 + 3, 1 - b, 1, w)
                    hidden(s, p * 2 + 1, 1)
                    if not first:
                        add_back(s, p - 1)

                s, o = pairs[l], overs[l]
                dve.wait_ge(zeroed, l + 2)
                dve.wait_ge(s["gathered"], 2)
                pair(s, 0, 0, first=True)
                pair(s, 1, 1)
                with dve.Fori(1, NPAIR // 2 - 1) as i:
                    for b in range(2):
                        pair(s, i * 2 + b, b)
                pair(s, NPAIR - 2, 0)
                last = NPAIR - 1
                add_back(s, last - 1, 0, NT)
                hidden(s, last * 2, 0)
                add_back(s, last - 1, NT, 2 * NT)
                hidden(s, last * 2 + 1, 1)
                dve.wait_ge(plan_ready, l + 1)
                dve.sem_inc(o["done"], 1)
                blocks = dve.value_load(plan_i[0:1, NOV:NOV + 1], min_val=0, max_val=NOV)
                with dve.If(blocks > 0):
                    with dve.Fori(0, NOV) as j:
                        with dve.If(j < blocks):
                            select(o, 0, BLK)
                            for q in range(2):
                                gather_out(o, j * 2 + q, 0, q, BLK)
                            hidden(o, j, 0)
                            add_back(o, j)
                            dve.drain().then_inc(o["done"], 1)
                dve.drain().then_inc(sums_ready, 1)
                dve.wait_ge(act_emptied, turn[("gate", LAST_GATE[l] + 1, 1)][3])
                for i in range(NT):
                    dve.tensor_tensor(acc[:, i, :], acc[:, i, :], gate_b[:, min(i, 1), :], ALU.mult)
                settle()
                for i in range(NT):
                    dve.tensor_tensor(x[:, i, :], x[:, i, :], acc[:, i, :], ALU.add)
                settle()
                for n in range(2 * NT):
                    i, cs = n // 2, slice(HALF * (n % 2), HALF * (n % 2 + 1))
                    dve.wait_ge(s["back_full"], last * 2 * NT + n + 1)
                    gated = ys_over[:, HALF * (n % 2):HALF * (n % 2 + 1)]
                    dve.tensor_tensor(gated, psK[n % 2][:, :], gate_b[:, min(i, 1), cs], ALU.mult)\
                       .then_inc(s["back_out"], 1)
                    settle()
                    ins = dve.tensor_tensor(x[:, i, cs], x[:, i, cs], gated, ALU.add)
                    if n % 2:
                        ins.then_inc(x_ready, 1)
                        if l == 0 and i > 0:
                            norm(2, i - 1)

            dve.wait_ge(small_in, loads[small_in])
            dve.tensor_copy(before_bf, con("before"))
            dve.tensor_copy(ones_bf, con("ones"))
            dve.memset(Ms[:, NT, :], 0.0)
            b = stage_bank("rows", dve)
            dve.wait_ge(zeroed, 1)
            dve.tensor_copy(colv[:, :], b[:, 0:N_ROWS])
            dve.tensor_copy(bcol[:, :], b[:, P:P + N_BROWS])
            for k, r in enumerate((R_CCTX, R_C)):
                last = dve.tensor_copy(cond[:, :, k], b[:, 2 * P + r:2 * P + r + KT])
            emptied_inc(last)
            norm(0, 0)
            ada(0, 2)
            norm(0, 1)
            ada(2, 4)
            affine(0, 0)
            norm(0, 2)
            affine(0, 1)
            for cc in range(len(W_IN_COLS)):
                for i in range(NT):
                    if turn[("z", cc, i)][2] == "dve":
                        b = stage_bank(("z", cc, i), dve)
                        w, a = W_IN_COLS[cc], sum(W_IN_COLS[:cc])
                        emptied_inc(dve.tensor_copy(z[:, i, a:a + w], b[:, 0:w]))
                    if (cc, i) == (0, 0):
                        affine(0, 2)
            dve.wait_ge(params_in, loads[params_in])
            dve.tensor_copy(sink[:, :].rearrange("p (c k) -> p k c", k=NKV), sink_in[:, :].rearrange("p (k c) -> p k c", k=NKV))
            dve.wait_ge(qk_squares, 1)
            dve.tensor_reduce(ssq, sq[:, :, :].rearrange("p t (h d) -> p (t h) d", d=HD), AX.X, ALU.add)\
               .then_inc(qk_sums, 1)
            dve.wait_ge(qk_rms_ready, 1)
            dve.reciprocal(rsq, rsq)
            settle()
            zq = z[:, :, 0:QKW].rearrange("p t (h d) -> p t h d", d=HD)
            rq = rsq.rearrange("p (t h) -> p t h", t=NT).unsqueeze(3)
            dve.tensor_tensor(zq, zq, bc(rq, NT, NQK, HD), ALU.mult)
            settle()
            for i in range(NT):
                dve.tensor_tensor(qk[:, i, 0:AW].rearrange("p (c k d) -> p k c d", k=NKV, d=HD),
                                  z[:, i, 0:AW].rearrange("p (k c d) -> p k c d", k=NKV, d=HD),
                                  bc(qk_gain[:, 0, :].unsqueeze(1).unsqueeze(1), NKV, NH // NKV, HD), ALU.mult)
            kz = zq[:, :, NH:NQK]
            dve.tensor_tensor(qk[:, :, AW:QKW].rearrange("p t (h d) -> p t h d", d=HD), kz,
                              bc(qk_gain[:, 1, :].unsqueeze(1).unsqueeze(1), NT, NKV, HD), ALU.mult)\
               .then_inc(kv_out_ready, 1)
            settle()
            dve.wait_ge(special_in, 16)
            for i in (1, 2):
                zi = qk[:, i, :].rearrange("p (h d) -> p h d", d=HD)
                cosr = att("cos")[:, (i - 1) * HD:i * HD].unsqueeze(1)
                r0 = rot0.rearrange("p (h d) -> p h d", d=HD)
                dve.tensor_tensor(r0, zi, bc(cosr, NQK, HD), ALU.mult)
                z5 = qk[:, i, :].rearrange("p (h a b f) -> p h a b f", a=2, b=2, f=HD // 4)
                r5 = rot1.rearrange("p (h a b f) -> p h a b f", a=2, b=2, f=HD // 4)
                s5 = att("sin")[:, (i - 1) * HD:i * HD].rearrange("p (a b f) -> p a b f", a=2, b=2)
                for b2 in range(2):
                    sn = s5[:, :, b2, :].unsqueeze(1)
                    dve.tensor_tensor(r5[:, :, :, b2, :], z5[:, :, :, 1 - b2, :], bc(sn, NQK, 2, HD // 4), ALU.mult)
                settle()
                last = dve.tensor_tensor(zi, r0, rot1.rearrange("p (h d) -> p h d", d=HD), ALU.add)
                settle()
            last.then_inc(qk_ready, 1)
            ada(4, 7)

            def scores(i, half):
                w = SEQ if i == 0 else TOK
                a, e = 4 * half, 4 * half + 4
                for n in range(a, e):
                    b = stage_bank(("score", i, n), dve)
                    out = heads(i, n, n + 1)[:, 0, :]
                    if i == 0:
                        emptied_inc(dve.tensor_scalar(out, b[:, 0:w], HD ** -0.5, None, ALU.mult))
                    else:
                        m = att("mask")[:, (i - 1) * TOK:i * TOK]
                        emptied_inc(dve.scalar_tensor_tensor(out, b[:, 0:w], HD ** -0.5, m, ALU.mult, ALU.add))
                settle()
                mx, nmx, den, es = stats(i, half)
                if (i, half) == (2, 1):
                    dve.tensor_reduce(mx[:, 0:2], heads(i, 4, 6), AX.X, ALU.max)
                    dve.tensor_reduce(mx[:, 2:4], heads(i, 6, 8), AX.X, ALU.max)
                else:
                    dve.tensor_reduce(mx, heads(i, a, e), AX.X, ALU.max)
                settle()
                dve.tensor_tensor(mx, mx, sink[:, a:e], ALU.max)
                settle()
                dve.tensor_scalar(nmx, mx, -1.0, None, ALU.mult)
                dve.tensor_tensor(es, sink[:, a:e], mx, ALU.subtract).then_inc(p_max, 1)

            def normalize(i, half):
                w = SEQ if i == 0 else TOK
                dve.wait_ge(p_exp, 2 * i + half + 1)
                mx, nmx, den, es = stats(i, half)
                dve.tensor_tensor(den, den, es, ALU.add)
                settle()
                dve.reciprocal(den, den)
                settle()
                for n in range(4):
                    pr = heads(i, 4 * half + n, 4 * half + n + 1)[:, 0, 0:w]
                    last = dve.tensor_scalar(pr, pr, den[:, n:n + 1], None, ALU.mult)
                last.then_inc(p_ready, 1)

            def attended(i):
                b = stage_bank(("oT", i), dve)
                emptied_inc(dve.tensor_copy(T[:, 0:4, i * P:(i + 1) * P], b[:, :].rearrange("p (c n) -> p c n", c=4)))

            scores(0, 0)
            scores(0, 1)
            ada(7, 9)
            normalize(0, 0)
            dve.wait_ge(kv_out_done, 32)
            scores(1, 0)
            normalize(0, 1)
            ada_read(9)
            scores(1, 1)
            normalize(1, 0)
            attended(0)
            ada_read(10)
            scores(2, 0)
            ada(11, 13)
            normalize(1, 1)
            scores(2, 1)
            ada_read(13)
            ada(14, 16)
            normalize(2, 0)
            attended(1)
            normalize(2, 1)
            ada_read(16)
            attended(2)
            ada_read(17)
            gated_add(0)
            dve.drain().then_inc(special_free, 1)
            route(0)
            moe(0)
            affine(2, 0)
            norm(2, 2)
            affine(2, 1)
            affine(2, 2)
            def halves_apart(key, g, out, op0, op1):
                b = stage_bank((key, 2 * g), dve)
                dve.wait_ge(act_emptied, turn[(key, 2 * g + 1)][3])
                dve.tensor_tensor(out[:, 2 * g, :], b[:, 0:TOK], out[:, 2 * g + 1, :], op0)
                settle()
                emptied_inc(dve.tensor_tensor(out[:, 2 * g + 1, :], b[:, 0:TOK], out[:, 2 * g + 1, :], op1))

            for g in range(FG):
                halves_apart("uT", g, uT, ALU.add, ALU.subtract)
            for g in range(FG):
                for i in range(NT):
                    if turn[("v", i, g)][2] == "dve":
                        b = stage_bank(("v", i, g), dve)
                        emptied_inc(dve.tensor_copy(v[:, i, g, :], b[:, 0:VW]))
            for g in range(FG):
                halves_apart("fT", g, T, ALU.subtract, ALU.add)
            gated_add(1)
            route(1)
            moe(1)

        @block.tensor
        def _(pe):
            def begin(key):
                bank, n, who, k, before = turn[key]
                if before is not None:
                    pe.wait_ge(emptied[before[0]], before[1])
                return banks[bank]

            def done_by(*keys):
                for key in keys:
                    pe.wait_ge(emptied[turn[key][2]], turn[key][3])

            def item(n, w=HALF):
                pe.wait_ge(arrived[n % NS], 16 * (n // NS + 1))
                return ring[:, n % NS, 0:KT * w].rearrange("p (k n) -> p k n", k=KT)

            def ada_product(n):
                l, cc = ADA[n]
                w = item(ada_at(n))
                b = begin(("ada", n))
                gate = cc in GATE_CHUNKS
                for k in range(KT):
                    q = k % 4
                    last = pe.matmul(b[32 * q:32 * q + 32, :], cond[:, k, :], w[:, k, :],
                                     start=(k < 4), stop=(k >= 4 and not gate), skip_group_check=True)
                if gate:
                    for q in range(4):
                        r = (l * ADA_C + cc) * 4 + q
                        last = pe.matmul(b[32 * q:32 * q + 32, q * P:(q + 1) * P],
                                         ident[0:N_BROWS, r:r + 1].to_broadcast([N_BROWS, 32]), brows[:, :],
                                         start=False, stop=True, skip_group_check=True)
                last.then_inc(full, 1)

            def ada_read(n):
                done_by(("ada", n))
                row = ada_row[:, n % 2, :]
                if ADA[n][1] in GATE_CHUNKS:
                    for k in range(2):
                        b = begin(("gate", n, k))
                        pe.matmul(b[:, :], con(f"spread{k}"), row, start=True, stop=True).then_inc(full, 1)
                else:
                    b = begin(("adaT", n))
                    for q in range(4):
                        last = pe.transpose(b[:, q * P:(q + 1) * P], row[:, q * P:(q + 1) * P], ident)
                    last.then_inc(full, 1)

            def ada(n0, n1):
                for n in range(n0, n1):
                    ada_product(n)
                    if n > n0:
                        ada_read(n - 1)
                ada_read(n1 - 1)

            def norm(s, *tiles):
                for t in tiles:
                    pe.wait_ge(normed, NT * s + t + 1)
                    for q in range(2):
                        b = begin(("norm", s, t, q))
                        for k in range(4):
                            j = 4 * q + k
                            last = pe.transpose(b[:, k * P:(k + 1) * P], h[:, t, j * P:(j + 1) * P], ident)
                        last.then_inc(full, 1)

            def normed_cols(s, t=NT - 1):
                done_by(("norm", s, t, 0), ("norm", s, t, 1))

            def project(l, n0):
                for hh in range(2):
                    w = item(n0 + hh)
                    for i in range(NT):
                        b = begin(("out", l, hh, i))
                        if l == 0 and hh == 0:
                            done_by(("oT", i), ("pooled", NPG - 1))
                        if l == 1 and (hh, i) == (0, 0):
                            done_by(("fT", KT - 4))
                            pe.wait_ge(middle_out_done, FG - 1)
                        for k in range(KT):
                            if l == 1 and (hh, i, k) == (0, 0, KT - 2):
                                done_by(("fT", KT - 2), "fM")
                            last = pe.matmul(b[:, :], T[:, k, i * P:(i + 1) * P], w[:, k, :], start=(k == 0), stop=(k == KT - 1))
                        last.then_inc(full, 1)
                        if (hh, i) == (1, 1):
                            norm(2 * l + 1, 0)
                norm(2 * l + 1, 1)
                ada_product(LAST_GATE[l])
                norm(2 * l + 1, 2)

            def tokens(l, t):
                for hh in range(2):
                    b = begin(("tokens", l, t, hh))
                    for q in range(4):
                        last = pe.transpose(b[:, q * P:(q + 1) * P], T[:, 4 * hh + q, t * P:(t + 1) * P], ident)
                    last.then_inc(full, 1)

            def route(l):
                pe.wait_ge(params_in, loads[params_in])
                logits = begin(("logits", l))
                for t in range(NT):
                    if t == NT - 1:
                        tokens(l, 0)
                    normed_cols(2 * l + 1, t)
                    for k in range(KT):
                        q = k % 4
                        cs = slice(t * P, (t + 1) * P)
                        last = pe.matmul(logits[32 * q:32 * q + 32, cs], router_w[:, l, k, :], T[:, k, cs],
                                         start=(k < 4), stop=(k >= 4), skip_group_check=True)
                last.then_inc(full, 1)
                tokens(l, 1)
                done_by(("logits", l))
                b = begin(("router", l))
                for t in range(NT):
                    last = pe.transpose(b[:, t * P:(t + 1) * P], lrow[:, t * P:(t + 1) * P], ident)
                last.then_inc(full, 1)
                tokens(l, 2)
                n = LAST_GATE[l]
                ada_product(n + 1)
                ada_read(n)
                b = begin(("rank", l))
                pe.wait_ge(ms_ready, l + 1)
                pe.matmul(b[:, 0:(NT + 1) * NE], before_bf, Ms.rearrange("p t e -> p (t e)"),
                          start=True, stop=False, skip_group_check=True)
                for t in range(NT):
                    later = NT - t
                    last = pe.matmul(b[:, (t + 1) * NE:(NT + 1) * NE], ones_bf,
                                     Ms[:, t, :].unsqueeze(1).to_broadcast([P, later, NE]),
                                     start=False, stop=(t == NT - 1), skip_group_check=True)
                last.then_inc(full, 1)
                ada_read(n + 1)

            def moe(l):
                s, o = pairs[l], overs[l]
                n0 = n_exp[l]
                pe.wait_ge(act_emptied, marks[l]["act"])
                pe.wait_ge(dve_emptied, marks[l]["dve"])

                def gather(q, w, s):
                    for k in range(4):
                        for t in range(NT):
                            kk = 4 * q + k
                            last = pe.matmul(psX[q][:, k * w:(k + 1) * w], h[:, t, kk * P:(kk + 1) * P], Sel[:, t, 0:w],
                                             start=(t == 0), stop=(t == NT - 1))
                    last.then_inc(s["gathered"], 1)

                def up(s, b, s0, w1, w3):
                    for k in range(KT):
                        for q, w in enumerate((w1, w3)):
                            last = pe.matmul(psU[BLK * q:BLK * (q + 1), :], xT[:, b, k, s0:s0 + BLK], w[:, k, :],
                                             start=(k == 0), stop=(k == KT - 1), skip_group_check=True)
                    last.then_inc(s["up_full"], 1)

                def middle(s, u):
                    for k in range(FC):
                        last = pe.transpose(psT[:, k * P:(k + 1) * P], up_s[:, u, k * P:(k + 1) * P], ident)
                    last.then_inc(s["mid_full"], 1)

                def combine_rows(s, b, w):
                    for t in range(NT):
                        last = pe.transpose(psC[0:w, t * P:(t + 1) * P], CT[:, b, t, 0:w], ident)
                    last.then_inc(s["comb_full"], 1)

                def down(k, hh, ws):
                    for u, w2 in enumerate(ws):
                        last = pe.matmul(psD[hh][BLK * u:BLK * (u + 1), :], aT[:, u, k, :], w2[:, k, HALF * hh:HALF * (hh + 1)],
                                         start=(k == 0), stop=(k == FC - 1), skip_group_check=True)
                    return last

                def back(s, n, b, w):
                    t, hh = n // 2, n % 2
                    rows_in = ys if s is pairs[l] else ys_over
                    pe.matmul(psK[n % 2][:, :], Cs[0:w, b, t * P:(t + 1) * P], rows_in[0:w, HALF * hh:HALF * (hh + 1)],
                              start=True, stop=True).then_inc(s["back_full"], 1)

                def slot(k, kk):
                    return ring[:, (n0 + k) % NS, :].rearrange("p (k n) -> p k n", k=kk)

                def pair(i, p, b, first=False, last=False):
                    def weights(*ks):
                        for k in ks:
                            n = n0 + k
                            pe.wait_ge(arrived[n % NS], i * 16 + 16 * (n // NS + 1))

                    def backs(ns):
                        for m in ns:
                            if m == 0:
                                pe.wait_ge(s["down_out"], p)
                                pe.wait_ge(s["comb_out"], p)
                            if isinstance(p, int) and p == 1:
                                if m >= 2:
                                    pe.wait_ge(s["back_out"], m - 1)
                            else:
                                pe.wait_ge(s["back_out"], p * (2 * NT) + (m - 1 - 2 * NT))
                            back(s, m, 1 - b, 2 * BLK)

                    for u in range(2):
                        if u == 0:
                            pe.wait_ge(s["x_cols"], p * 2 + 2)
                            if not first:
                                pe.wait_ge(s["comb_out"], p)
                        else:
                            pe.wait_ge(s["up_out"], p * 2 + 1)
                        weights(2 * u, 2 * u + 1)
                        up(s, b, BLK * u, slot(2 * u, KT), slot(2 * u + 1, KT))
                        if last:
                            backs(range(NT * u, NT * (u + 1)))
                        else:
                            if u == 0:
                                pe.wait_ge(s["sel_ready"], p + 2)
                                pe.wait_ge(s["x_cols"], p * 2 + 2)
                            gather(u, 2 * BLK, s)
                        pe.wait_ge(s["up_out"], p * 2 + (u + 1))
                        if u == 1 or not first:
                            pe.wait_ge(s["act_cols"], p * 2 + u)
                        middle(s, u)
                    pe.wait_ge(s["weighted"], p + 1)
                    combine_rows(s, b, 2 * BLK)
                    for n in range(2 * FC):
                        if not first and not last and n % 3 == 0:
                            backs([2 * (n // 3), 2 * (n // 3) + 1])
                        if n == 0:
                            pe.wait_ge(s["act_cols"], p * 2 + 2)
                            if not first:
                                pe.wait_ge(s["down_out"], p)
                            weights(4, 5)
                        if last and n == FC:
                            pe.wait_ge(late_half, 16 * (l + 1))
                        done = down(n // 2, n % 2, (slot(4, FC), slot(5, FC)))
                    done.then_inc(s["down_full"], 1)

                pe.wait_ge(s["sel_ready"], 1)
                gather(0, 2 * BLK, s)
                gather(1, 2 * BLK, s)
                pair(0, 0, 0, first=True)
                pair(1, 1, 1)
                with pe.Fori(1, NPAIR // 2 - 1) as i:
                    for b in range(2):
                        pair(i * 2 + b, i * 2 + b, b)
                pair(NPAIR - 2, NPAIR - 2, 0)
                pair(NPAIR - 1, NPAIR - 1, 1, last=True)
                pe.wait_ge(plan_ready, l + 1)
                blocks = pe.value_load(plan_i[0:1, NOV:NOV + 1], min_val=0, max_val=NOV)
                with pe.If(blocks > 0):
                    pe.wait_ge(s["comb_out"], NPAIR)
                    pe.wait_ge(s["down_out"], NPAIR)
                    pe.wait_ge(s["back_out"], (NPAIR - 1) * 2 * NT)
                    with pe.Fori(0, NOV) as j:
                        with pe.If(j < blocks):
                            pe.wait_ge(o["sel_ready"], j + 1)
                            gather(0, BLK, o)
                            gather(1, BLK, o)
                            pe.wait_ge(o["x_cols"], j * 2 + 2)
                            pe.wait_ge(o["weights"], j * 48 + 48)
                            ow = [slot(m, KT if m < 2 else FC) for m in range(3)]
                            up(o, 0, 0, ow[0], ow[1])
                            pe.wait_ge(o["weighted"], j + 1)
                            pe.wait_ge(o["up_out"], j + 1)
                            middle(o, 0)
                            combine_rows(o, 0, BLK)
                            pe.wait_ge(o["act_cols"], j + 1)
                            for n in range(2 * FC):
                                done = down(n // 2, n % 2, ow[2:])
                            done.then_inc(o["down_full"], 1)
                            pe.wait_ge(o["comb_out"], j + 1)
                            pe.wait_ge(o["down_out"], j + 1)
                            for n in range(2 * NT):
                                if n >= 2:
                                    pe.wait_ge(o["back_out"], j * (2 * NT) + (n - 1))
                                back(o, n, 0, BLK)
                pe.wait_ge(sums_ready, l + 1)
                pe.wait_ge(s["comb_out"], NPAIR)
                pe.wait_ge(s["down_out"], NPAIR)
                for n in range(2 * NT):
                    if n >= 2:
                        pe.wait_ge(s["back_out"], (NPAIR - 1) * 2 * NT + n - 1)
                    back(s, n, 1, 2 * BLK)

            pe.wait_ge(small_in, loads[small_in])
            pe.wait_ge(cond_rows, 1)
            b = begin("rows")
            pe.transpose(b[:, 0:N_ROWS], rows[:, :], ident[0:N_ROWS, 0:N_ROWS])
            pe.transpose(b[:, P:P + N_BROWS], brows[:, :], ident[0:N_BROWS, 0:N_BROWS])
            pe.transpose(b[:, 2 * P:2 * P + N_ROWS], rows_silu[:, :], ident[0:N_ROWS, 0:N_ROWS]).then_inc(full, 1)
            done_by("rows")
            for n in range(3):
                ada_product(n)
                if n > 0:
                    ada_read(n - 1)
            norm(0, 0, 1)
            ada_product(3)
            ada_read(2)
            ada_read(3)
            for cc in range(len(W_IN_COLS)):
                wd = W_IN_COLS[cc]
                w = item(N_WIN + cc, wd)
                for i in range(NT):
                    normed_cols(0, i)
                    b = begin(("z", cc, i))
                    for k in range(KT):
                        last = pe.matmul(b[:, 0:wd], T[:, k, i * P:(i + 1) * P], w[:, k, :], start=(k == 0), stop=(k == KT - 1))
                    last.then_inc(full, 1)
                    if (cc, i) == (0, 0):
                        norm(0, 2)
            done_by(("z", 2, 2))
            pe.wait_ge(special_in, 16)
            pe.wait_ge(params_in, loads[params_in])
            U0 = AW + 2 * KVW

            def pooled_map(g):
                done_by(("pool", g))
                b = begin(("pooled", g))
                pe.matmul(b[:, 0:TOK], pool_ws[:, g, :], pooled[:, g % 2, :], start=True, stop=True).then_inc(full, 1)

            for g in range(NPG):
                b = begin(("pool", g))
                cs = slice(U0 + g * P, U0 + (g + 1) * P)
                pe.matmul(b[:, 0:SEQ], z[:, 0, cs], att("band_ctx")[:, g * P:(g + 1) * P], start=True, stop=True)
                bl = att("band_lat").rearrange("p (g s t) -> p g s t", g=NPG, s=2)
                for q in range(2):
                    last = pe.matmul(b[:, SEQ:TOK], z[:, 1 + q, cs], bl[:, g, q, :], start=(q == 0), stop=(q == 1))
                last.then_inc(full, 1)
                if g > 0:
                    pooled_map(g - 1)
            pooled_map(NPG - 1)
            ada(4, 7)
            pe.wait_ge(qk_ready, 1)
            for cc in range(NH // 2):
                b = begin(("qT", cc))
                for i in range(NT):
                    last = pe.transpose(b[:, i * P:(i + 1) * P], qk[:, i, cc * P:(cc + 1) * P], ident)
                last.then_inc(full, 1)
            b = begin("kT")
            for i in range(NT):
                pe.transpose(b[:, i * P:(i + 1) * P], qk[:, i, AW:QKW], ident)
            pe.transpose(b[:, TOK:TOK + PAST], ckT_in[:, :], ident).then_inc(full, 1)
            done_by("kT")

            def scores(i, half):
                for n in range(4 * half, 4 * half + 4):
                    cc, kv = n // 2, n % 2
                    b = begin(("score", i, n))
                    rows_ = slice(HD * kv, HD * (kv + 1))
                    q = qT[rows_, cc, i * P:(i + 1) * P]
                    keys = kT[rows_, 0:SEQ] if i == 0 else kT[rows_, SEQ:TOK + PAST]
                    pe.matmul(b[:, 0:keys.shape[1]], q, keys, start=True, stop=True).then_inc(full, 1)

            def values(i, half):
                pe.wait_ge(p_ready, 2 * i + half + 1)
                keys = [0] if i == 0 else [1, 2, NT]
                ob = begin(("oT", i))

                def turn_head(n):
                    b = begin(("PT", i, n))
                    for k in range(len(keys)):
                        last = pe.transpose(b[:, k * P:(k + 1) * P], heads(i, n, n + 1)[:, 0, k * P:(k + 1) * P], ident)
                    last.then_inc(full, 1)

                def products(n):
                    done_by(("PT", i, n + 1))
                    for k, kt in enumerate(keys):
                        for kv in range(NKV):
                            vals = cv[:, HD * kv:HD * (kv + 1)] if kt == NT else \
                                z[:, kt, AW + KVW + HD * kv:AW + KVW + HD * (kv + 1)]
                            out = ob[HD * kv:HD * (kv + 1), (n // 2) * P:(n // 2 + 1) * P]
                            last = pe.matmul(out, vals, PT[:, (n + kv) % 4, k * P:(k + 1) * P],
                                             start=(k == 0), stop=(k == len(keys) - 1), skip_group_check=True)
                    last.then_inc(pv_done, 1)

                a = 4 * half
                for n in range(a, a + 4):
                    turn_head(n)
                products(a)
                products(a + 2)
                if half:
                    pe.drain().then_inc(full, 1)

            scores(0, 0)
            scores(0, 1)
            ada(7, 9)
            scores(1, 0)
            ada_product(9)
            values(0, 0)
            ada_read(9)
            scores(1, 1)
            ada_product(10)
            values(0, 1)
            ada_read(10)
            scores(2, 0)
            ada(11, 13)
            values(1, 0)
            ada_product(13)
            scores(2, 1)
            ada_read(13)
            ada(14, 16)
            values(1, 1)
            ada_product(16)
            values(2, 0)
            ada_read(16)
            ada_product(17)
            values(2, 1)
            ada_read(17)
            project(0, N_WOUT)
            route(0)
            moe(0)
            ada_product(20)
            norm(2, 0)
            ada_product(21)
            norm(2, 1, 2)
            for cc in range(2):
                w = item(N_FIN + cc)
                for q in range(4):
                    b = begin(("uT", 4 * cc + q))
                    if cc == 0 and q == 0:
                        for t in range(NT):
                            if t == NT - 1:
                                ada_read(20)
                            normed_cols(2, t)
                            for k in range(KT):
                                last = pe.matmul(b[:, t * P:(t + 1) * P], w[:, k, 0:P], T[:, k, t * P:(t + 1) * P],
                                                 start=(k == 0), stop=(k == KT - 1))
                        last.then_inc(full, 1)
                        ada_read(21)
                        continue
                    for k in range(KT):
                        last = pe.matmul(b[:, 0:TOK], w[:, k, q * P:(q + 1) * P], T[:, k, :], start=(k == 0), stop=(k == KT - 1))
                    last.then_inc(full, 1)
            pe.wait_ge(special_in, 32)
            for g in range(FG):
                done_by(("uT", 2 * g))
                for i in range(NT):
                    b = begin(("v", i, g))
                    sums, differences = (uT[:, 2 * g + n, i * P:(i + 1) * P] for n in range(2))
                    pe.matmul(b[:, 0:FH + 1], sums, four("sums"), start=True, stop=False, skip_group_check=True)
                    pe.matmul(b[:, 1 + FH // 2:1 + FH], differences, four("odd"), start=False, stop=True, skip_group_check=True)
                    pe.matmul(b[:, 1 + FH:VW], differences, four("sines"), start=True, stop=True).then_inc(full, 1)
            done_by(("v", NT - 1, FG - 1), ("v", NT - 2, FG - 1))
            tl = four("time_lat").rearrange("p (s c t) -> p s c t", s=2, c=2)

            def along_tokens(out, g, a, e, part):
                pe.matmul(out[:, 0:SEQ], v[:, 0, g, a:e], four("time_ctx")[:, part * SEQ:(part + 1) * SEQ],
                          start=True, stop=True, skip_group_check=True)
                for q in range(2):
                    last = pe.matmul(out[:, SEQ:TOK], v[:, 1 + q, g, a:e], tl[:, q, part, :],
                                     start=(q == 0), stop=(q == 1), skip_group_check=True)
                return last

            b = begin("fM")
            for g in range(FG):
                last = along_tokens(b[32 * g:32 * g + 1, :], g, 0, 1, 0)
            last.then_inc(full, 1)
            for g in range(FG):
                along_tokens(begin(("fT", 2 * g)), g, 1, 1 + FH, 0).then_inc(full, 1)
                along_tokens(begin(("fT", 2 * g + 1)), g, 1 + FH, VW, 1).then_inc(full, 1)
            project(1, N_FOUT)
            route(1)
            moe(1)


NAMES = ["x_prompt", "x_sample", "cache_k", "cache_v", "c", "c_ctx", "ada_w", "ada_b", "norm_mix",
         "norm_ffn", "a_w_in", "a_q_norm", "a_k_norm", "a_sink", "pool_w", "pool_scale", "a_w_out",
         "f_w_in", "f_w_out", "router_g_w", "router_g_b", "router_e_w", "router_e_b", "moe_w1",
         "moe_w3", "moe_w2"]


def kernel(**inputs):
    import concourse.bacc as bacc
    from concourse.bass_utils import run_bass_kernel_spmd

    nc = bacc.Bacc("TRN2", target_bir_lowering=False, num_devices=1)
    arrays, args = {}, []
    for name in NAMES:
        arrays[name] = np.ascontiguousarray(inputs[name])
    heads = arrays["a_w_out"][:, 0:AW].reshape(1, NKV, NH // NKV, HD, D).transpose(0, 2, 1, 3, 4)
    arrays["a_w_out"] = np.concatenate([heads.reshape(1, AW, D), arrays["a_w_out"][:, AW:]], 1)
    arrays["f_w_in"] = np.ascontiguousarray(arrays["f_w_in"][:, :, slot_order(FEATURE_SLOTS)])
    arrays["f_w_out"] = np.ascontiguousarray(arrays["f_w_out"][:, slot_order(FREQ_SLOTS), :])
    arrays["rows"] = np.concatenate([arrays.pop(name).reshape(-1, P) for name in
                                     ("norm_mix", "norm_ffn", "c_ctx", "c", "pool_scale", "ada_b")])
    for name, columns in (("const", constant_columns()), ("att_const", attention_columns()),
                          ("four_const", fourier_columns())):
        arrays[name] = np.concatenate([np.asarray(v, np.float32) for v in columns.values()], 1)
    for name, a in arrays.items():
        args.append(nc.dram_tensor(f"in_{name}", a.shape, F32, kind="ExternalInput").ap())
    outs = {"y_prompt": (1, SEQ, D), "y_sample": (1, DEC, D),
            "new_cache_k": (1, 1, SEQ, NKV, HD), "new_cache_v": (1, 1, SEQ, NKV, HD)}
    for name, shape in outs.items():
        args.append(nc.dram_tensor(name, shape, F32, kind="ExternalOutput").ap())
    build(nc, *args)
    got = run_bass_kernel_spmd(nc, [{f"in_{k}": a for k, a in arrays.items()}], core_ids=[0]).results[0]
    return tuple(got[name] for name in outs)
```
